# Optimizing a Trainium2 kernel written in Bass

```python
import math
import jax, jax.numpy as jnp
from jax import lax
import numpy as np

D_MODEL = 2048
BATCH = 1
SEQ = 256
DEPTH = 2

HEAD_DIM = 64
BLOCK = 128
WINDOW = 128
A_HEADS = D_MODEL // HEAD_DIM
A_KV_HEADS = 4
A_GROUP = A_HEADS // A_KV_HEADS
A_Q_DIM = A_HEADS * HEAD_DIM
A_KV_DIM = A_KV_HEADS * HEAD_DIM
B_HEADS = D_MODEL // HEAD_DIM
B_DIM = B_HEADS * HEAD_DIM
REL_BUCKETS = 32
REL_MAX_DIST = 128
D_FF = 5632
CONV_WIDTH = 3
LN_EPS = 1e-5
ALPHA = (2 * DEPTH) ** 0.25
BETA = (8 * DEPTH) ** -0.25
SCALE = HEAD_DIM ** -0.5
N_A_LAYERS = (DEPTH + 1) // 2
N_B_LAYERS = DEPTH // 2

kernel_name = 'hybrid_swa_sink_fox_convffn_deepnorm'

def layer_norm(x, g, b):
    xf = x.astype(jnp.float32)
    mu = jnp.mean(xf, axis=-1, keepdims=True)
    xc = xf - mu
    var = jnp.mean(xc * xc, axis=-1, keepdims=True)
    y = xc * lax.rsqrt(var + LN_EPS)
    return (y * g.astype(jnp.float32) + b.astype(jnp.float32)).astype(x.dtype)

def t5_causal_bucket(dist):
    n = jnp.maximum(dist, 0)
    max_exact = REL_BUCKETS // 2
    nf = jnp.maximum(n, 1).astype(jnp.float32)
    large = max_exact + (jnp.log(nf / max_exact) / math.log(REL_MAX_DIST / max_exact)
                         * (REL_BUCKETS - max_exact)).astype(jnp.int32)
    large = jnp.minimum(large, REL_BUCKETS - 1)
    return jnp.where(n < max_exact, n, large)

def swa_sink_attention(x, w_qkv, w_o, sinks, rel_bias):
    B, S, _ = x.shape
    nb = S // BLOCK
    qkv = x @ w_qkv
    q = qkv[..., :A_Q_DIM].reshape(B, nb, BLOCK, A_KV_HEADS, A_GROUP, HEAD_DIM)
    k = qkv[..., A_Q_DIM:A_Q_DIM + A_KV_DIM].reshape(B, nb, BLOCK, A_KV_HEADS, HEAD_DIM)
    v = qkv[..., A_Q_DIM + A_KV_DIM:].reshape(B, nb, BLOCK, A_KV_HEADS, HEAD_DIM)

    def with_prev(t):
        prev = jnp.concatenate([jnp.zeros_like(t[:, :1]), t[:, :-1]], axis=1)
        return jnp.concatenate([prev, t], axis=2)

    kb, vb = with_prev(k), with_prev(v)
    s = jnp.einsum('bnqkgd,bnskd->bnkgqs', q, kb).astype(jnp.float32) * SCALE
    qi = jnp.arange(BLOCK)
    kj = jnp.arange(2 * BLOCK)
    dist = (BLOCK + qi)[:, None] - kj[None, :]
    bias = rel_bias.astype(jnp.float32)[t5_causal_bucket(dist)]
    bias = jnp.transpose(bias, (2, 0, 1)).reshape(A_KV_HEADS, A_GROUP, BLOCK, 2 * BLOCK)
    kpos = jnp.arange(nb)[:, None] * BLOCK + kj[None, :] - BLOCK
    mask = ((dist >= 0) & (dist < WINDOW))[None] & (kpos >= 0)[:, None, :]
    mask = mask[:, None, None]
    s = jnp.where(mask, s + bias, -jnp.inf)
    sink = sinks.astype(jnp.float32).reshape(A_KV_HEADS, A_GROUP, 1, 1)
    m = jnp.maximum(jnp.max(s, axis=-1, keepdims=True), sink)
    p = jnp.exp(s - m)
    p = p / (jnp.sum(p, axis=-1, keepdims=True) + jnp.exp(sink - m))
    o = jnp.einsum('bnkgqs,bnskd->bnqkgd', p.astype(v.dtype), vb).reshape(B, S, A_Q_DIM)
    return o @ w_o

def forgetting_attention(x, w_qkvf, f_bias, w_o):
    B, S, _ = x.shape
    nb = S // BLOCK
    proj = x @ w_qkvf
    q = proj[..., :B_DIM].reshape(B, S, B_HEADS, HEAD_DIM).transpose(0, 2, 1, 3)
    k = proj[..., B_DIM:2 * B_DIM].reshape(B, S, B_HEADS, HEAD_DIM).transpose(0, 2, 1, 3)
    v = proj[..., 2 * B_DIM:3 * B_DIM].reshape(B, S, B_HEADS, HEAD_DIM).transpose(0, 2, 1, 3)
    fz = proj[..., 3 * B_DIM:].astype(jnp.float32) + f_bias.astype(jnp.float32)
    cum = jnp.cumsum(jax.nn.log_sigmoid(fz), axis=1).transpose(0, 2, 1)
    kpos = jnp.arange(S)

    def block(i):
        start = i * BLOCK
        qb = lax.dynamic_slice_in_dim(q, start, BLOCK, axis=2)
        cb = lax.dynamic_slice_in_dim(cum, start, BLOCK, axis=2)
        s = (jnp.einsum('bhqd,bhkd->bhqk', qb, k).astype(jnp.float32) * SCALE
             + cb[..., :, None] - cum[:, :, None, :])
        qpos = start + jnp.arange(BLOCK)
        s = jnp.where(kpos[None, :] <= qpos[:, None], s, -jnp.inf)
        p = jax.nn.softmax(s, axis=-1)
        return jnp.einsum('bhqk,bhkd->bqhd', p.astype(v.dtype), v)

    o = lax.map(block, jnp.arange(nb))
    o = jnp.transpose(o, (1, 0, 2, 3, 4)).reshape(B, S, B_DIM)
    return o @ w_o

def conv_ffn(x, w_up, conv_w, conv_b, w_down):
    h = x @ w_up
    c = h.shape[-1]
    h = lax.conv_general_dilated(h, conv_w[:, None, :].astype(h.dtype), window_strides=(1,),
                                 padding=[(CONV_WIDTH - 1, 0)],
                                 dimension_numbers=('NWC', 'WIO', 'NWC'),
                                 feature_group_count=c) + conv_b
    g, u = h[..., :D_FF], h[..., D_FF:]
    return (jax.nn.silu(g) * u) @ w_down

def setup_inputs(seed: int = 0) -> dict:
    key = jax.random.key(seed)
    ks = jax.random.split(key, 20)
    nrm = jax.random.normal
    f32 = jnp.float32
    x = nrm(ks[0], (BATCH, SEQ, D_MODEL), f32)
    din = D_MODEL ** -0.5
    a_w_qkv = jnp.concatenate([
        nrm(ks[1], (N_A_LAYERS, D_MODEL, A_Q_DIM), f32) * din,
        nrm(ks[2], (N_A_LAYERS, D_MODEL, A_KV_DIM), f32) * din,
        nrm(ks[3], (N_A_LAYERS, D_MODEL, A_KV_DIM), f32) * (din * BETA)], axis=-1)
    a_w_o = nrm(ks[4], (N_A_LAYERS, A_Q_DIM, D_MODEL), f32) * (A_Q_DIM ** -0.5 * BETA)
    a_sinks = nrm(ks[5], (N_A_LAYERS, A_HEADS), f32) * 0.5
    rel_bias = nrm(ks[6], (REL_BUCKETS, A_HEADS), f32) * 0.5
    b_w_qkvf = jnp.concatenate([
        nrm(ks[7], (N_B_LAYERS, D_MODEL, B_DIM), f32) * din,
        nrm(ks[8], (N_B_LAYERS, D_MODEL, B_DIM), f32) * din,
        nrm(ks[9], (N_B_LAYERS, D_MODEL, B_DIM), f32) * (din * BETA),
        nrm(ks[10], (N_B_LAYERS, D_MODEL, B_HEADS), f32) * (din * 0.5)], axis=-1)
    b_f_bias = 3.0 + 0.5 * nrm(ks[11], (N_B_LAYERS, B_HEADS), f32)
    b_w_o = nrm(ks[12], (N_B_LAYERS, B_DIM, D_MODEL), f32) * (B_DIM ** -0.5 * BETA)
    ffn_w_up = nrm(ks[13], (DEPTH, D_MODEL, 2 * D_FF), f32) * (din * BETA)
    ffn_conv_w = nrm(ks[14], (DEPTH, CONV_WIDTH, 2 * D_FF), f32) * (CONV_WIDTH ** -0.5)
    ffn_conv_b = nrm(ks[15], (DEPTH, 2 * D_FF), f32) * 0.02
    ffn_w_down = nrm(ks[16], (DEPTH, D_FF, D_MODEL), f32) * (D_FF ** -0.5 * BETA)
    ln_g = 1.0 + 0.02 * nrm(ks[17], (DEPTH, 2, D_MODEL), f32)
    ln_b = 0.02 * nrm(ks[18], (DEPTH, 2, D_MODEL), f32)
    return {'x': x, 'a_w_qkv': a_w_qkv, 'a_w_o': a_w_o, 'a_sinks': a_sinks, 'rel_bias': rel_bias,
            'b_w_qkvf': b_w_qkvf, 'b_f_bias': b_f_bias, 'b_w_o': b_w_o,
            'ffn_w_up': ffn_w_up, 'ffn_conv_w': ffn_conv_w, 'ffn_conv_b': ffn_conv_b,
            'ffn_w_down': ffn_w_down, 'ln_g': ln_g, 'ln_b': ln_b}

def reference(x, a_w_qkv, a_w_o, a_sinks, rel_bias, b_w_qkvf, b_f_bias, b_w_o,
              ffn_w_up, ffn_conv_w, ffn_conv_b, ffn_w_down, ln_g, ln_b):
    for i in range(DEPTH):
        j = i // 2
        if i % 2 == 0:
            y = swa_sink_attention(x, a_w_qkv[j], a_w_o[j], a_sinks[j], rel_bias)
        else:
            y = forgetting_attention(x, b_w_qkvf[j], b_f_bias[j], b_w_o[j])
        x = layer_norm(ALPHA * x + y, ln_g[i, 0], ln_b[i, 0])
        y = conv_ffn(x, ffn_w_up[i], ffn_conv_w[i], ffn_conv_b[i], ffn_w_down[i])
        x = layer_norm(ALPHA * x + y, ln_g[i, 1], ln_b[i, 1])
    return x


_drawn_inputs = setup_inputs


def setup_inputs(seed=0):
    import zlib

    import numpy as np

    out = dict(_drawn_inputs(seed))
    spreads = {}
    factors = {'a_sinks': 30.76, 'rel_bias': 3.714, 'b_f_bias': 34.2, 'ffn_conv_b': 8.0}
    for name, (base, spread) in spreads.items():
        noise = np.random.default_rng([zlib.crc32(name.encode()), seed]).standard_normal(out[name].shape)
        drawn = base * np.exp(spread * noise) if base else spread * noise
        out[name] = __import__('jax').numpy.asarray(drawn.astype(out[name].dtype))
    for name, factor in factors.items():
        out[name] = (out[name] * factor).astype(out[name].dtype)
    return out
```

```python
import math
from contextlib import ExitStack

import concourse.bass as bass
from concourse import mybir

FP32 = mybir.dt.float32
F32R = mybir.dt.float32r
ALU = mybir.AluOpType
ACT = mybir.ActivationFunctionType

P = 128
D = 2048
SEQ = 256
MT = SEQ // P
DEPTH = 2
HD = 64
HEADS = D // HD
KV_HEADS = 4
BUCKETS = 32
MAX_DIST = 128
D_FF = 5632
COLS = 512
KT = D // P
FT = D_FF // P
HG = 8
GROUPS = HEADS // HG
UP_PAIRS = D_FF // COLS
OUT_GROUPS = D // COLS
RING = 4
AHEAD = 2
ALPHA = (2 * DEPTH) ** 0.25
SCALE = HD ** -0.5
LN_EPS = 1e-5
MASKED = -3.0e38
SPAN = 3 * P
STEPS = HG + 3

KC = KT // 2
FC = FT // 2
CH_A_KV = 0
CH_A_Q = CH_A_KV + KC
CH_O = [CH_A_Q + GROUPS * KC]
CH_UP = [CH_O[0] + OUT_GROUPS * KC]
CH_DOWN = [CH_UP[0] + 2 * UP_PAIRS * KC]
CH_B = CH_DOWN[0] + OUT_GROUPS * FC
CH_O.append(CH_B + 3 * GROUPS * KC)
CH_UP.append(CH_O[1] + OUT_GROUPS * KC)
CH_DOWN.append(CH_UP[1] + 2 * UP_PAIRS * KC)
CH_END = CH_DOWN[1] + OUT_GROUPS * FC

TURN_A_KV = 0
TURN_A_QT = 2
TURN_A_Q = 0
TURN_O = [(TURN_A_QT + GROUPS, TURN_A_Q + GROUPS)]
TURN_UP = [tuple(t + 2 for t in TURN_O[0])]
TURN_DOWN = [tuple(t + 2 * UP_PAIRS for t in TURN_UP[0])]
TURN_B = tuple(t + 2 for t in TURN_DOWN[0])
TURN_O.append((TURN_B[0] + 3 * GROUPS, TURN_B[1] + 2 * GROUPS))
TURN_UP.append(tuple(t + 2 for t in TURN_O[1]))
TURN_DOWN.append(tuple(t + 2 * UP_PAIRS for t in TURN_UP[1]))

TT_A = 0
TT_UP = [TT_A + 1 + GROUPS]
TT_B = TT_UP[0] + 2 * UP_PAIRS
TT_UP.append(TT_B + 2 * GROUPS)

PASSES = 3


def bucket(dist):
    exact = BUCKETS // 2
    if dist < exact:
        return dist
    return min(BUCKETS - 1, exact + int(math.log(dist / exact) / math.log(MAX_DIST / exact) * (BUCKETS - exact)))


class Links:

    def __init__(self, eng, sem):
        self.eng, self.sem, self.base, self.n = eng, sem, 0, 0

    def link(self, ins):
        ins.then_inc(self.sem, 1)
        self.n += 1
        self.eng.wait_ge(self.sem, self.base + self.n)

    def enter(self, i, per):
        self.start, self.per = self.n + (self.base if isinstance(self.base, int) else 0), per
        self.base, self.n = i * per + self.start, 0

    def leave(self, turns):
        assert self.n == self.per, (self.n, self.per)
        self.base, self.n = self.start + turns * self.per, 0


def trunk(nc, x, a_w_qkv, a_w_o, a_sinks, rel_bias, b_w_qkvf, b_f_bias, b_w_o,
          ffn_w_up, ffn_conv_w, ffn_conv_b, ffn_w_down, ln_g, ln_b, out):
    ctx = ExitStack()
    with ctx:
        def sb(name, shape, dt=FP32, where=ctx):
            return where.enter_context(nc.sbuf_tensor(name, shape, dt))

        def sem(name):
            return ctx.enter_context(nc.semaphore(name))

        res = sb("res", [P, MT, D])
        raw = sb("raw", [P, RING, 2, COLS])
        w_hi = sb("w_hi", [P, RING, 2, COLS], F32R)
        w_lo = sb("w_lo", [P, RING, 2, COLS], F32R)
        tok = sb("tok", [P, MT, COLS])
        cg = sb("cg", [P, 4, SEQ])
        cu = sb("cu", [P, 4, SEQ])
        lnp = sb("lnp", [P, 2, COLS])
        ident = sb("ident", [P, P])
        lncol = sb("lncol", [P, 2, DEPTH, 2, KT])
        convcol = sb("convcol", [P, DEPTH, 4, 2 * FT])
        cw = sb("cw", [P, 2, 4, 4])
        stats = sb("stats", [P, MT, OUT_GROUPS, 6])
        mv = sb("mv", [P, MT, 2])
        var = sb("var", [P, MT])
        sd = sb("sd", [P, MT])
        rstd = sb("rstd", [P, 3, MT])
        mark = sb("mark", [P, HG])
        nmr = sb("nmr", [P, MT])
        with ExitStack() as first:
            xh = sb("xh", [P, KT, SEQ], F32R, first)
        with ExitStack() as later:
            lnfull = sb("lnfull", [P, 2, D], FP32, later)
        xh_hold = sb("xh_hold", [P, KT * SEQ])
        xl = sb("xl", [P, KT, SEQ], F32R)
        with ExitStack() as mix:
            oh = sb("oh", [P, KT, SEQ], F32R, mix)
            ol = sb("ol", [P, KT, SEQ], F32R, mix)
            bias = sb("bias", [P, HG, SPAN], FP32, mix)
            qT = sb("qT", [P, 4, SEQ], FP32, mix)
            kT = sb("kT", [P, 4, SEQ], FP32, mix)
            vv = sb("vv", [P, MT, COLS], FP32, mix)
            kTall = sb("kTall", [P, KV_HEADS, SEQ], FP32, mix)
            vall = sb("vall", [P, MT, KV_HEADS * HD], FP32, mix)
            prob = sb("prob", [P, 4, SPAN], FP32, mix)
            probT = sb("probT", [P, 2, SPAN], FP32, mix)
            onorm = sb("onorm", [P, MT, 4 * HD], FP32, mix)
            nmax = sb("nmax", [P, MT, HG], FP32, mix)
            rsum = sb("rsum", [P, 2, MT, 4], FP32, mix)
            esink = sb("esink", [P, 2, MT, 4], FP32, mix)
            den = sb("den", [P, 2, MT * 4], FP32, mix)
            rden = sb("rden", [P, 2, MT * 4], FP32, mix)
            sinks = sb("sinks", [P, 2, HEADS], FP32, mix)
            sinkc = sb("sinkc", [P, 2, HG], FP32, mix)
            relT = sb("relT", [BUCKETS, HEADS], FP32, mix)
            reld = sb("reld", [HEADS, SPAN], FP32, mix)
            wf = sb("wf", [P, KT, HEADS], FP32, mix)
            wf_hi = sb("wf_hi", [P, KT, HEADS], F32R, mix)
            wf_lo = sb("wf_lo", [P, KT, HEADS], F32R, mix)
            fz = sb("fz", [P, MT, P], FP32, mix)
            fbc = sb("fbc", [HEADS, 1], FP32, mix)
            fs = [sb(f"fs{i}", [HEADS, SEQ], FP32, mix) for i in range(9)]
            cumq = sb("cumq", [P, MT, HEADS], FP32, mix)
        hid_h = sb("hid_h", [P, FT, SEQ], F32R)
        hid_l = sb("hid_l", [P, FT, SEQ], F32R)
        ps = ctx.enter_context(nc.psum_tensor("ps", [P, 8, COLS], FP32))
        S_BANK, O_BANK, PT_BANK, X_BANK = 4, 6, 7, 4

        rel_dram = nc.dram_tensor("rel_by_distance", (HEADS, P, SPAN), FP32).ap()
        cum_dram = nc.dram_tensor("minus_cumulated_decay", (HEADS, SEQ), FP32).ap()

        raw_in = [sem(f"raw_in{i}") for i in range(RING)]
        res_in = [sem(f"res_in{i}") for i in range(4)]
        par_in = sem("par_in")
        high_ready = sem("high_ready")
        low_ready = sem("low_ready")
        chunks_used = sem("chunks_used")
        acc_free = [sem("acc_free0"), sem("acc_free1")]
        tok_turned = sem("tok_turned")
        ident_ready = sem("ident_ready")
        par_turned = sem("par_turned")
        par_ready = sem("par_ready")
        xt_turned = sem("xt_turned")
        xt_high = sem("xt_high")
        xt_low = sem("xt_low")
        cols_free = sem("cols_free")
        scores_ready = sem("scores_ready")
        scores_used = sem("scores_used")
        probs_ready = sem("probs_ready")
        probsT_turned = sem("probsT_turned")
        probsT_ready = sem("probsT_ready")
        pv_done = sem("pv_done")
        o_ready = sem("o_ready")
        oT_turned = sem("oT_turned")
        oT_high = sem("oT_high")
        oT_low = sem("oT_low")
        bias_ready = sem("bias_ready")
        kv_ready = sem("kv_ready")
        conv_started = sem("conv_started")
        silu_done = sem("silu_done")
        prod_ready = sem("prod_ready")
        hid_high = sem("hid_high")
        hid_low = sem("hid_low")
        cw_ready = sem("cw_ready")
        var_ready = sem("var_ready")
        sd_ready = sem("sd_ready")
        norm_ready = sem("norm_ready")
        z0_ready = sem("z0_ready")
        z1_ready = sem("z1_ready")
        res_ready = sem("res_ready")
        wf_in = sem("wf_in")
        wf_high = sem("wf_high")
        wf_low = sem("wf_low")
        fz_done = sem("fz_done")
        fz_copied = sem("fz_copied")
        fz_cleared = sem("fz_cleared")
        fz_turned = sem("fz_turned")
        decay_abs = sem("decay_abs")
        decay_exp = sem("decay_exp")
        decay_u = sem("decay_u")
        decay_ln = sem("decay_ln")
        cum_ready = sem("cum_ready")
        cum_turned = sem("cum_turned")
        cumq_ready = sem("cumq_ready")
        fin_scaled = sem("fin_scaled")
        fin_ready = sem("fin_ready")
        full_in = sem("full_in")
        out_done = sem("out_done")
        gp_in = sem("gp_in")
        dve_own = sem("dve_own")
        act_own = sem("act_own")
        gp_own = sem("gp_own")

        block = ctx.enter_context(nc.Block())

        def k_tiles(w):
            return w.rearrange("(k p) n -> p k n", p=P)

        def bank(s, m):
            return ps[:, 2 * s + m, :]

        @block.sync
        def _(sp):
            for i in range(4):
                sp.dma_start(res[:, :, i * COLS:(i + 1) * COLS],
                             x[0].rearrange("(m p) d -> p m d", p=P)[:, :, i * COLS:(i + 1) * COLS]).then_inc(res_in[i], 16)

            def load_group(w, col, b4, loc0, chunks):
                for c in range(chunks):
                    loc = loc0 + c
                    if not (isinstance(b4, int) and 4 * b4 + loc < RING):
                        sp.wait_ge(low_ready, b4 * 4 + (loc - RING + 1))
                    sp.dma_start(raw[:, loc % RING], w[:, 2 * c:2 * c + 2, bass.ds(col, COLS)]).then_inc(raw_in[loc % RING], 16)

            wa = k_tiles(a_w_qkv[0])
            wb = k_tiles(b_w_qkvf[0])
            load_group(wa, D, CH_A_KV // 4, 0, KC)
            with sp.Fori(0, GROUPS) as n:
                load_group(wa, n * COLS, n * (KC // 4) + CH_A_Q // 4, 0, KC)
            for l in range(DEPTH):
                if l == 1:
                    sp.wait_ge(chunks_used, CH_B)
                    sp.dma_start(wf[:, :, :], wb[:, :, 3 * D:3 * D + HEADS]).then_inc(wf_in, 16)
                    with sp.Fori(0, GROUPS) as n:
                        for part in range(3):
                            load_group(wb, n * COLS + part * D, n * (3 * KC // 4) + CH_B // 4, part * KC, KC)
                wo = k_tiles((a_w_o if l == 0 else b_w_o)[0])
                with sp.Fori(0, OUT_GROUPS // 2) as n:
                    for i in range(2):
                        load_group(wo, n * (2 * COLS) + i * COLS, n * (2 * KC // 4) + CH_O[l] // 4, i * KC, KC)
                wu = k_tiles(ffn_w_up[l])
                with sp.Fori(0, UP_PAIRS) as n:
                    for i in range(2):
                        load_group(wu, n * COLS + i * D_FF, n * (2 * KC // 4) + CH_UP[l] // 4, i * KC, KC)
                wd = k_tiles(ffn_w_down[l])
                with sp.Fori(0, OUT_GROUPS // 2) as n:
                    for i in range(2):
                        load_group(wd, n * (2 * COLS) + i * COLS, n * (2 * FC // 4) + CH_DOWN[l] // 4, i * FC, FC)
            ov = out[0].rearrange("(m p) d -> p m d", p=P)
            for i in range(4):
                sp.wait_ge(fin_ready, 2 * i + 2)
                sp.dma_start(ov[:, :, i * COLS:(i + 1) * COLS], res[:, :, i * COLS:(i + 1) * COLS]).then_inc(out_done, 16)
            sp.wait_ge(out_done, 64)

        @block.gpsimd
        def _(gp):
            own = Links(gp, gp_own)
            own.link(gp.memset(ident[:, :], 0.0))
            gp.affine_select(out=ident[:, :], in_=ident[:, :], compare_op=ALU.not_equal, fill=1.0, base=0,
                             pattern=[[-1, P]], channel_multiplier=1).then_inc(ident_ready, 1)
            gp.dma_start(sinks[:, 0, :], a_sinks[0:1, :].to_broadcast([P, HEADS])).then_inc(gp_in, 16)
            gp.dma_start(relT[:, :], rel_bias.rearrange("b h -> h b"), allow_slow_non_contiguous=True).then_inc(gp_in, 16)
            own.link(gp.memset(reld[:, :], MASKED))
            gp.wait_ge(gp_in, 32)
            own.link(gp.tensor_scalar(sinks[:, 1, :], sinks[:, 0, :], -1.0, None, ALU.mult))
            for b in range(BUCKETS):
                ds_ = [d for d in range(P) if bucket(d) == b]
                lo, n = 2 * P - 1 - ds_[-1], len(ds_)
                last = gp.tensor_copy(reld[:, lo:lo + n], relT[:, b:b + 1].to_broadcast([HEADS, n]))
            own.link(last)
            gp.dma_start(rel_dram, reld[:, :].unsqueeze(1).to_broadcast([HEADS, P, SPAN])).then_inc(gp_in, 16)
            gp.wait_ge(gp_in, 48)

            with gp.Fori(0, GROUPS) as n:
                own.enter(n, 0)
                gp.wait_ge(scores_used, n * HG)
                off = n * (HG * P * SPAN)
                for lo, hi, at in ((P, SPAN, P - 1), (0, P, 2 * P - 1)):
                    gp.dma_start(bias[:, :, lo:hi], bass.AP(rel_dram.tensor, off + at, [[SPAN - 1, P], [P * SPAN, HG], [1, hi - lo]])).then_inc(gp_in, 16)
                gp.wait_ge(probs_ready, n * HG)
                gp.tensor_copy(sinkc[:, :, :], sinks[:, :, bass.ds(n * HG, HG)])
                gp.wait_ge(acc_free[0], 2 * (TURN_A_KV + 2))
                gp.wait_ge(scores_ready, n * HG)
                gp.tensor_copy(kT[:, 0:1, :], kTall[:, bass.ds(n, 1), :]).then_inc(kv_ready, 1)
                gp.wait_ge(pv_done, n * HG)
                gp.tensor_copy(vv[:, :, 0:HD], vall[:, :, bass.ds(n * HD, HD)]).then_inc(kv_ready, 1)
                gp.wait_ge(gp_in, n * 32 + 80)
                gp.wait_ge(kv_ready, n * 2 + 2)
                gp.sem_inc(bias_ready, 1)
                own.leave(GROUPS)
            gp_loads = 48 + 32 * GROUPS

            def scale_residual(l, s, count, loads):
                row_g, row_b = ln_g[l, s:s + 1, :], ln_b[l, s:s + 1, :]
                for i in range(4):
                    cols = slice(i * COLS, (i + 1) * COLS)
                    gp.dma_start(lnp[:, 0, :], row_g[:, cols].to_broadcast([P, COLS])).then_inc(gp_in, 16)
                    gp.dma_start(lnp[:, 1, :], row_b[:, cols].to_broadcast([P, COLS])).then_inc(gp_in, 16)
                    loads += 32
                    gp.wait_ge(gp_in, loads)
                    gp.wait_ge(xt_turned, KC * (count + 1) + 2 * (i + 1))
                    for m in range(MT):
                        last = gp.tensor_tensor(res[:, m, cols], res[:, m, cols], lnp[:, 0, :], ALU.mult)
                    own.link(last)
                    for m in range(MT):
                        last = gp.tensor_tensor(res[:, m, cols], res[:, m, cols], lnp[:, 1, :], ALU.add)
                    last.then_inc(res_ready, 1)
                    gp.wait_ge(res_ready, 4 * count + i + 1)
                return loads

            def conv_weights(l):
                with gp.Fori(0, UP_PAIRS) as n:
                    for h in range(2):
                        gp.wait_ge(acc_free[h], n * 4 + 2 * TURN_UP[l][h])
                        gp.tensor_copy(cw[:, h], convcol[:, l, :, bass.ds(n * 4 + h * FT, 4)]).then_inc(cw_ready, 1)

            gp_loads = scale_residual(0, 0, 0, gp_loads)
            gp.wait_ge(par_ready, 5)
            conv_weights(0)
            gp_loads = scale_residual(0, 1, 1, gp_loads)

            gp.wait_ge(chunks_used, CH_B)
            gp.memset(fz[:, :, :], 0.0).then_inc(fz_cleared, 1)
            gp.dma_start(fbc[:, :], b_f_bias.rearrange("a h -> h a"), allow_slow_non_contiguous=True).then_inc(gp_in, 16)
            gp.wait_ge(cum_ready, 1)
            gp.dma_start(cum_dram, fs[8][:, :]).then_inc(gp_in, 16)
            gp_loads += 32
            gp.wait_ge(gp_in, gp_loads)
            gp.wait_ge(cumq_ready, 1)
            with gp.Fori(0, GROUPS) as n:
                own.enter(n, 2)
                gp.wait_ge(scores_used, n * HG + GROUPS * HG)
                off = n * (HG * SEQ)
                gp.dma_start(bias[:, :, P:SPAN], bass.AP(cum_dram.tensor, off, [[0, P], [SEQ, HG], [1, 2 * P]])).then_inc(gp_in, 16)
                gp.dma_start(bias[:, :, 0:P], bass.AP(cum_dram.tensor, off, [[0, P], [SEQ, HG], [1, P]])).then_inc(gp_in, 16)
                gp.wait_ge(gp_in, n * 32 + (gp_loads + 32))

                def add_query(a, m):
                    return gp.tensor_tensor(bias[:, :, a:a + P], bias[:, :, a:a + P],
                                            cumq[:, m, bass.ds(n * HG, HG)].unsqueeze(2).to_broadcast([P, HG, P]), ALU.add)
                add_query(P, 1)
                for a in (0, 2 * P):
                    last = gp.affine_select(out=bias[:, :, a:a + P], in_=bias[:, :, a:a + P], compare_op=ALU.is_ge,
                                            fill=MASKED, base=0, pattern=[[0, HG], [-1, P]], channel_multiplier=1)
                own.link(last)
                add_query(0, 0)
                own.link(add_query(2 * P, 1))
                gp.sem_inc(bias_ready, 1)
                own.leave(GROUPS)
            gp_loads += 32 * GROUPS
            gp_loads = scale_residual(1, 0, 2, gp_loads)
            conv_weights(1)
            gp.wait_ge(chunks_used, CH_DOWN[1])
            for i, src in enumerate((ln_g, ln_b)):
                gp.dma_start(lnfull[:, i, :], src[1, 1:2, :].to_broadcast([P, D])).then_inc(full_in, 16)
            gp.wait_ge(full_in, 32)

        @block.scalar
        def _(act):
            def split(b4, loc):
                if isinstance(b4, int) and 4 * b4 + loc >= CH_END:
                    return
                act.wait_ge(raw_in[loc % RING], b4 * 16 + 16 * (loc // RING + 1))
                if not (isinstance(b4, int) and 4 * b4 + loc < RING):
                    act.wait_ge(chunks_used, b4 * 4 + (loc - RING + 1))
                act.activation(w_hi[:, loc % RING], raw[:, loc % RING], ACT.Copy).then_inc(high_ready, 1)

            def slots(b4, loc0, nk=KT):
                for k in range(nk):
                    if k % 2 == 0:
                        split(b4, loc0 + k // 2 + AHEAD)
                    yield k

            def split_run(b4, loc0, count):
                while loc0 % 4 and count:
                    split(b4, loc0)
                    loc0, count = loc0 + 1, count - 1
                if count >= 8:
                    with act.Fori(0, count // 4) as i:
                        for c in range(4):
                            split(i + (b4 + loc0 // 4), c)
                    loc0, count = loc0 + count // 4 * 4, count % 4
                for c in range(count):
                    split(b4, loc0 + c)

            def xt_evacuate(xi, l, s, g):
                act.wait_ge(xt_turned, KC * xi + g + 1)
                src = ps[:, X_BANK + g % 4, :].rearrange("p (a t) -> p a t", a=2)
                if xi == 0:
                    act.activation(xh[:, 2 * g:2 * g + 2, :], src, ACT.Copy).then_inc(xt_high, 1)
                    return
                for a in range(2):
                    k = 2 * g + a
                    last = act.activation(xh[:, k, :], src[:, a, :], ACT.Identity, scale=lncol[:, 0, l, s, k:k + 1],
                                          bias=lncol[:, 1, l, s, k:k + 1])
                last.then_inc(xt_high, 1)

            def tok_copy(s, used, batch, scale=1.0):
                act.wait_ge(chunks_used, used)
                act.wait_ge(tok_turned, batch)
                act.activation(tok[:, 0, :], bank(s, 0), ACT.Copy, scale=scale).then_inc(acc_free[s], 1)

            def turned_copy(dst, s, batch):
                act.wait_ge(tok_turned, batch + 1)
                act.activation(dst[:, 0:2, :], bank(s, 0).rearrange("p (a t) -> p a t", a=2), ACT.Copy).then_inc(acc_free[s], 1)

            def attend(s, hc, sink):
                if s < HG:
                    act.wait_ge(scores_used, hc + s + 1)
                    q, j = s // 4, s % 4
                    if sink:
                        act.activation(esink[:, q, :, j], nmax[:, :, s], ACT.Exp, bias=sinkc[:, 0, s:s + 1])
                    b = s % 4
                    act.activation(prob[:, b, 0:P], prob[:, b, 0:P], ACT.Exp, scale=-1.0, bias=nmax[:, 0, s:s + 1],
                                   accum_out=rsum[:, q, 0, j:j + 1])
                    act.activation(prob[:, b, P:SPAN], prob[:, b, P:SPAN], ACT.Exp, scale=-1.0, bias=nmax[:, 1, s:s + 1],
                                   accum_out=rsum[:, q, 1, j:j + 1]).then_inc(probs_ready, 1)

            def out_high(q, quads, kt):
                act.wait_ge(oT_turned, quads + (q + 1))
                act.activation(oh[:, bass.ds(kt + 2 * q, 2), :], ps[:, S_BANK + q, :].rearrange("p (a t) -> p a t", a=2),
                               ACT.Copy).then_inc(oT_high, 1)

            def attention_slot(k, hc, quads, kt, sink):
                if k >= 4 and k < 4 + STEPS:
                    attend(k - 4, hc, sink)
                if k == 13:
                    out_high(0, quads, kt)
                if k == 15:
                    out_high(1, quads, kt)

            def layer_norm(xi):
                act.wait_ge(var_ready, xi)
                act.activation(sd[:, :], var[:, :], ACT.Sqrt).then_inc(sd_ready, 1)

            def normalise(i, xi):
                cols = slice(i * COLS, (i + 1) * COLS)
                act.activation(res[:, 0, cols], res[:, 0, cols], ACT.Identity, scale=rstd[:, 2, 0:1],
                               bias=nmr[:, 0:1]).then_inc(z0_ready, 1)

            def norm_and_first(xi, l, s):
                layer_norm(xi)
                act.wait_ge(norm_ready, xi)
                normalise(0, xi)
                normalise(1, xi)
                xt_evacuate(xi, l, s, 0)
                normalise(2, xi)
                normalise(3, xi)
                xt_evacuate(xi, l, s, 1)

            def mixer_a():
                own_b4 = CH_A_KV // 4
                for k in slots(own_b4, 0):
                    if k % 2 == 0 and k // 2 + 2 < KC:
                        xt_evacuate(0, 0, 0, k // 2 + 2)
                for k in slots(CH_A_Q // 4, 0):
                    if k == 0:
                        act.wait_ge(chunks_used, CH_A_Q)
                        act.wait_ge(par_turned, 3)
                        act.activation(vall[:, 0, :], bank(0, 0)[:, KV_HEADS * HD:], ACT.Copy)
                        both = tok[:, 0, :].rearrange("p (h c d) -> p h c d", c=2, d=HD)
                        for c in range(2):
                            last = act.activation(both[:, :, c, :], bank(0, 0)[:, 0:KV_HEADS * HD].rearrange("p (h d) -> p h d", d=HD), ACT.Copy)
                        last.then_inc(acc_free[0], 1)
                    if k == 3:
                        turned_copy(kTall, 0, TT_A)

                def turn(n, b4, products):
                    ks = slots(b4, 0) if products else range(KT)
                    for k in ks:
                        if k == 0:
                            tok_copy(1, n * KC + CH_A_Q, n + TT_A, SCALE)
                        if k == 3:
                            turned_copy(qT, 0, n + TT_A)
                        attention_slot(k, (n - 1) * HG, (n - 1) * 2, (n - 1) * 4, True)

                with act.Fori(0, GROUPS - 1) as i:
                    turn(i + 1, i * (KC // 4) + (CH_A_Q + KC) // 4, True)
                turn(GROUPS, 0, False)

            def mixer_b():
                def turn(n, b4, first=False, products=True):
                    for k in (slots(b4, 0) if products else range(KT)):
                        if first:
                            if k % 2 == 0 and k // 2 + 2 < KC:
                                xt_evacuate(2, 0, 1, k // 2 + 2)
                            if k == 13:
                                act.wait_ge(wf_in, 16)
                                act.activation(wf_hi[:, :, :], wf[:, :, :], ACT.Copy).then_inc(wf_high, 1)
                            continue
                        if k == 0:
                            act.wait_ge(chunks_used, n * (3 * KC) + CH_B)
                            act.wait_ge(pv_done, n * HG + (GROUPS - 1) * HG)
                            act.activation(vv[:, 0, :], bank(0, 0), ACT.Copy).then_inc(acc_free[0], 1)
                        attention_slot(k, (n + (GROUPS - 1)) * HG, (n + (GROUPS - 1)) * 2, (n - 1) * 4, False)
                    if not products:
                        return
                    for k in slots(b4, KC):
                        if k == 0:
                            tok_copy(0, n * (3 * KC) + (CH_B + KC), n * 2 + TT_B, SCALE)
                        if k == 3:
                            turned_copy(qT, 0, n * 2 + TT_B)
                        if first and k == 7:
                            act.wait_ge(decay_abs, 1)
                            act.activation(fs[2][:, :], fs[1][:, :], ACT.Exp).then_inc(decay_exp, 1)
                        if first and k == 9:
                            act.wait_ge(decay_u, 1)
                            act.activation(fs[4][:, :], fs[3][:, :], ACT.Ln).then_inc(decay_ln, 1)
                    for k in slots(b4, 2 * KC):
                        if k == 0:
                            tok_copy(1, n * (3 * KC) + (CH_B + 2 * KC), n * 2 + (TT_B + 1))
                        if k == 3:
                            turned_copy(kT, 1, n * 2 + (TT_B + 1))

                turn(0, CH_B // 4, first=True)
                with act.Fori(0, GROUPS - 1) as i:
                    turn(i + 1, i * (3 * KC // 4) + (CH_B + 3 * KC) // 4)
                turn(GROUPS, 0, products=False)

            def conv(dst, h, l, n, wait_sem, wait_val):
                act.wait_ge(tok_turned, n * 2 + (TT_UP[l] + h + 1))
                act.wait_ge(cw_ready, n * 2 + (l * 2 * UP_PAIRS + h + 1))
                act.wait_ge(wait_sem, wait_val)
                for j in range(4):
                    act.activation(dst[:, j, :], ps[:, 2 * h + j // 2, (j % 2) * SEQ:(j % 2 + 1) * SEQ], ACT.Identity,
                                   scale=cw[:, h, 2, j:j + 1], bias=cw[:, h, 3, j:j + 1]).then_inc(conv_started, 1)

            def up_finish(k, l, n):
                if k == 0:
                    tok_copy(1, n * (2 * KC) + (CH_UP[l] + 2 * KC), n * 2 + (TT_UP[l] + 1))
                if k == 3:
                    conv(cu, 1, l, n, hid_low, n + l * UP_PAIRS)
                if k == 9:
                    act.wait_ge(prod_ready, n + (l * UP_PAIRS + 1))
                    act.activation(hid_h[:, bass.ds(n * 4, 4), :], cu[:, :, :], ACT.Copy).then_inc(hid_high, 1)

            def mlp(l):
                def turn(n, b4, first=False):
                    for k in slots(b4, 0):
                        if first:
                            if k % 2 == 0 and k // 2 + 2 < KC:
                                xt_evacuate(1 + 2 * l, l, 0, k // 2 + 2)
                        else:
                            up_finish(k, l, n - 1)
                    for k in slots(b4, KC):
                        if k == 0:
                            tok_copy(0, n * (2 * KC) + (CH_UP[l] + KC), n * 2 + TT_UP[l])
                        if k == 3:
                            conv(cg, 0, l, n, prod_ready, n + l * UP_PAIRS)
                        if k == 9:
                            act.wait_ge(acc_free[0], n * 4 + 2 * (TURN_UP[l][0] + 2))
                            act.activation(cg[:, :, :], cg[:, :, :], ACT.Silu).then_inc(silu_done, 1)

                turn(0, CH_UP[l] // 4, first=True)
                with act.Fori(0, UP_PAIRS - 1) as i:
                    turn(i + 1, i * (2 * KC // 4) + (CH_UP[l] + 2 * KC) // 4)
                b4 = CH_DOWN[l] // 4
                for k in slots(b4, 0, 10):
                    up_finish(k, l, UP_PAIRS - 1)
                split_run(b4, 5 + AHEAD, OUT_GROUPS * FC - 5 - (AHEAD if l == DEPTH - 1 else 0))

            for c in range(AHEAD):
                split(0, c)
            act.dma_start(tok[0:2 * FT, :, :].rearrange("p m (a b) -> p (m a) b", b=P)[:, 0:3, :],
                          ffn_conv_w[0].rearrange("w (t p) -> t w p", p=P)).then_inc(par_in, 16)
            act.dma_start(tok[0:2 * FT, :, :].rearrange("p m (a b) -> p (m a) b", b=P)[:, 4:7, :],
                          ffn_conv_w[1].rearrange("w (t p) -> t w p", p=P)).then_inc(par_in, 16)
            for l in range(DEPTH):
                act.dma_start(tok[0:2 * FT, :, :].rearrange("p m (a b) -> p (m a) b", b=P)[:, 4 * l + 3, :],
                              ffn_conv_b[l].rearrange("(t p) -> t p", p=P)).then_inc(par_in, 16)
            for i, src in enumerate((ln_g, ln_b)):
                act.dma_start(cu[64 * i:64 * i + 64, 0, 0:P], src.rearrange("l s (k p) -> (l s k) p", p=P)).then_inc(par_in, 16)
            xt_evacuate(0, 0, 0, 0)
            xt_evacuate(0, 0, 0, 1)
            mixer_a()
            for l in range(DEPTH):
                if l == 1:
                    mixer_b()
                split_run(CH_O[l] // 4, AHEAD, OUT_GROUPS * KC)
                norm_and_first(1 + 2 * l, l, 0)
                mlp(l)
                if l == 0:
                    norm_and_first(2, 0, 1)
            layer_norm(4)
            act.wait_ge(norm_ready, 4)
            for i in range(4):
                cols = slice(i * COLS, (i + 1) * COLS)
                for m in range(MT):
                    act.activation(res[:, m, cols], res[:, m, cols], ACT.Identity, scale=rstd[:, 2, m:m + 1],
                                   bias=nmr[:, m:m + 1]).then_inc(z0_ready, 1)

        @block.vector
        def _(dve):
            own = Links(dve, dve_own)

            def split(b4, loc):
                if isinstance(b4, int) and 4 * b4 + loc >= CH_END:
                    return
                dve.wait_ge(high_ready, b4 * 4 + (loc + 1))
                if not (isinstance(b4, int) and 4 * b4 + loc < RING):
                    dve.wait_ge(chunks_used, b4 * 4 + (loc - RING + 1))
                s = loc % RING
                dve.tensor_tensor(w_lo[:, s], raw[:, s], w_hi[:, s].bitcast(FP32), ALU.subtract).then_inc(low_ready, 1)

            def slots(b4, loc0, nk=KT):
                for k in range(nk):
                    if k % 2 == 0:
                        split(b4, loc0 + k // 2 + AHEAD)
                    yield k

            def split_run(b4, loc0, count):
                while loc0 % 4 and count:
                    split(b4, loc0)
                    loc0, count = loc0 + 1, count - 1
                if count >= 8:
                    with dve.Fori(0, count // 4) as i:
                        for c in range(4):
                            split(i + (b4 + loc0 // 4), c)
                    loc0, count = loc0 + count // 4 * 4, count % 4
                for c in range(count):
                    split(b4, loc0 + c)

            def xt_evacuate(xi, l, s, g):
                src = ps[:, X_BANK + g % 4, :].rearrange("p (a t) -> p a t", a=2)
                dst = xl[:, 2 * g:2 * g + 2, :]
                high = xh[:, 2 * g:2 * g + 2, :].bitcast(FP32)
                dve.wait_ge(xt_high, KC * xi + g + 1)
                if xi == 0:
                    dve.tensor_tensor(dst, src, high, ALU.subtract).then_inc(xt_low, 1)
                    return
                full = cg[:, 2 * (g % 2):2 * (g % 2) + 2, :]
                for a in range(2):
                    k = 2 * g + a
                    last = dve.tensor_scalar(full[:, a, :], src[:, a, :], lncol[:, 0, l, s, k:k + 1],
                                             lncol[:, 1, l, s, k:k + 1], ALU.mult, ALU.add)
                own.link(last)
                dve.tensor_tensor(dst, full, high, ALU.subtract).then_inc(xt_low, 1)

            def tok_copy(s, used, batch, scale=None):
                dve.wait_ge(chunks_used, used)
                dve.wait_ge(tok_turned, batch)
                if scale is None:
                    dve.tensor_copy(tok[:, 1, :], bank(s, 1)).then_inc(acc_free[s], 1)
                else:
                    dve.tensor_scalar(tok[:, 1, :], bank(s, 1), scale, None, ALU.mult).then_inc(acc_free[s], 1)

            def turned_copy(dst, s, batch):
                dve.wait_ge(tok_turned, batch + 1)
                dve.tensor_copy(dst[:, 2:4, :], bank(s, 1).rearrange("p (a t) -> p a t", a=2)).then_inc(acc_free[s], 1)

            def attend(s, hc, group, sink):
                if s < HG:
                    if s == 0:
                        dve.wait_ge(bias_ready, group + 1)
                    dve.wait_ge(scores_ready, hc + (s + 1))
                    if s >= 4:
                        dve.wait_ge(probsT_turned, hc + (s - 3))
                    dve.memset(mark[:, s:s + 1], 0.0)
                    b = s % 4
                    src = ps[:, S_BANK + s % 2, :]
                    for m, (lo, hi) in enumerate(((0, P), (P, SPAN))):
                        last = dve.tensor_tensor_reduce(out=prob[:, b, lo:hi], in0=src[:, lo:hi], in1=bias[:, s, lo:hi],
                                                        scale=-1.0, scalar=sinkc[:, 1, s:s + 1] if sink else -MASKED,
                                                        op0=ALU.add, op1=ALU.min, accum_out=nmax[:, m, s:s + 1])
                    last.then_inc(scores_used, 1)
                j = s - 2
                if 0 <= j < HG:
                    dve.wait_ge(probsT_turned, hc + (j + 1))
                    if j >= 2:
                        dve.wait_ge(pv_done, hc + (j - 1))
                    dve.tensor_copy(probT[:, j % 2, :], ps[:, PT_BANK, 0:SPAN]).then_inc(probsT_ready, 1)

            def out_norm(q, hc, quads, sink):
                dve.wait_ge(probs_ready, hc + 4 * (q + 1))
                d = rsum[:, q].rearrange("p m j -> p (m j)")
                if sink:
                    own.link(dve.tensor_tensor(den[:, q, :], d, esink[:, q].rearrange("p m j -> p (m j)"), ALU.add))
                    d = den[:, q, :]
                own.link(dve.reciprocal(rden[:, q, :], d))
                dve.wait_ge(pv_done, hc + 4 * (q + 1))
                dve.wait_ge(oT_turned, quads + q)
                dve.tensor_tensor(onorm[:, :, :].rearrange("p m (j d) -> p (m j) d", d=HD),
                                  ps[:, O_BANK, :].rearrange("p (g d) -> p g d", d=HD),
                                  rden[:, q, :].unsqueeze(2).to_broadcast([P, MT * 4, HD]), ALU.mult).then_inc(o_ready, 1)

            def out_low(q, quads, kt):
                dve.wait_ge(oT_high, quads + (q + 1))
                at = bass.ds(kt + 2 * q, 2)
                dve.tensor_tensor(ol[:, at, :], ps[:, S_BANK + q, :].rearrange("p (a t) -> p a t", a=2),
                                  oh[:, at, :].bitcast(FP32), ALU.subtract).then_inc(oT_low, 1)

            def attention_slot(k, hc, quads, kt, group, sink):
                if k >= 4 and k < 4 + STEPS:
                    attend(k - 4, hc, group, sink)
                if k == 11:
                    out_norm(0, hc, quads, sink)
                if k == 13:
                    out_low(0, quads, kt)
                if k == 15:
                    out_norm(1, hc, quads, sink)
                    out_low(1, quads, kt)

            def residual(s, turn, used, n, pieces):
                dve.wait_ge(chunks_used, used)
                if pieces:
                    dve.wait_ge(res_ready, pieces)
                cols = bass.ds(n * COLS, COLS)
                for m in range(MT):
                    dve.scalar_tensor_tensor(res[:, m, cols], res[:, m, cols], ALPHA, bank(s, m), ALU.mult, ALU.add)\
                       .then_inc(acc_free[s], 1)
                dve.wait_ge(acc_free[s], 2 * (turn + 1))
                for m in range(MT):
                    last = dve.bn_stats(stats[:, m, bass.ds(n, 1), :].rearrange("p a b -> p (a b)"), res[:, m, cols])
                return last

            def layer_norm(xi, last, split_z=True):
                own.link(last)
                for m in range(MT):
                    last = dve.bn_aggr(mv[:, m, :], stats[:, m, :, :].rearrange("p a b -> p (a b)"))
                own.link(last)
                dve.tensor_scalar(var[:, :], mv[:, :, 1], LN_EPS, None, ALU.add).then_inc(var_ready, 1)
                dve.wait_ge(sd_ready, xi)
                own.link(dve.reciprocal(rstd[:, 0, :], sd[:, :]))
                own.link(dve.tensor_tensor(rstd[:, 1, :], rstd[:, 0, :], rstd[:, 0, :], ALU.mult))
                own.link(dve.tensor_tensor(rstd[:, 1, :], rstd[:, 1, :], var[:, :], ALU.mult))
                own.link(dve.tensor_scalar(rstd[:, 1, :], rstd[:, 1, :], -0.5, 1.5, ALU.mult, ALU.add))
                own.link(dve.tensor_tensor(rstd[:, 2, :], rstd[:, 0, :], rstd[:, 1, :], ALU.mult))
                dve.scalar_tensor_tensor(nmr[:, :], mv[:, :, 0], -1.0, rstd[:, 2, :], ALU.mult, ALU.mult).then_inc(norm_ready, 1)
                dve.wait_ge(norm_ready, xi)

            def normalise(i):
                cols = slice(i * COLS, (i + 1) * COLS)
                dve.tensor_scalar(res[:, 1, cols], res[:, 1, cols], rstd[:, 2, 1:2], nmr[:, 1:2], ALU.mult, ALU.add)\
                   .then_inc(z1_ready, 1)

            def norm_and_first(xi, l, s, last):
                layer_norm(xi, last)
                normalise(0)
                normalise(1)
                xt_evacuate(xi, l, s, 0)
                normalise(2)
                normalise(3)
                xt_evacuate(xi, l, s, 1)

            def mixer_a():
                for k in slots(CH_A_KV // 4, 0):
                    if k % 2 == 0 and k // 2 + 2 < KC:
                        xt_evacuate(0, 0, 0, k // 2 + 2)
                    if k == 7:
                        dve.wait_ge(par_turned, 1)
                        dve.tensor_copy(lncol[:, :, :, :, :].rearrange("p a l s k -> p (a l s k)"), ps[:, 2, 0:P]).then_inc(par_ready, 1)
                        for l in range(DEPTH):
                            dve.wait_ge(par_turned, l + 2)
                            dve.tensor_copy(convcol[:, l].rearrange("p w t -> p (w t)"), ps[:, 2 + (1 + l) % 2, 0:8 * FT]).then_inc(par_ready, 2)
                for k in slots(CH_A_Q // 4, 0):
                    if k == 0:
                        dve.wait_ge(chunks_used, CH_A_Q)
                        dve.wait_ge(par_turned, 3)
                        dve.tensor_copy(vall[:, 1, :], bank(0, 1)[:, KV_HEADS * HD:])
                        both = tok[:, 1, :].rearrange("p (h c d) -> p h c d", c=2, d=HD)
                        for c in range(2):
                            last = dve.tensor_copy(both[:, :, c, :], bank(0, 1)[:, 0:KV_HEADS * HD].rearrange("p (h d) -> p h d", d=HD))
                        last.then_inc(acc_free[0], 1)
                    if k == 3:
                        turned_copy(kTall, 0, TT_A)

                def turn(n, b4, products):
                    for k in (slots(b4, 0) if products else range(KT)):
                        if k == 0:
                            tok_copy(1, n * KC + CH_A_Q, n + TT_A, SCALE)
                        if k == 3:
                            turned_copy(qT, 0, n + TT_A)
                        attention_slot(k, (n - 1) * HG, (n - 1) * 2, (n - 1) * 4, n - 1, True)

                with dve.Fori(0, GROUPS - 1) as i:
                    own.enter(i, 4)
                    turn(i + 1, i * (KC // 4) + (CH_A_Q + KC) // 4, True)
                    own.leave(GROUPS - 1)
                turn(GROUPS, 0, False)

            def decay(k):
                z, nabs, e, u, lnu, d, zero, cum, ncum = fs
                if k == 1:
                    dve.wait_ge(fz_done, 1)
                    dve.wait_ge(fz_cleared, 1)
                    for m in range(MT):
                        last = dve.tensor_copy(fz[:, m, 0:HEADS], ps[:, 6 + m, 0:HEADS])
                    last.then_inc(fz_copied, 1)
                if k == 5:
                    dve.wait_ge(fz_turned, 1)
                    dve.wait_ge(gp_in, 48 + 32 * GROUPS + 2 * 128 + 16)
                    own.link(dve.tensor_scalar(z[:, :], ps[0:HEADS, 6, 0:SEQ], fbc[:, 0:1], None, ALU.add))
                    dve.scalar_tensor_tensor(nabs[:, :], z[:, :], -1.0, z[:, :], ALU.mult, ALU.min).then_inc(decay_abs, 1)
                if k == 7:
                    dve.wait_ge(decay_exp, 1)
                    dve.tensor_scalar(u[:, :], e[:, :], 1.0, None, ALU.add).then_inc(decay_u, 1)
                    dve.wait_ge(decay_u, 1)
                    own.link(dve.tensor_scalar(d[:, :], u[:, :], -1.0, None, ALU.add))
                    own.link(dve.tensor_scalar(zero[:, :], d[:, :], 0.0, None, ALU.is_equal))
                    own.link(dve.tensor_tensor(d[:, :], d[:, :], zero[:, :], ALU.add))
                    own.link(dve.reciprocal(d[:, :], d[:, :]))
                    own.link(dve.tensor_tensor(d[:, :], d[:, :], e[:, :], ALU.mult))
                if k == 9:
                    dve.wait_ge(decay_ln, 1)
                    own.link(dve.tensor_tensor(lnu[:, :], lnu[:, :], zero[:, :], ALU.add))
                    own.link(dve.tensor_tensor(d[:, :], lnu[:, :], d[:, :], ALU.mult))
                    own.link(dve.scalar_tensor_tensor(z[:, :], z[:, :], 0.0, d[:, :], ALU.min, ALU.subtract))
                    own.link(dve.memset(zero[:, :], 1.0))
                    own.link(dve.tensor_tensor_scan(cum[:, :], zero[:, :], z[:, :], 0.0, ALU.mult, ALU.add))
                    dve.tensor_scalar(ncum[:, :], cum[:, :], -1.0, None, ALU.mult).then_inc(cum_ready, 1)
                if k == 13:
                    dve.wait_ge(cum_turned, 1)
                    dve.tensor_copy(cumq[:, :, :], ps[:, 7, 0:MT * HEADS].rearrange("p (m h) -> p m h", m=MT)).then_inc(cumq_ready, 1)

            def mixer_b():
                def turn(n, b4, first=False, products=True):
                    for k in (slots(b4, 0) if products else range(KT)):
                        if first:
                            if k % 2 == 0 and k // 2 + 2 < KC:
                                xt_evacuate(2, 0, 1, k // 2 + 2)
                            if k == 13:
                                dve.wait_ge(wf_high, 1)
                                dve.tensor_tensor(wf_lo[:, :, :], wf[:, :, :], wf_hi[:, :, :].bitcast(FP32), ALU.subtract).then_inc(wf_low, 1)
                            continue
                        if k == 0:
                            dve.wait_ge(chunks_used, n * (3 * KC) + CH_B)
                            dve.wait_ge(pv_done, n * HG + (GROUPS - 1) * HG)
                            dve.tensor_copy(vv[:, 1, :], bank(0, 1)).then_inc(acc_free[0], 1)
                        attention_slot(k, (n + (GROUPS - 1)) * HG, (n + (GROUPS - 1)) * 2, (n - 1) * 4, n + (GROUPS - 1), False)
                    if not products:
                        return
                    for k in slots(b4, KC):
                        if k == 0:
                            tok_copy(0, n * (3 * KC) + (CH_B + KC), n * 2 + TT_B, SCALE)
                        if k == 3:
                            turned_copy(qT, 0, n * 2 + TT_B)
                        if first:
                            decay(k)
                    for k in slots(b4, 2 * KC):
                        if k == 0:
                            tok_copy(1, n * (3 * KC) + (CH_B + 2 * KC), n * 2 + (TT_B + 1))
                        if k == 3:
                            turned_copy(kT, 1, n * 2 + (TT_B + 1))

                turn(0, CH_B // 4, first=True)
                with dve.Fori(0, GROUPS - 1) as i:
                    own.enter(i, 2)
                    turn(i + 1, i * (3 * KC // 4) + (CH_B + 3 * KC) // 4)
                    own.leave(GROUPS - 1)
                turn(GROUPS, 0, products=False)

            def out_projection(l):
                b4, (t0, t1) = CH_O[l] // 4, TURN_O[l]
                pieces = 0 if l == 0 else 8
                for k in slots(b4, 0):
                    pass
                for n in range(1, OUT_GROUPS):
                    for k in slots(b4, n * KC):
                        if k == 0:
                            stat = residual((n - 1) % 2, (t0, t1)[(n - 1) % 2] + (n - 1) // 2, CH_O[l] + n * KC, n - 1, pieces)
                n = OUT_GROUPS
                return residual((n - 1) % 2, (t0, t1)[(n - 1) % 2] + (n - 1) // 2, CH_O[l] + n * KC, n - 1, pieces)

            def conv(dst, h, l, n, done):
                for j0 in (0, 2):
                    dve.wait_ge(conv_started, n * 8 + (l * 8 * UP_PAIRS + 4 * h + j0 + 2))
                    for tap in (1, 0):
                        for j in (j0, j0 + 1):
                            lag = 2 - tap
                            src = ps[:, 2 * h + j // 2, (j % 2) * SEQ:(j % 2 + 1) * SEQ - lag]
                            last = dve.scalar_tensor_tensor(dst[:, j, lag:SEQ], src, cw[:, h, tap, j:j + 1], dst[:, j, lag:SEQ],
                                                            ALU.mult, ALU.add)
                            if tap == 0 and j0 == 2:
                                last.then_inc(acc_free[h], 1)
                        if tap == 1:
                            own.link(last)
                dve.wait_ge(acc_free[h], done)

            def up_finish(k, l, n):
                if k == 0:
                    tok_copy(1, n * (2 * KC) + (CH_UP[l] + 2 * KC), n * 2 + (TT_UP[l] + 1))
                if k == 5:
                    conv(cu, 1, l, n, n * 4 + 2 * (TURN_UP[l][1] + 2))
                    dve.wait_ge(silu_done, n + (l * UP_PAIRS + 1))
                    dve.tensor_tensor(cu[:, :, :], cu[:, :, :], cg[:, :, :], ALU.mult).then_inc(prod_ready, 1)
                if k == 9:
                    dve.wait_ge(hid_high, n + (l * UP_PAIRS + 1))
                    at = bass.ds(n * 4, 4)
                    dve.tensor_tensor(hid_l[:, at, :], cu[:, :, :], hid_h[:, at, :].bitcast(FP32), ALU.subtract).then_inc(hid_low, 1)

            def mlp(l):
                def turn(n, b4, first=False):
                    for k in slots(b4, 0):
                        if first:
                            if k % 2 == 0 and k // 2 + 2 < KC:
                                xt_evacuate(1 + 2 * l, l, 0, k // 2 + 2)
                        else:
                            up_finish(k, l, n - 1)
                    for k in slots(b4, KC):
                        if k == 0:
                            tok_copy(0, n * (2 * KC) + (CH_UP[l] + KC), n * 2 + TT_UP[l])
                        if k == 5:
                            conv(cg, 0, l, n, n * 4 + 2 * (TURN_UP[l][0] + 2))

                turn(0, CH_UP[l] // 4, first=True)
                with dve.Fori(0, UP_PAIRS - 1) as i:
                    own.enter(i, 4)
                    turn(i + 1, i * (2 * KC // 4) + (CH_UP[l] + 2 * KC) // 4)
                    own.leave(UP_PAIRS - 1)
                b4, (t0, t1) = CH_DOWN[l] // 4, TURN_DOWN[l]
                pieces = 4 if l == 0 else 12
                for k in slots(b4, 0, 10):
                    up_finish(k, l, UP_PAIRS - 1)
                split_run(b4, 5 + AHEAD, FC - 5)
                for n in range(1, OUT_GROUPS):
                    residual((n - 1) % 2, (t0, t1)[(n - 1) % 2] + (n - 1) // 2, CH_DOWN[l] + n * FC, n - 1, pieces)
                    split_run(b4, n * FC + AHEAD, FC - (AHEAD if l == DEPTH - 1 and n == OUT_GROUPS - 1 else 0))
                n = OUT_GROUPS
                return residual((n - 1) % 2, (t0, t1)[(n - 1) % 2] + (n - 1) // 2, CH_DOWN[l] + n * FC, n - 1, pieces)

            for c in range(AHEAD):
                split(0, c)
            xt_evacuate(0, 0, 0, 0)
            xt_evacuate(0, 0, 0, 1)
            mixer_a()
            for l in range(DEPTH):
                if l == 1:
                    mixer_b()
                norm_and_first(1 + 2 * l, l, 0, out_projection(l))
                last = mlp(l)
                if l == 0:
                    norm_and_first(2, 0, 1, last)
            layer_norm(4, last)
            dve.wait_ge(full_in, 32)
            for i in range(4):
                cols = slice(i * COLS, (i + 1) * COLS)
                dve.wait_ge(z0_ready, 12 + 2 * (i + 1))
                for m in range(MT):
                    last = dve.tensor_tensor(res[:, m, cols], res[:, m, cols], lnfull[:, 0, cols], ALU.mult)
                own.link(last)
                for m in range(MT):
                    dve.tensor_tensor(res[:, m, cols], res[:, m, cols], lnfull[:, 1, cols], ALU.add).then_inc(fin_ready, 1)

        @block.tensor
        def _(pe):
            def product(s, k, nk, lh, ll, slot):
                for m in range(MT):
                    rows = slice(m * P, (m + 1) * P)
                    o = bank(s, m)
                    pe.matmul(o, lh[:, k, rows], w_lo[:, slot, k % 2, :], start=(k == 0), stop=False)
                    pe.matmul(o, ll[:, k, rows], w_hi[:, slot, k % 2, :], start=False, stop=False)
                    last = pe.matmul(o, lh[:, k, rows], w_hi[:, slot, k % 2, :], start=False, stop=(k == nk - 1))
                return last

            def group(s, turn, b4, loc0, lh=xh, ll=xl, nk=KT, before=None):
                pe.wait_ge(acc_free[s], 2 * turn)
                for k in range(nk):
                    loc = loc0 + k // 2
                    if k % 2 == 0:
                        if before:
                            before(k // 2)
                        pe.wait_ge(low_ready, b4 * 4 + (loc + 1))
                    last = product(s, k, nk, lh, ll, loc % RING)
                    if k % 2 == 1:
                        last.then_inc(chunks_used, 1)
                    yield k

            def xt_turn(xi, g):
                if xi == 0:
                    pe.wait_ge(res_in[g // 2], 16)
                elif g % 2 == 0:
                    pe.wait_ge(z0_ready, 4 * (xi - 1) + g // 2 + 1)
                    pe.wait_ge(z1_ready, 4 * (xi - 1) + g // 2 + 1)
                for a in range(2):
                    k = 2 * g + a
                    for m in range(MT):
                        last = pe.transpose(ps[:, X_BANK + g % 4, a * SEQ + m * P:a * SEQ + (m + 1) * P],
                                            res[:, m, k * P:(k + 1) * P], ident[:, :])
                last.then_inc(xt_turned, 1)

            def x_ready(xi):
                def before(c):
                    if c == 0:
                        for g in range(4):
                            xt_turn(xi, g)
                    elif c + 3 < KC:
                        xt_turn(xi, c + 3)
                    pe.wait_ge(xt_low, KC * xi + c + 1)
                return before

            def turn_tok(s, turn, source_free, source_turns, n_tiles=4):
                pe.wait_ge(acc_free[source_free], source_turns)
                pe.wait_ge(acc_free[s], 2 * turn)
                for j in range(4):
                    for m in range(MT):
                        last = pe.transpose(ps[:, 2 * s + j // 2, (j % 2) * SEQ + m * P:(j % 2) * SEQ + (m + 1) * P],
                                            tok[:, m, j * P:(j + 1) * P], ident[:, :])
                last.then_inc(tok_turned, 1)

            def attend(s, hc, quads, shared, first_waits, value_waits):
                if s < HG:
                    if s == 0:
                        first_waits()
                    if s >= 2:
                        pe.wait_ge(scores_used, hc + (s - 1))
                    if s == 0:
                        pe.wait_ge(oT_low, quads)
                    rows = slice(HD * (s % 2), HD * (s % 2) + HD)
                    kt = 0 if shared else s // 2
                    o = ps[:, S_BANK + s % 2, :]
                    pe.matmul(o[:, 0:P], qT[rows, s // 2, 0:P], kT[rows, kt, 0:P], start=True, stop=True)
                    pe.matmul(o[:, P:SPAN], qT[rows, s // 2, P:SEQ], kT[rows, kt, :], start=True, stop=True).then_inc(scores_ready, 1)
                j = s - 2
                if 0 <= j < HG:
                    pe.wait_ge(probs_ready, hc + (j + 1))
                    if j >= 1:
                        pe.wait_ge(probsT_ready, hc + j)
                    for b in range(3):
                        last = pe.transpose(ps[:, PT_BANK, b * P:(b + 1) * P], prob[:, j % 4, b * P:(b + 1) * P], ident[:, :])
                    last.then_inc(probsT_turned, 1)
                j = s - 3
                if 0 <= j < HG:
                    if j == 0:
                        value_waits()
                    if j % 4 == 0:
                        pe.wait_ge(o_ready, quads + j // 4)
                    pe.wait_ge(probsT_ready, hc + (j + 1))
                    cols = slice(0, HD) if shared else slice(j * HD, (j + 1) * HD)
                    o = [ps[:, O_BANK, m * 4 * HD + (j % 4) * HD:m * 4 * HD + (j % 4 + 1) * HD] for m in range(MT)]
                    pt = probT[:, j % 2, :]
                    pe.matmul(o[0], pt[:, 0:P], vv[:, 0, cols], start=True, stop=True)
                    pe.matmul(o[1], pt[:, P:2 * P], vv[:, 0, cols], start=True, stop=False)
                    pe.matmul(o[1], pt[:, 2 * P:SPAN], vv[:, 1, cols], start=False, stop=True).then_inc(pv_done, 1)

            def turn_out(q, quads):
                pe.wait_ge(o_ready, quads + (q + 1))
                for a in range(2):
                    for m in range(MT):
                        last = pe.transpose(ps[:, S_BANK + q, a * SEQ + m * P:a * SEQ + (m + 1) * P],
                                            onorm[:, m, a * P:(a + 1) * P], ident[:, :])
                last.then_inc(oT_turned, 1)

            def attention_slot(k, hc, quads, shared, first_waits, value_waits):
                if k >= 4 and k < 4 + STEPS:
                    attend(k - 4, hc, quads, shared, first_waits, value_waits)
                if k == 12:
                    pe.wait_ge(scores_used, hc + HG)
                    turn_out(0, quads)
                if k == 15:
                    turn_out(1, quads)

            def mixer_a():
                for k in group(0, TURN_A_KV, CH_A_KV // 4, 0, before=x_ready(0)):
                    if k == 5:
                        pe.wait_ge(par_in, 96)
                        rows = tok[:, :, :].rearrange("p m (a b) -> p (m a) b", b=P)
                        pe.transpose(ps[:, 2, 0:P], cu[:, 0, 0:P], ident[:, :]).then_inc(par_turned, 1)
                        for l in range(DEPTH):
                            if l == 1:
                                pe.wait_ge(par_ready, 1)
                            for w in range(4):
                                last = pe.transpose(ps[:, 2 + (1 + l) % 2, w * 2 * FT:(w + 1) * 2 * FT],
                                                    rows[0:2 * FT, 4 * l + w, :], ident[0:2 * FT, 0:2 * FT])
                            last.then_inc(par_turned, 1)
                pe.wait_ge(par_ready, 5)
                for k in group(1, TURN_A_Q, CH_A_Q // 4, 0):
                    if k == 2:
                        turn_tok(0, TURN_A_KV + 1, 0, 2 * (TURN_A_KV + 1))

                def woven(k, n):
                    if k == 2:
                        turn_tok(0, n - 1 + TURN_A_QT, 1, 2 * (n + TURN_A_Q))

                    def first_waits():
                        pe.wait_ge(acc_free[0], 2 * (n + TURN_A_QT))
                        pe.wait_ge(kv_ready, 2 * n - 1)
                    attention_slot(k, (n - 1) * HG, (n - 1) * 2, True, first_waits, lambda: pe.wait_ge(kv_ready, 2 * n))

                with pe.Fori(0, GROUPS - 1) as i:
                    for k in group(1, i + (TURN_A_Q + 1), i * (KC // 4) + (CH_A_Q + KC) // 4, 0):
                        woven(k, i + 1)
                for k in range(KT):
                    woven(k, GROUPS)

            def mixer_b():
                t0, t1 = TURN_B

                def woven(k, n):
                    def first_waits():
                        pe.wait_ge(acc_free[1], 2 * (n * 2 + t1))
                        pe.wait_ge(acc_free[0], 2 * (n * 3 - 1 + t0))
                    attention_slot(k, (n + (GROUPS - 1)) * HG, (n + (GROUPS - 1)) * 2, False, first_waits,
                                   lambda: pe.wait_ge(acc_free[0], 2 * (n * 3 + t0)))

                def turn(n, b4, first=False):
                    for k in group(0, n * 3 + t0, b4, 0, before=x_ready(2) if first else None):
                        if not first:
                            woven(k, n)
                    if first:
                        pe.wait_ge(wf_low, 1)
                        for m in range(MT):
                            rows = slice(m * P, (m + 1) * P)
                            o = ps[:, 6 + m, 0:HEADS]
                            for k in range(KT):
                                pe.matmul(o, xh[:, k, rows], wf_lo[:, k, :], start=(k == 0), stop=False)
                                pe.matmul(o, xl[:, k, rows], wf_hi[:, k, :], start=False, stop=False)
                                last = pe.matmul(o, xh[:, k, rows], wf_hi[:, k, :], start=False, stop=(k == KT - 1))
                        last.then_inc(fz_done, 1)
                    for k in group(1, n * 2 + t1, b4, KC):
                        if k == 2:
                            turn_tok(0, n * 3 + (t0 + 1), 0, 2 * (n * 3 + (t0 + 1)))
                        if first and k == 4:
                            pe.wait_ge(fz_copied, 1)
                            for m in range(MT):
                                last = pe.transpose(ps[:, 6, m * P:(m + 1) * P], fz[:, m, :], ident[:, :])
                            last.then_inc(fz_turned, 1)
                        if first and k == 12:
                            pe.wait_ge(cum_ready, 1)
                            for m in range(MT):
                                last = pe.transpose(ps[:, 7, m * HEADS:(m + 1) * HEADS], fs[7][:, m * P:(m + 1) * P],
                                                    ident[0:HEADS, 0:HEADS])
                            last.then_inc(cum_turned, 1)
                    for k in group(0, n * 3 + (t0 + 2), b4, 2 * KC):
                        if k == 2:
                            turn_tok(1, n * 2 + (t1 + 1), 1, 2 * (n * 2 + (t1 + 1)))

                turn(0, CH_B // 4, first=True)
                with pe.Fori(0, GROUPS - 1) as i:
                    turn(i + 1, i * (3 * KC // 4) + (CH_B + 3 * KC) // 4)
                for k in range(KT):
                    woven(k, GROUPS)

            def out_projection(l):
                pe.wait_ge(oT_low, 2 * GROUPS * (l + 1))
                with pe.Fori(0, OUT_GROUPS // 2) as n:
                    for i in range(2):
                        for k in group(i, n + TURN_O[l][i], n * (2 * KC // 4) + CH_O[l] // 4, i * KC, oh, ol):
                            pass

            def mlp(l):
                t0, t1 = TURN_UP[l]

                def turn(n, b4, first=False):
                    for k in group(0, n * 2 + t0, b4, 0, before=x_ready(1 + 2 * l) if first else None):
                        if k == 2 and not first:
                            turn_tok(1, n * 2 + (t1 - 1), 1, 2 * (n * 2 + (t1 - 1)))
                    for k in group(1, n * 2 + t1, b4, KC):
                        if k == 2:
                            turn_tok(0, n * 2 + (t0 + 1), 0, 2 * (n * 2 + (t0 + 1)))

                turn(0, CH_UP[l] // 4, first=True)
                with pe.Fori(0, UP_PAIRS - 1) as i:
                    turn(i + 1, i * (2 * KC // 4) + (CH_UP[l] + 2 * KC) // 4)
                last_turn = t1 + 2 * UP_PAIRS - 1
                turn_tok(1, last_turn, 1, 2 * last_turn)
                with pe.Fori(0, OUT_GROUPS // 2) as n:
                    for i in range(2):
                        for k in group(i, n + TURN_DOWN[l][i], n * (2 * FC // 4) + CH_DOWN[l] // 4, i * FC, hid_h, hid_l, FT,
                                       before=lambda c: pe.wait_ge(hid_low, UP_PAIRS * (l + 1) - (1 if c < FC - 2 else 0))
                                       if c in (0, FC - 2) else None):
                            pass

            pe.wait_ge(ident_ready, 1)
            mixer_a()
            for l in range(DEPTH):
                if l == 1:
                    mixer_b()
                out_projection(l)
                mlp(l)


_INS = ['x', 'a_w_qkv', 'a_w_o', 'a_sinks', 'rel_bias', 'b_w_qkvf', 'b_f_bias', 'b_w_o',
        'ffn_w_up', 'ffn_conv_w', 'ffn_conv_b', 'ffn_w_down', 'ln_g', 'ln_b']
_OUTS = [((1, 256, 2048), 'float32')]


def kernel(**inputs):
    import numpy as _np
    import concourse.bacc as _bacc
    from concourse import mybir as _mybir
    from concourse.bass_utils import run_bass_kernel_spmd as _run

    nc = _bacc.Bacc("TRN2", target_bir_lowering=False, num_devices=1)
    arrays, args = {}, []
    for name in _INS:
        a = _np.ascontiguousarray(inputs[name])
        arrays[f"in_{name}_dram"] = a
        args.append(nc.dram_tensor(f"in_{name}_dram", a.shape, _mybir.dt.from_np(a.dtype), kind="ExternalInput").ap())
    for i, (shape, dtype) in enumerate(_OUTS):
        dt = _mybir.dt.from_np(_np.dtype(dtype))
        args.append(nc.dram_tensor(f"out_{i}_dram", shape, dt, kind="ExternalOutput").ap())
    trunk(nc, *args)
    r = _run(nc, [arrays], core_ids=[0])
    got = tuple(r.results[0][f"out_{i}_dram"] for i in range(len(_OUTS)))
    return got[0]
```

```python
import math
from contextlib import ExitStack

import concourse.bass as bass
from concourse import mybir

FP32 = mybir.dt.float32
F32R = mybir.dt.float32r
ALU = mybir.AluOpType
ACT = mybir.ActivationFunctionType

P = 128
D = 2048
SEQ = 256
MT = SEQ // P
DEPTH = 2
HD = 64
HEADS = D // HD
KV_HEADS = 4
BUCKETS = 32
MAX_DIST = 128
D_FF = 5632
COLS = 512
KT = D // P
FT = D_FF // P
HG = 8
GROUPS = HEADS // HG
UP_PAIRS = D_FF // COLS
OUT_GROUPS = D // COLS
RING = 4
AHEAD = 3
LOW_AHEAD = 2
ALPHA = (2 * DEPTH) ** 0.25
SCALE = HD ** -0.5
LN_EPS = 1e-5
GP_COLS = slice(3 * COLS, D)
MASKED = -3.0e38
SPAN = 3 * P
FIRST_STEP = 3
STEPS = HG + 3

KC = KT // 2
FC = FT // 2
CH_A_KV = 0
CH_A_Q = CH_A_KV + KC
CH_O = [CH_A_Q + GROUPS * KC]
CH_UP = [CH_O[0] + OUT_GROUPS * KC]
CH_DOWN = [CH_UP[0] + 2 * UP_PAIRS * KC]
CH_B = CH_DOWN[0] + OUT_GROUPS * FC
CH_O.append(CH_B + 3 * GROUPS * KC)
CH_UP.append(CH_O[1] + OUT_GROUPS * KC)
CH_DOWN.append(CH_UP[1] + 2 * UP_PAIRS * KC)
CH_END = CH_DOWN[1] + OUT_GROUPS * FC

TURN_A_KV = 0
TURN_A_QT = 2
TURN_A_Q = 0
TURN_O = [(TURN_A_QT + GROUPS, TURN_A_Q + GROUPS)]
TURN_UP = [tuple(t + 2 for t in TURN_O[0])]
TURN_DOWN = [tuple(t + 2 * UP_PAIRS for t in TURN_UP[0])]
TURN_B = tuple(t + 2 for t in TURN_DOWN[0])
TURN_O.append((TURN_B[0] + 3 * GROUPS, TURN_B[1] + 2 * GROUPS))
TURN_UP.append(tuple(t + 2 for t in TURN_O[1]))
TURN_DOWN.append(tuple(t + 2 * UP_PAIRS for t in TURN_UP[1]))

TT_A = 0
TT_UP = [TT_A + 1 + GROUPS]
TT_B = TT_UP[0] + 2 * UP_PAIRS
TT_UP.append(TT_B + 2 * GROUPS)

LATE = KT - KT // GROUPS
OUT_DONE = 2 * KT - KT // GROUPS
WOVEN_OUT = [(i, k) for ks in (range(LATE), range(LATE, KT)) for i in range(2) for k in ks]


def bucket(dist):
    exact = BUCKETS // 2
    if dist < exact:
        return dist
    return min(BUCKETS - 1, exact + int(math.log(dist / exact) / math.log(MAX_DIST / exact) * (BUCKETS - exact)))


class Links:

    def __init__(self, eng, sem):
        self.eng, self.sem, self.base, self.n = eng, sem, 0, 0

    def link(self, ins):
        ins.then_inc(self.sem, 1)
        self.n += 1
        self.eng.wait_ge(self.sem, self.base + self.n)

    def enter(self, i, per):
        self.start, self.per = self.n + (self.base if isinstance(self.base, int) else 0), per
        self.base, self.n = i * per + self.start, 0

    def leave(self, turns):
        assert self.n == self.per, (self.n, self.per)
        self.base, self.n = self.start + turns * self.per, 0


def trunk(nc, x, a_w_qkv, a_w_o, a_sinks, rel_bias, b_w_qkvf, b_f_bias, b_w_o,
          ffn_w_up, ffn_conv_w, ffn_conv_b, ffn_w_down, ln_g, ln_b, out):
    ctx = ExitStack()
    with ctx:
        def sb(name, shape, dt=FP32, where=ctx):
            return where.enter_context(nc.sbuf_tensor(name, shape, dt))

        def sem(name):
            return ctx.enter_context(nc.semaphore(name))

        res = sb("res", [P, MT, D])
        raw = sb("raw", [P, RING, 2, COLS])
        w_hi = sb("w_hi", [P, RING, 2, COLS], F32R)
        w_lo = sb("w_lo", [P, RING, 2, COLS], F32R)
        tok = sb("tok", [P, MT, COLS])
        cg = sb("cg", [P, 4, SEQ])
        cu = sb("cu", [P, 4, SEQ])
        lnp = sb("lnp", [P, 2, COLS])
        ident = sb("ident", [P, P])
        lncol = sb("lncol", [P, 2, DEPTH, 2, KT])
        convcol = sb("convcol", [P, DEPTH, 4, 2 * FT])
        cw = sb("cw", [P, 2, 4, 4])
        stats = sb("stats", [P, MT, OUT_GROUPS, 6])
        mv = sb("mv", [P, MT, 2])
        var = sb("var", [P, MT])
        sd = sb("sd", [P, MT])
        rstd = sb("rstd", [P, 3, MT])
        mark = sb("mark", [P, HG])
        nmr = sb("nmr", [P, MT])
        with ExitStack() as first:
            xh = sb("xh", [P, KT, SEQ], F32R, first)
        with ExitStack() as later:
            lnfull = sb("lnfull", [P, 2, D], FP32, later)
        xh_hold = sb("xh_hold", [P, KT * SEQ])
        xl = sb("xl", [P, KT, SEQ], F32R)
        with ExitStack() as mix:
            oh = sb("oh", [P, KT, SEQ], F32R, mix)
            ol = sb("ol", [P, KT, SEQ], F32R, mix)
            bias = sb("bias", [P, HG, SPAN], FP32, mix)
            qT = sb("qT", [P, 4, SEQ], FP32, mix)
            kT = sb("kT", [P, 4, SEQ], FP32, mix)
            vv = sb("vv", [P, MT, COLS], FP32, mix)
            kTall = sb("kTall", [P, KV_HEADS, SEQ], FP32, mix)
            vall = sb("vall", [P, MT, KV_HEADS * HD], FP32, mix)
            prob = sb("prob", [P, 4, SPAN], FP32, mix)
            probT = sb("probT", [P, 2, SPAN], FP32, mix)
            onorm = sb("onorm", [P, MT, 4 * HD], FP32, mix)
            nmax = sb("nmax", [P, MT, HG], FP32, mix)
            rsum = sb("rsum", [P, 2, MT, 4], FP32, mix)
            esink = sb("esink", [P, 2, MT, 4], FP32, mix)
            den = sb("den", [P, 2, MT * 4], FP32, mix)
            rden = sb("rden", [P, 2, MT * 4], FP32, mix)
            sinks = sb("sinks", [P, 2, HEADS], FP32, mix)
            sinkc = sb("sinkc", [P, 2, HG], FP32, mix)
            relT = sb("relT", [BUCKETS, HEADS], FP32, mix)
            reld = sb("reld", [HEADS, SPAN], FP32, mix)
            wf = sb("wf", [P, KT, HEADS], FP32, mix)
            wf_hi = sb("wf_hi", [P, KT, HEADS], F32R, mix)
            wf_lo = sb("wf_lo", [P, KT, HEADS], F32R, mix)
            fbc = sb("fbc", [HEADS, 1], FP32, mix)
            fs = [sb(f"fs{i}", [HEADS, SEQ], FP32, mix) for i in range(9)]
            cumq = sb("cumq", [P, MT, HEADS], FP32, mix)
        hid_h = sb("hid_h", [P, FT, SEQ], F32R)
        hid_l = sb("hid_l", [P, FT, SEQ], F32R)
        ps = ctx.enter_context(nc.psum_tensor("ps", [P, 8, COLS], FP32))
        S_BANK, O_BANK, PT_BANK, X_BANK = 4, 6, 7, 4

        rel_dram = nc.dram_tensor("rel_by_distance", (HEADS, P, SPAN), FP32).ap()
        cum_dram = nc.dram_tensor("minus_cumulated_decay", (HEADS, SEQ), FP32).ap()

        raw_in = [sem(f"raw_in{i}") for i in range(RING)]
        res_in = [sem(f"res_in{i}") for i in range(4)]
        par_in = sem("par_in")
        high_ready = sem("high_ready")
        low_ready = sem("low_ready")
        chunks_used = sem("chunks_used")
        acc_free = [sem("acc_free0"), sem("acc_free1")]
        tok_turned = sem("tok_turned")
        ident_ready = sem("ident_ready")
        par_turned = sem("par_turned")
        par_ready = sem("par_ready")
        xt_turned = sem("xt_turned")
        xt_full = sem("xt_full")
        xt_high = sem("xt_high")
        xt_low = sem("xt_low")
        cols_free = sem("cols_free")
        scores_ready = sem("scores_ready")
        scores_used = sem("scores_used")
        probs_ready = sem("probs_ready")
        probsT_turned = sem("probsT_turned")
        probsT_ready = sem("probsT_ready")
        pv_done = sem("pv_done")
        o_ready = sem("o_ready")
        oT_turned = sem("oT_turned")
        oT_high = sem("oT_high")
        oT_low = sem("oT_low")
        rel_built = sem("rel_built")
        rel_out = sem("rel_out")
        bias_ready = sem("bias_ready")
        kv_ready = sem("kv_ready")
        conv_started = sem("conv_started")
        silu_done = sem("silu_done")
        prod_ready = sem("prod_ready")
        hid_high = sem("hid_high")
        hid_low = sem("hid_low")
        cw_ready = sem("cw_ready")
        var_ready = sem("var_ready")
        sd_ready = sem("sd_ready")
        norm_ready = sem("norm_ready")
        z0_ready = sem("z0_ready")
        z1_ready = sem("z1_ready")
        res_ready = sem("res_ready")
        wf_in = sem("wf_in")
        wf_high = sem("wf_high")
        wf_low = sem("wf_low")
        fz_done = sem("fz_done")
        decay_abs = sem("decay_abs")
        decay_exp = sem("decay_exp")
        decay_u = sem("decay_u")
        decay_ln = sem("decay_ln")
        cum_ready = sem("cum_ready")
        cum_turned = sem("cum_turned")
        cumq_ready = sem("cumq_ready")
        fin_ready = sem("fin_ready")
        fin_gp = sem("fin_gp")
        full_in = sem("full_in")
        out_done = sem("out_done")
        gp_in = sem("gp_in")
        dve_own = sem("dve_own")
        act_own = sem("act_own")
        gp_own = sem("gp_own")

        block = ctx.enter_context(nc.Block())

        def k_tiles(w):
            return w.rearrange("(k p) n -> p k n", p=P)

        def bank(s, m):
            return ps[:, 2 * s + m, :]

        @block.sync
        def _(sp):
            def load_input(i):
                sp.dma_start(res[:, :, i * COLS:(i + 1) * COLS],
                             x[0].rearrange("(m p) d -> p m d", p=P)[:, :, i * COLS:(i + 1) * COLS]).then_inc(res_in[i], 16)

            def repeat_bias(n):
                if n == 0:
                    sp.wait_ge(rel_built, 1)
                else:
                    sp.wait_ge(rel_out, 16 * n)
                heads = slice(n * HG, (n + 1) * HG)
                sp.dma_start(rel_dram[heads], reld[heads, :].unsqueeze(1).to_broadcast([HG, P, SPAN])).then_inc(rel_out, 16)

            def load_chunk(w, col, b4, loc, c):
                if not (isinstance(b4, int) and 4 * b4 + loc < RING):
                    sp.wait_ge(low_ready, b4 * 4 + (loc - RING + 1))
                sp.dma_start(raw[:, loc % RING], w[:, 2 * c:2 * c + 2, bass.ds(col, COLS)]).then_inc(raw_in[loc % RING], 16)

            def load_group(w, col, b4, loc0, chunks):
                for c in range(chunks):
                    load_chunk(w, col, b4, loc0 + c, c)

            wa = k_tiles(a_w_qkv[0])
            wb = k_tiles(b_w_qkvf[0])
            for c in range(KC):
                if c < 4:
                    load_input(c)
                load_chunk(wa, D, CH_A_KV // 4, c, c)
                if c == 3:
                    repeat_bias(0)
                if c == 7:
                    repeat_bias(1)
            for n in range(2):
                load_group(wa, n * COLS, n * (KC // 4) + CH_A_Q // 4, 0, KC)
                repeat_bias(n + 2)
            with sp.Fori(2, GROUPS) as n:
                load_group(wa, n * COLS, n * (KC // 4) + CH_A_Q // 4, 0, KC)
            for l in range(DEPTH):
                if l == 1:
                    with sp.Fori(0, GROUPS) as n:
                        for part in range(3):
                            load_group(wb, n * COLS + part * D, n * (3 * KC // 4) + CH_B // 4, part * KC, KC)
                wo = k_tiles((a_w_o if l == 0 else b_w_o)[0])
                for loc, (i, k) in enumerate(WOVEN_OUT[::2]):
                    load_chunk(wo, i * COLS, CH_O[l] // 4, loc, k // 2)
                for i in range(2, OUT_GROUPS):
                    load_group(wo, i * COLS, CH_O[l] // 4, i * KC, KC)
                wu = k_tiles(ffn_w_up[l])
                with sp.Fori(0, UP_PAIRS) as n:
                    for i in range(2):
                        load_group(wu, n * COLS + i * D_FF, n * (2 * KC // 4) + CH_UP[l] // 4, i * KC, KC)
                wd = k_tiles(ffn_w_down[l])
                with sp.Fori(0, OUT_GROUPS // 2) as n:
                    for i in range(2):
                        load_group(wd, n * (2 * COLS) + i * COLS, n * (2 * FC // 4) + CH_DOWN[l] // 4, i * FC, FC)
            ov = out[0].rearrange("(m p) d -> p m d", p=P)
            for i in (0, 1, 3, 2):
                if i < 3:
                    sp.wait_ge(fin_ready, 2 * i + 2)
                else:
                    sp.wait_ge(fin_gp, 2)
                sp.dma_start(ov[:, :, i * COLS:(i + 1) * COLS], res[:, :, i * COLS:(i + 1) * COLS]).then_inc(out_done, 16)
            sp.wait_ge(out_done, 64)

        @block.gpsimd
        def _(gp):
            own = Links(gp, gp_own)
            own.link(gp.memset(ident[:, :], 0.0))
            gp.affine_select(out=ident[:, :], in_=ident[:, :], compare_op=ALU.not_equal, fill=1.0, base=0,
                             pattern=[[-1, P]], channel_multiplier=1).then_inc(ident_ready, 1)
            gp.dma_start(sinks[:, 0, :], a_sinks[0:1, :].to_broadcast([P, HEADS])).then_inc(gp_in, 16)
            gp.dma_start(relT[:, :], rel_bias.rearrange("b h -> h b"), allow_slow_non_contiguous=True).then_inc(gp_in, 16)
            own.link(gp.memset(reld[:, :], MASKED))
            gp.wait_ge(gp_in, 32)
            own.link(gp.tensor_scalar(sinks[:, 1, :], sinks[:, 0, :], -1.0, None, ALU.mult))
            for b in range(BUCKETS):
                ds_ = [d for d in range(P) if bucket(d) == b]
                lo, n = 2 * P - 1 - ds_[-1], len(ds_)
                last = gp.tensor_copy(reld[:, lo:lo + n], relT[:, b:b + 1].to_broadcast([HEADS, n]))
            own.link(last)
            gp.sem_inc(rel_built, 1)

            with gp.Fori(0, GROUPS) as n:
                own.enter(n, 0)
                gp.wait_ge(rel_out, n * 16 + 16)
                gp.wait_ge(scores_used, n * HG)
                off = n * (HG * P * SPAN)
                for lo, hi, at in ((P, SPAN, P - 1), (0, P, 2 * P - 1)):
                    gp.dma_start(bias[:, :, lo:hi], bass.AP(rel_dram.tensor, off + at, [[SPAN - 1, P], [P * SPAN, HG], [1, hi - lo]])).then_inc(gp_in, 16)
                gp.wait_ge(probs_ready, n * HG)
                gp.tensor_copy(sinkc[:, :, :], sinks[:, :, bass.ds(n * HG, HG)])
                gp.wait_ge(acc_free[0], 2 * (TURN_A_KV + 2))
                gp.wait_ge(scores_ready, n * HG)
                gp.tensor_copy(kT[:, 0:1, :], kTall[:, bass.ds(n, 1), :]).then_inc(kv_ready, 1)
                gp.wait_ge(pv_done, n * HG)
                gp.tensor_copy(vv[:, :, 0:HD], vall[:, :, bass.ds(n * HD, HD)]).then_inc(kv_ready, 1)
                gp.wait_ge(gp_in, n * 32 + 64)
                gp.wait_ge(kv_ready, n * 2 + 2)
                gp.sem_inc(bias_ready, 1)
                own.leave(GROUPS)
            gp_loads = 32 + 32 * GROUPS

            def scale_residual(l, s, count, loads):
                row_g, row_b = ln_g[l, s:s + 1, :], ln_b[l, s:s + 1, :]
                for i in range(4):
                    cols = slice(i * COLS, (i + 1) * COLS)
                    gp.dma_start(lnp[:, 0, :], row_g[:, cols].to_broadcast([P, COLS])).then_inc(gp_in, 16)
                    gp.dma_start(lnp[:, 1, :], row_b[:, cols].to_broadcast([P, COLS])).then_inc(gp_in, 16)
                    loads += 32
                    gp.wait_ge(gp_in, loads)
                    gp.wait_ge(xt_turned, KC * (count + 1) + 2 * (i + 1))
                    for m in range(MT):
                        last = gp.tensor_tensor(res[:, m, cols], res[:, m, cols], lnp[:, 0, :], ALU.mult)
                    own.link(last)
                    for m in range(MT):
                        last = gp.tensor_tensor(res[:, m, cols], res[:, m, cols], lnp[:, 1, :], ALU.add)
                    last.then_inc(res_ready, 1)
                    gp.wait_ge(res_ready, 4 * count + i + 1)
                return loads

            def conv_weights(l):
                with gp.Fori(0, UP_PAIRS) as n:
                    for h in range(2):
                        gp.wait_ge(acc_free[h], n * 4 + 2 * TURN_UP[l][h])
                        gp.tensor_copy(cw[:, h], convcol[:, l, :, bass.ds(n * 4 + h * FT, 4)]).then_inc(cw_ready, 1)

            gp_loads = scale_residual(0, 0, 0, gp_loads)
            gp.wait_ge(par_ready, 5)
            conv_weights(0)
            gp.wait_ge(chunks_used, CH_B)
            gp.dma_start(wf[:, :, :], k_tiles(b_w_qkvf[0])[:, :, 3 * D:3 * D + HEADS]).then_inc(wf_in, 16)
            gp.dma_start(fbc[:, :], b_f_bias.rearrange("a h -> h a"), allow_slow_non_contiguous=True).then_inc(wf_in, 16)
            gp_loads = scale_residual(0, 1, 1, gp_loads)

            gp.wait_ge(cum_ready, 1)
            gp.dma_start(cum_dram, fs[8][:, :]).then_inc(gp_in, 16)
            gp_loads += 16
            gp.wait_ge(gp_in, gp_loads)
            gp.wait_ge(cumq_ready, 1)
            with gp.Fori(0, GROUPS) as n:
                own.enter(n, 2)
                gp.wait_ge(scores_used, n * HG + GROUPS * HG)
                off = n * (HG * SEQ)
                gp.dma_start(bias[:, :, P:SPAN], bass.AP(cum_dram.tensor, off, [[0, P], [SEQ, HG], [1, 2 * P]])).then_inc(gp_in, 16)
                gp.dma_start(bias[:, :, 0:P], bass.AP(cum_dram.tensor, off, [[0, P], [SEQ, HG], [1, P]])).then_inc(gp_in, 16)
                gp.wait_ge(gp_in, n * 32 + (gp_loads + 32))

                def add_query(a, m):
                    return gp.tensor_tensor(bias[:, :, a:a + P], bias[:, :, a:a + P],
                                            cumq[:, m, bass.ds(n * HG, HG)].unsqueeze(2).to_broadcast([P, HG, P]), ALU.add)
                add_query(P, 1)
                for a in (0, 2 * P):
                    last = gp.affine_select(out=bias[:, :, a:a + P], in_=bias[:, :, a:a + P], compare_op=ALU.is_ge,
                                            fill=MASKED, base=0, pattern=[[0, HG], [-1, P]], channel_multiplier=1)
                own.link(last)
                add_query(0, 0)
                own.link(add_query(2 * P, 1))
                gp.sem_inc(bias_ready, 1)
                own.leave(GROUPS)
            gp_loads += 32 * GROUPS
            gp_loads = scale_residual(1, 0, 2, gp_loads)
            conv_weights(1)
            gp.wait_ge(chunks_used, CH_DOWN[1])
            for i, src in enumerate((ln_g, ln_b)):
                gp.dma_start(lnfull[:, i, :], src[1, 1:2, :].to_broadcast([P, D])).then_inc(full_in, 16)
            gp.wait_ge(full_in, 32)
            for m in range(MT):
                gp.wait_ge(z0_ready, 3 * KC + m + 1)
                own.link(gp.tensor_tensor(res[:, m, GP_COLS], res[:, m, GP_COLS], lnfull[:, 0, GP_COLS], ALU.mult))
                gp.tensor_tensor(res[:, m, GP_COLS], res[:, m, GP_COLS], lnfull[:, 1, GP_COLS], ALU.add).then_inc(fin_gp, 1)

        @block.scalar
        def _(act):
            def split(b4, loc):
                if isinstance(b4, int) and 4 * b4 + loc >= CH_END:
                    return
                act.wait_ge(raw_in[loc % RING], b4 * 16 + 16 * (loc // RING + 1))
                if not (isinstance(b4, int) and 4 * b4 + loc < RING):
                    act.wait_ge(chunks_used, b4 * 4 + (loc - RING + 1))
                act.activation(w_hi[:, loc % RING], raw[:, loc % RING], ACT.Copy).then_inc(high_ready, 1)

            def slots(b4, loc0, nk=KT):
                for k in range(nk):
                    if k == nk - 2:
                        split(b4, loc0 + k // 2 + AHEAD)
                    yield k
                    if k % 2 == 0 and k != nk - 2:
                        split(b4, loc0 + k // 2 + AHEAD)

            def split_run(b4, loc0, count):
                while loc0 % 4 and count:
                    split(b4, loc0)
                    loc0, count = loc0 + 1, count - 1
                if count >= 8:
                    with act.Fori(0, count // 4) as i:
                        for c in range(4):
                            split(i + (b4 + loc0 // 4), c)
                    loc0, count = loc0 + count // 4 * 4, count % 4
                for c in range(count):
                    split(b4, loc0 + c)

            def xt_evacuate(xi, l, s, g):
                if xi == 0:
                    act.wait_ge(xt_turned, g + 1)
                    src = ps[:, X_BANK + g % 4, :].rearrange("p (a t) -> p a t", a=2)
                else:
                    act.wait_ge(xt_full, KC * (xi - 1) + g + 1)
                    src = cg[:, 2 * (g % 2):2 * (g % 2) + 2, :]
                act.activation(xh[:, 2 * g:2 * g + 2, :], src, ACT.Copy).then_inc(xt_high, 1)

            def tok_copy(s, used, batch, scale=1.0):
                act.wait_ge(tok_turned, batch)
                act.wait_ge(chunks_used, used)
                act.activation(tok[:, 0, :], bank(s, 0), ACT.Copy, scale=scale).then_inc(acc_free[s], 1)

            def turned_copy(dst, s, batch):
                act.wait_ge(tok_turned, batch + 1)
                act.activation(dst[:, 0:2, :], bank(s, 0).rearrange("p (a t) -> p a t", a=2), ACT.Copy).then_inc(acc_free[s], 1)

            def attend(s, hc, sink):
                if s < HG:
                    act.wait_ge(scores_used, hc + s + 1)
                    q, j = s // 4, s % 4
                    if sink:
                        act.activation(esink[:, q, :, j], nmax[:, :, s], ACT.Exp, bias=sinkc[:, 0, s:s + 1])
                    b = s % 4
                    act.activation(prob[:, b, 0:P], prob[:, b, 0:P], ACT.Exp, scale=-1.0, bias=nmax[:, 0, s:s + 1],
                                   accum_out=rsum[:, q, 0, j:j + 1])
                    act.activation(prob[:, b, P:SPAN], prob[:, b, P:SPAN], ACT.Exp, scale=-1.0, bias=nmax[:, 1, s:s + 1],
                                   accum_out=rsum[:, q, 1, j:j + 1]).then_inc(probs_ready, 1)

            def out_high(q, quads, kt):
                act.wait_ge(oT_turned, quads + (q + 1))
                act.activation(oh[:, bass.ds(kt + 2 * q, 2), :], ps[:, S_BANK + q, :].rearrange("p (a t) -> p a t", a=2),
                               ACT.Copy).then_inc(oT_high, 1)

            def attention_slot(k, hc, quads, kt, sink):
                if FIRST_STEP <= k < FIRST_STEP + STEPS:
                    attend(k - FIRST_STEP, hc, sink)
                if k == 12:
                    out_high(0, quads, kt)
                if k == 14:
                    out_high(1, quads, kt)

            def layer_norm(xi):
                act.wait_ge(var_ready, xi)
                act.activation(sd[:, :], var[:, :], ACT.Sqrt).then_inc(sd_ready, 1)

            def normalise(i):
                cols = slice(i * 2 * P, (i + 1) * 2 * P)
                act.activation(res[:, 0, cols], res[:, 0, cols], ACT.Identity, scale=rstd[:, 2, 0:1],
                               bias=nmr[:, 0:1]).then_inc(z0_ready, 1)

            def norm_and_first(xi, l, s):
                layer_norm(xi)
                act.wait_ge(norm_ready, xi)
                for i in range(3):
                    normalise(i)
                xt_evacuate(xi, l, s, 0)
                for i in range(3, 6):
                    normalise(i)
                xt_evacuate(xi, l, s, 1)
                for i in range(6, KC):
                    normalise(i)

            def mixer_a():
                own_b4 = CH_A_KV // 4
                for k in slots(own_b4, 0):
                    if k % 2 == 0 and k // 2 + 2 < KC:
                        xt_evacuate(0, 0, 0, k // 2 + 2)
                for k in slots(CH_A_Q // 4, 0):
                    if k == 0:
                        act.wait_ge(chunks_used, CH_A_Q)
                        act.wait_ge(par_turned, 3)
                        act.activation(vall[:, 0, :], bank(0, 0)[:, KV_HEADS * HD:], ACT.Copy)
                        both = tok[:, 0, :].rearrange("p (h c d) -> p h c d", c=2, d=HD)
                        for c in range(2):
                            last = act.activation(both[:, :, c, :], bank(0, 0)[:, 0:KV_HEADS * HD].rearrange("p (h d) -> p h d", d=HD), ACT.Copy)
                        last.then_inc(acc_free[0], 1)
                    if k == 2:
                        turned_copy(kTall, 0, TT_A)

                def turn(n, b4, nk=KT):
                    tok_copy(1, n * KC + CH_A_Q, n + TT_A, SCALE)
                    for k in slots(b4, 0, nk):
                        if k == 2:
                            turned_copy(qT, 0, n + TT_A)
                        attention_slot(k, (n - 1) * HG, (n - 1) * 2, (n - 1) * 4, True)

                with act.Fori(0, GROUPS - 1) as i:
                    turn(i + 1, i * (KC // 4) + (CH_A_Q + KC) // 4)
                turn(GROUPS, CH_O[0] // 4, 2 * KT)

            def mixer_b():
                def turn(n, b4, first=False, nk=KT):
                    if not first:
                        act.wait_ge(pv_done, n * HG + (GROUPS - 1) * HG)
                        act.wait_ge(chunks_used, n * (3 * KC) + CH_B)
                        act.activation(vv[:, 0, :], bank(0, 0), ACT.Copy).then_inc(acc_free[0], 1)
                    for k in slots(b4, 0, nk):
                        if first:
                            if k % 2 == 0 and k // 2 + 2 < KC:
                                xt_evacuate(2, 0, 1, k // 2 + 2)
                            if k == 13:
                                act.wait_ge(wf_in, 32)
                                act.activation(wf_hi[:, :, :], wf[:, :, :], ACT.Copy).then_inc(wf_high, 1)
                            continue
                        attention_slot(k, (n + (GROUPS - 1)) * HG, (n + (GROUPS - 1)) * 2, (n - 1) * 4, False)
                    if nk > KT:
                        return
                    tok_copy(0, n * (3 * KC) + (CH_B + KC), n * 2 + TT_B, SCALE)
                    for k in slots(b4, KC):
                        if k == 2:
                            turned_copy(qT, 0, n * 2 + TT_B)
                        if first and k == 7:
                            act.wait_ge(decay_abs, 1)
                            act.activation(fs[2][:, :], fs[1][:, :], ACT.Exp).then_inc(decay_exp, 1)
                        if first and k == 9:
                            act.wait_ge(decay_u, 1)
                            act.activation(fs[4][:, :], fs[3][:, :], ACT.Ln).then_inc(decay_ln, 1)
                    tok_copy(1, n * (3 * KC) + (CH_B + 2 * KC), n * 2 + (TT_B + 1))
                    for k in slots(b4, 2 * KC):
                        if k == 2:
                            turned_copy(kT, 1, n * 2 + (TT_B + 1))

                turn(0, CH_B // 4, first=True)
                with act.Fori(0, GROUPS - 1) as i:
                    turn(i + 1, i * (3 * KC // 4) + (CH_B + 3 * KC) // 4)
                turn(GROUPS, CH_O[1] // 4, nk=2 * KT)

            def conv(dst, h, l, n, j0, wait_sem, wait_val):
                if j0 == 0:
                    act.wait_ge(tok_turned, n * 2 + (TT_UP[l] + h + 1))
                    act.wait_ge(cw_ready, n * 2 + (l * 2 * UP_PAIRS + h + 1))
                    act.wait_ge(wait_sem, wait_val)
                for j in (j0, j0 + 1):
                    act.activation(dst[:, j, :], ps[:, 2 * h + j // 2, (j % 2) * SEQ:(j % 2 + 1) * SEQ], ACT.Identity,
                                   scale=cw[:, h, 2, j:j + 1], bias=cw[:, h, 3, j:j + 1]).then_inc(conv_started, 1)

            def up_copy(l, n):
                tok_copy(1, n * (2 * KC) + (CH_UP[l] + 2 * KC), n * 2 + (TT_UP[l] + 1))

            def up_finish(k, l, n):
                if k in (3, 5):
                    conv(cu, 1, l, n, k - 3, hid_low, n + l * UP_PAIRS)
                if k == 11:
                    act.wait_ge(prod_ready, n + (l * UP_PAIRS + 1))
                    act.activation(hid_h[:, bass.ds(n * 4, 4), :], cu[:, :, :], ACT.Copy).then_inc(hid_high, 1)

            def mlp(l):
                def turn(n, b4, first=False):
                    if not first:
                        up_copy(l, n - 1)
                    for k in slots(b4, 0):
                        if first:
                            if k % 2 == 0 and k // 2 + 2 < KC:
                                xt_evacuate(1 + 2 * l, l, 0, k // 2 + 2)
                        else:
                            up_finish(k, l, n - 1)
                    tok_copy(0, n * (2 * KC) + (CH_UP[l] + KC), n * 2 + TT_UP[l])
                    for k in slots(b4, KC):
                        if k in (3, 5):
                            conv(cg, 0, l, n, k - 3, prod_ready, n + l * UP_PAIRS)
                        if k == 9:
                            act.wait_ge(acc_free[0], n * 4 + 2 * (TURN_UP[l][0] + 2))
                            act.activation(cg[:, :, :], cg[:, :, :], ACT.Silu).then_inc(silu_done, 1)

                turn(0, CH_UP[l] // 4, first=True)
                with act.Fori(0, UP_PAIRS - 1) as i:
                    turn(i + 1, i * (2 * KC // 4) + (CH_UP[l] + 2 * KC) // 4)
                b4 = CH_DOWN[l] // 4
                up_copy(l, UP_PAIRS - 1)
                for k in slots(b4, 0, KT):
                    up_finish(k, l, UP_PAIRS - 1)
                split_run(b4, KC + AHEAD, OUT_GROUPS * FC - KC - (AHEAD if l == DEPTH - 1 else 0))

            act.dma_start(tok[0:2 * FT, :, :].rearrange("p m (a b) -> p (m a) b", b=P)[:, 0:3, :],
                          ffn_conv_w[0].rearrange("w (t p) -> t w p", p=P)).then_inc(par_in, 16)
            act.dma_start(tok[0:2 * FT, :, :].rearrange("p m (a b) -> p (m a) b", b=P)[:, 4:7, :],
                          ffn_conv_w[1].rearrange("w (t p) -> t w p", p=P)).then_inc(par_in, 16)
            for l in range(DEPTH):
                act.dma_start(tok[0:2 * FT, :, :].rearrange("p m (a b) -> p (m a) b", b=P)[:, 4 * l + 3, :],
                              ffn_conv_b[l].rearrange("(t p) -> t p", p=P)).then_inc(par_in, 16)
            for i, src in enumerate((ln_g, ln_b)):
                act.dma_start(cu[64 * i:64 * i + 64, 0, 0:P], src.rearrange("l s (k p) -> (l s k) p", p=P)).then_inc(par_in, 16)
            xt_evacuate(0, 0, 0, 0)
            split(0, 0)
            xt_evacuate(0, 0, 0, 1)
            for c in range(1, AHEAD):
                split(0, c)
            mixer_a()
            for l in range(DEPTH):
                if l == 1:
                    mixer_b()
                split_run(CH_O[l] // 4, 2 * KC + AHEAD, (OUT_GROUPS - 2) * KC)
                norm_and_first(1 + 2 * l, l, 0)
                mlp(l)
                if l == 0:
                    norm_and_first(2, 0, 1)
            layer_norm(4)
            act.wait_ge(norm_ready, 4)
            for m in range(MT):
                act.activation(res[:, m, GP_COLS], res[:, m, GP_COLS], ACT.Identity, scale=rstd[:, 2, m:m + 1],
                               bias=nmr[:, m:m + 1]).then_inc(z0_ready, 1)

        @block.vector
        def _(dve):
            own = Links(dve, dve_own)

            def split(b4, loc):
                if isinstance(b4, int) and 4 * b4 + loc >= CH_END:
                    return
                dve.wait_ge(high_ready, b4 * 4 + (loc + 1))
                if not (isinstance(b4, int) and 4 * b4 + loc < RING):
                    dve.wait_ge(chunks_used, b4 * 4 + (loc - RING + 1))
                s = loc % RING
                dve.tensor_tensor(w_lo[:, s], raw[:, s], w_hi[:, s].bitcast(FP32), ALU.subtract).then_inc(low_ready, 1)

            def slots(b4, loc0, nk=KT):
                for k in range(nk):
                    if k == nk - 2:
                        split(b4, loc0 + k // 2 + LOW_AHEAD)
                    yield k
                    if k % 2 == 0 and k != nk - 2:
                        split(b4, loc0 + k // 2 + LOW_AHEAD)

            def split_run(b4, loc0, count):
                while loc0 % 4 and count:
                    split(b4, loc0)
                    loc0, count = loc0 + 1, count - 1
                if count >= 8:
                    with dve.Fori(0, count // 4) as i:
                        for c in range(4):
                            split(i + (b4 + loc0 // 4), c)
                    loc0, count = loc0 + count // 4 * 4, count % 4
                for c in range(count):
                    split(b4, loc0 + c)

            def xt_evacuate(xi, l, s, g):
                if xi == 0:
                    src = ps[:, X_BANK + g % 4, :].rearrange("p (a t) -> p a t", a=2)
                else:
                    src = cg[:, 2 * (g % 2):2 * (g % 2) + 2, :]
                high = xh[:, 2 * g:2 * g + 2, :].bitcast(FP32)
                dve.wait_ge(xt_high, KC * xi + g + 1)
                dve.tensor_tensor(xl[:, 2 * g:2 * g + 2, :], src, high, ALU.subtract).then_inc(xt_low, 1)

            def xt_full_tiles(xi, l, s, g):
                dve.wait_ge(xt_turned, KC * xi + g + 1)
                if g >= 2:
                    dve.wait_ge(xt_low, KC * xi + g - 1)
                for a in range(2):
                    k = 2 * g + a
                    last = dve.tensor_scalar(cg[:, 2 * (g % 2) + a, :], ps[:, X_BANK + g % 4, a * SEQ:(a + 1) * SEQ],
                                             lncol[:, 0, l, s, k:k + 1], lncol[:, 1, l, s, k:k + 1], ALU.mult, ALU.add)
                last.then_inc(xt_full, 1)

            def xt_next(xi, l, s, k):
                if k % 2 == 0 and k // 2 + 2 < KC:
                    if k == 0:
                        xt_full_tiles(xi, l, s, 2)
                    xt_evacuate(xi, l, s, k // 2 + 2)
                    if k // 2 + 3 < KC:
                        xt_full_tiles(xi, l, s, k // 2 + 3)

            def tok_copy(s, used, batch, scale=None):
                dve.wait_ge(tok_turned, batch)
                dve.wait_ge(chunks_used, used)
                if scale is None:
                    dve.tensor_copy(tok[:, 1, :], bank(s, 1)).then_inc(acc_free[s], 1)
                else:
                    dve.tensor_scalar(tok[:, 1, :], bank(s, 1), scale, None, ALU.mult).then_inc(acc_free[s], 1)

            def turned_copy(dst, s, batch):
                dve.wait_ge(tok_turned, batch + 1)
                dve.tensor_copy(dst[:, 2:4, :], bank(s, 1).rearrange("p (a t) -> p a t", a=2)).then_inc(acc_free[s], 1)

            def attend(s, hc, group, sink):
                if s < HG:
                    if s == 0:
                        dve.wait_ge(bias_ready, group + 1)
                    dve.wait_ge(scores_ready, hc + (s + 1))
                    if s >= 4:
                        dve.wait_ge(probsT_turned, hc + (s - 3))
                    dve.memset(mark[:, s:s + 1], 0.0)
                    b = s % 4
                    src = ps[:, S_BANK + s % 2, :]
                    for m, (lo, hi) in enumerate(((0, P), (P, SPAN))):
                        last = dve.tensor_tensor_reduce(out=prob[:, b, lo:hi], in0=src[:, lo:hi], in1=bias[:, s, lo:hi],
                                                        scale=-1.0, scalar=sinkc[:, 1, s:s + 1] if sink else -MASKED,
                                                        op0=ALU.add, op1=ALU.min, accum_out=nmax[:, m, s:s + 1])
                    last.then_inc(scores_used, 1)
                j = s - 2
                if 0 <= j < HG:
                    dve.wait_ge(probsT_turned, hc + (j + 1))
                    if j >= 2:
                        dve.wait_ge(pv_done, hc + (j - 1))
                    dve.tensor_copy(probT[:, j % 2, :], ps[:, PT_BANK, 0:SPAN]).then_inc(probsT_ready, 1)

            def out_norm(q, hc, quads, sink):
                dve.wait_ge(probs_ready, hc + 4 * (q + 1))
                d = rsum[:, q].rearrange("p m j -> p (m j)")
                if sink:
                    own.link(dve.tensor_tensor(den[:, q, :], d, esink[:, q].rearrange("p m j -> p (m j)"), ALU.add))
                    d = den[:, q, :]
                own.link(dve.reciprocal(rden[:, q, :], d))
                dve.wait_ge(pv_done, hc + 4 * (q + 1))
                dve.wait_ge(oT_turned, quads + q)
                dve.tensor_tensor(onorm[:, :, :].rearrange("p m (j d) -> p (m j) d", d=HD),
                                  ps[:, O_BANK, :].rearrange("p (g d) -> p g d", d=HD),
                                  rden[:, q, :].unsqueeze(2).to_broadcast([P, MT * 4, HD]), ALU.mult).then_inc(o_ready, 1)

            def out_low(q, quads, kt):
                dve.wait_ge(oT_high, quads + (q + 1))
                at = bass.ds(kt + 2 * q, 2)
                dve.tensor_tensor(ol[:, at, :], ps[:, S_BANK + q, :].rearrange("p (a t) -> p a t", a=2),
                                  oh[:, at, :].bitcast(FP32), ALU.subtract).then_inc(oT_low, 1)

            def attention_slot(k, hc, quads, kt, group, sink):
                if k == FIRST_STEP + 7:
                    out_norm(0, hc, quads, sink)
                if FIRST_STEP <= k < FIRST_STEP + STEPS:
                    attend(k - FIRST_STEP, hc, group, sink)
                if k == 12:
                    out_low(0, quads, kt)
                if k == 13:
                    out_norm(1, hc, quads, sink)
                if k == 14:
                    out_low(1, quads, kt)

            def residual(s, turn, used, n, pieces):
                dve.wait_ge(chunks_used, used)
                if pieces:
                    dve.wait_ge(res_ready, pieces)
                cols = bass.ds(n * COLS, COLS)
                for m in range(MT):
                    dve.scalar_tensor_tensor(res[:, m, cols], res[:, m, cols], ALPHA, bank(s, m), ALU.mult, ALU.add)\
                       .then_inc(acc_free[s], 1)
                dve.wait_ge(acc_free[s], 2 * (turn + 1))
                for m in range(MT):
                    last = dve.bn_stats(stats[:, m, bass.ds(n, 1), :].rearrange("p a b -> p (a b)"), res[:, m, cols])
                return last

            def out_residual(l, n):
                s = (n + 1) % 2
                used = CH_O[l] + (OUT_DONE // 2 if n == 0 else (n + 1) * KC)
                return residual(s, TURN_O[l][s] + n // 2, used, n, 8 * l)

            def out_projection(l):
                for n in range(2, OUT_GROUPS):
                    out_residual(l, n - 1)
                    for k in slots(CH_O[l] // 4, n * KC):
                        pass
                return out_residual(l, OUT_GROUPS - 1)

            def layer_norm(xi, last):
                own.link(last)
                for m in range(MT):
                    last = dve.bn_aggr(mv[:, m, :], stats[:, m, :, :].rearrange("p a b -> p (a b)"))
                own.link(last)
                dve.tensor_scalar(var[:, :], mv[:, :, 1], LN_EPS, None, ALU.add).then_inc(var_ready, 1)
                dve.wait_ge(sd_ready, xi)
                own.link(dve.reciprocal(rstd[:, 0, :], sd[:, :]))
                own.link(dve.scalar_tensor_tensor(rstd[:, 1, :], rstd[:, 0, :], -0.5, rstd[:, 0, :], ALU.mult, ALU.mult))
                own.link(dve.tensor_tensor(rstd[:, 1, :], rstd[:, 1, :], var[:, :], ALU.mult))
                own.link(dve.scalar_tensor_tensor(rstd[:, 2, :], rstd[:, 1, :], 1.5, rstd[:, 0, :], ALU.add, ALU.mult))
                dve.scalar_tensor_tensor(nmr[:, :], mv[:, :, 0], -1.0, rstd[:, 2, :], ALU.mult, ALU.mult).then_inc(norm_ready, 1)
                dve.wait_ge(norm_ready, xi)

            def normalise(i):
                cols = slice(i * 2 * P, (i + 1) * 2 * P)
                dve.tensor_scalar(res[:, 1, cols], res[:, 1, cols], rstd[:, 2, 1:2], nmr[:, 1:2], ALU.mult, ALU.add)\
                   .then_inc(z1_ready, 1)

            def norm_and_first(xi, l, s, last):
                layer_norm(xi, last)
                for i in range(2):
                    normalise(i)
                xt_full_tiles(xi, l, s, 0)
                normalise(2)
                normalise(3)
                xt_evacuate(xi, l, s, 0)
                xt_full_tiles(xi, l, s, 1)
                normalise(4)
                normalise(5)
                xt_evacuate(xi, l, s, 1)
                normalise(6)
                normalise(7)

            def mixer_a():
                for k in slots(CH_A_KV // 4, 0):
                    if k % 2 == 0 and k // 2 + 2 < KC:
                        xt_evacuate(0, 0, 0, k // 2 + 2)
                    if k == 7:
                        dve.wait_ge(par_turned, 1)
                        dve.tensor_copy(lncol[:, :, :, :, :].rearrange("p a l s k -> p (a l s k)"), ps[:, 2, 0:P]).then_inc(par_ready, 1)
                        for l in range(DEPTH):
                            dve.wait_ge(par_turned, l + 2)
                            dve.tensor_copy(convcol[:, l].rearrange("p w t -> p (w t)"), ps[:, 2 + (1 + l) % 2, 0:8 * FT]).then_inc(par_ready, 2)
                for k in slots(CH_A_Q // 4, 0):
                    if k == 0:
                        dve.wait_ge(chunks_used, CH_A_Q)
                        dve.wait_ge(par_turned, 3)
                        dve.tensor_copy(vall[:, 1, :], bank(0, 1)[:, KV_HEADS * HD:])
                        both = tok[:, 1, :].rearrange("p (h c d) -> p h c d", c=2, d=HD)
                        for c in range(2):
                            last = dve.tensor_copy(both[:, :, c, :], bank(0, 1)[:, 0:KV_HEADS * HD].rearrange("p (h d) -> p h d", d=HD))
                        last.then_inc(acc_free[0], 1)
                    if k == 2:
                        turned_copy(kTall, 0, TT_A)

                def turn(n, b4, nk=KT):
                    tok_copy(1, n * KC + CH_A_Q, n + TT_A, SCALE)
                    for k in slots(b4, 0, nk):
                        if k == 2:
                            turned_copy(qT, 0, n + TT_A)
                        attention_slot(k, (n - 1) * HG, (n - 1) * 2, (n - 1) * 4, n - 1, True)
                        if k == OUT_DONE:
                            out_residual(0, 0)

                with dve.Fori(0, GROUPS - 1) as i:
                    own.enter(i, 4)
                    turn(i + 1, i * (KC // 4) + (CH_A_Q + KC) // 4)
                    own.leave(GROUPS - 1)
                turn(GROUPS, CH_O[0] // 4, 2 * KT)

            def decay(k):
                z, nabs, e, u, lnu, d, zero, cum, ncum = fs
                if k == 3:
                    dve.wait_ge(fz_done, 1)
                    dve.wait_ge(wf_in, 32)
                    own.link(dve.tensor_scalar(z[:, :], ps[0:HEADS, 6, 0:SEQ], fbc[:, 0:1], None, ALU.add))
                    dve.scalar_tensor_tensor(nabs[:, :], z[:, :], -1.0, z[:, :], ALU.mult, ALU.min).then_inc(decay_abs, 1)
                if k == 7:
                    dve.wait_ge(decay_exp, 1)
                    dve.tensor_scalar(u[:, :], e[:, :], 1.0, None, ALU.add).then_inc(decay_u, 1)
                    dve.wait_ge(decay_u, 1)
                    own.link(dve.tensor_scalar(d[:, :], u[:, :], -1.0, None, ALU.add))
                    own.link(dve.tensor_scalar(zero[:, :], d[:, :], 0.0, None, ALU.is_equal))
                    own.link(dve.tensor_tensor(d[:, :], d[:, :], zero[:, :], ALU.add))
                    own.link(dve.reciprocal(d[:, :], d[:, :]))
                    own.link(dve.tensor_tensor(d[:, :], d[:, :], e[:, :], ALU.mult))
                if k == 9:
                    dve.wait_ge(decay_ln, 1)
                    own.link(dve.tensor_tensor(lnu[:, :], lnu[:, :], zero[:, :], ALU.add))
                    own.link(dve.tensor_tensor(d[:, :], lnu[:, :], d[:, :], ALU.mult))
                    own.link(dve.scalar_tensor_tensor(z[:, :], z[:, :], 0.0, d[:, :], ALU.min, ALU.subtract))
                    own.link(dve.memset(zero[:, :], 1.0))
                    own.link(dve.tensor_tensor_scan(cum[:, :], zero[:, :], z[:, :], 0.0, ALU.mult, ALU.add))
                    dve.tensor_scalar(ncum[:, :], cum[:, :], -1.0, None, ALU.mult).then_inc(cum_ready, 1)
                if k == 13:
                    dve.wait_ge(cum_turned, 1)
                    dve.tensor_copy(cumq[:, :, :], ps[:, 7, 0:MT * HEADS].rearrange("p (m h) -> p m h", m=MT)).then_inc(cumq_ready, 1)

            def mixer_b():
                def turn(n, b4, first=False, nk=KT):
                    if not first:
                        dve.wait_ge(pv_done, n * HG + (GROUPS - 1) * HG)
                        dve.wait_ge(chunks_used, n * (3 * KC) + CH_B)
                        dve.tensor_copy(vv[:, 1, :], bank(0, 1)).then_inc(acc_free[0], 1)
                    for k in slots(b4, 0, nk):
                        if first:
                            xt_next(2, 0, 1, k)
                            if k == 13:
                                dve.wait_ge(wf_high, 1)
                                dve.tensor_tensor(wf_lo[:, :, :], wf[:, :, :], wf_hi[:, :, :].bitcast(FP32), ALU.subtract).then_inc(wf_low, 1)
                            continue
                        attention_slot(k, (n + (GROUPS - 1)) * HG, (n + (GROUPS - 1)) * 2, (n - 1) * 4, n + (GROUPS - 1), False)
                        if k == OUT_DONE:
                            out_residual(1, 0)
                    if nk > KT:
                        return
                    tok_copy(0, n * (3 * KC) + (CH_B + KC), n * 2 + TT_B, SCALE)
                    for k in slots(b4, KC):
                        if k == 2:
                            turned_copy(qT, 0, n * 2 + TT_B)
                        if first:
                            decay(k)
                    tok_copy(1, n * (3 * KC) + (CH_B + 2 * KC), n * 2 + (TT_B + 1))
                    for k in slots(b4, 2 * KC):
                        if k == 2:
                            turned_copy(kT, 1, n * 2 + (TT_B + 1))

                turn(0, CH_B // 4, first=True)
                with dve.Fori(0, GROUPS - 1) as i:
                    own.enter(i, 2)
                    turn(i + 1, i * (3 * KC // 4) + (CH_B + 3 * KC) // 4)
                    own.leave(GROUPS - 1)
                turn(GROUPS, CH_O[1] // 4, nk=2 * KT)

            def conv(dst, h, l, n, j0):
                dve.wait_ge(conv_started, n * 8 + (l * 8 * UP_PAIRS + 4 * h + j0 + 2))
                for tap in (1, 0):
                    for j in (j0, j0 + 1):
                        lag = 2 - tap
                        src = ps[:, 2 * h + j // 2, (j % 2) * SEQ:(j % 2 + 1) * SEQ - lag]
                        last = dve.scalar_tensor_tensor(dst[:, j, lag:SEQ], src, cw[:, h, tap, j:j + 1], dst[:, j, lag:SEQ],
                                                        ALU.mult, ALU.add)
                        if tap == 0 and j0 == 2:
                            last.then_inc(acc_free[h], 1)
                    if tap == 1:
                        own.link(last)

            def up_copy(l, n):
                tok_copy(1, n * (2 * KC) + (CH_UP[l] + 2 * KC), n * 2 + (TT_UP[l] + 1))

            def up_finish(k, l, n):
                if k in (5, 7):
                    conv(cu, 1, l, n, k - 5)
                if k == 9:
                    dve.wait_ge(acc_free[1], n * 4 + 2 * (TURN_UP[l][1] + 2))
                    dve.wait_ge(silu_done, n + (l * UP_PAIRS + 1))
                    dve.tensor_tensor(cu[:, :, :], cu[:, :, :], cg[:, :, :], ALU.mult).then_inc(prod_ready, 1)
                if k == 13:
                    dve.wait_ge(hid_high, n + (l * UP_PAIRS + 1))
                    at = bass.ds(n * 4, 4)
                    dve.tensor_tensor(hid_l[:, at, :], cu[:, :, :], hid_h[:, at, :].bitcast(FP32), ALU.subtract).then_inc(hid_low, 1)

            def mlp(l):
                def turn(n, b4, first=False):
                    if not first:
                        up_copy(l, n - 1)
                    for k in slots(b4, 0):
                        if first:
                            xt_next(1 + 2 * l, l, 0, k)
                        else:
                            up_finish(k, l, n - 1)
                    tok_copy(0, n * (2 * KC) + (CH_UP[l] + KC), n * 2 + TT_UP[l])
                    for k in slots(b4, KC):
                        if k in (5, 7):
                            conv(cg, 0, l, n, k - 5)

                turn(0, CH_UP[l] // 4, first=True)
                with dve.Fori(0, UP_PAIRS - 1) as i:
                    own.enter(i, 4)
                    turn(i + 1, i * (2 * KC // 4) + (CH_UP[l] + 2 * KC) // 4)
                    own.leave(UP_PAIRS - 1)
                b4, (t0, t1) = CH_DOWN[l] // 4, TURN_DOWN[l]
                pieces = 4 if l == 0 else 12
                up_copy(l, UP_PAIRS - 1)
                for k in slots(b4, 0, KT):
                    up_finish(k, l, UP_PAIRS - 1)
                split_run(b4, KC + LOW_AHEAD, FC - KC)
                for n in range(1, OUT_GROUPS):
                    residual((n - 1) % 2, (t0, t1)[(n - 1) % 2] + (n - 1) // 2, CH_DOWN[l] + n * FC, n - 1, pieces)
                    split_run(b4, n * FC + LOW_AHEAD, FC - (LOW_AHEAD if l == DEPTH - 1 and n == OUT_GROUPS - 1 else 0))
                n = OUT_GROUPS
                return residual((n - 1) % 2, (t0, t1)[(n - 1) % 2] + (n - 1) // 2, CH_DOWN[l] + n * FC, n - 1, pieces)

            xt_evacuate(0, 0, 0, 0)
            split(0, 0)
            xt_evacuate(0, 0, 0, 1)
            for c in range(1, LOW_AHEAD):
                split(0, c)
            mixer_a()
            for l in range(DEPTH):
                if l == 1:
                    mixer_b()
                norm_and_first(1 + 2 * l, l, 0, out_projection(l))
                last = mlp(l)
                if l == 0:
                    norm_and_first(2, 0, 1, last)
            layer_norm(4, last)
            dve.wait_ge(full_in, 32)
            for i in range(3):
                cols = slice(i * COLS, (i + 1) * COLS)
                for m in range(MT):
                    last = dve.scalar_tensor_tensor(res[:, m, cols], res[:, m, cols], mv[:, m, 0:1], lnfull[:, 0, cols],
                                                    ALU.subtract, ALU.mult)
                own.link(last)
                for m in range(MT):
                    dve.scalar_tensor_tensor(res[:, m, cols], res[:, m, cols], rstd[:, 2, m:m + 1], lnfull[:, 1, cols],
                                             ALU.mult, ALU.add).then_inc(fin_ready, 1)

        @block.tensor
        def _(pe):
            def product(s, k, nk, lh, ll, slot):
                for m in range(MT):
                    rows = slice(m * P, (m + 1) * P)
                    o = bank(s, m)
                    pe.matmul(o, lh[:, k, rows], w_lo[:, slot, k % 2, :], start=(k == 0), stop=False)
                    pe.matmul(o, ll[:, k, rows], w_hi[:, slot, k % 2, :], start=False, stop=False)
                    last = pe.matmul(o, lh[:, k, rows], w_hi[:, slot, k % 2, :], start=False, stop=(k == nk - 1))
                return last

            def group(s, turn, b4, loc0, lh=xh, ll=xl, nk=KT, before=None):
                pe.wait_ge(acc_free[s], 2 * turn)
                for k in range(nk):
                    loc = loc0 + k // 2
                    if k % 2 == 0:
                        if before:
                            before(k // 2)
                        pe.wait_ge(low_ready, b4 * 4 + (loc + 1))
                    last = product(s, k, nk, lh, ll, loc % RING)
                    if k % 2 == 1:
                        last.then_inc(chunks_used, 1)
                    yield k

            def xt_turn(xi, g):
                if xi == 0:
                    pe.wait_ge(res_in[g // 2], 16)
                else:
                    pe.wait_ge(z0_ready, KC * (xi - 1) + g + 1)
                    pe.wait_ge(z1_ready, KC * (xi - 1) + g + 1)
                for a in range(2):
                    k = 2 * g + a
                    for m in range(MT):
                        last = pe.transpose(ps[:, X_BANK + g % 4, a * SEQ + m * P:a * SEQ + (m + 1) * P],
                                            res[:, m, k * P:(k + 1) * P], ident[:, :])
                last.then_inc(xt_turned, 1)

            def x_ready(xi):
                def before(c):
                    if c == 0:
                        xt_turn(xi, 0)
                        xt_turn(xi, 1)
                    pe.wait_ge(xt_low, KC * xi + c + 1)
                return before

            def x_next(xi, k):
                if k == 0:
                    xt_turn(xi, 2)
                if k % 2 == 0 and k // 2 + 3 < KC:
                    xt_turn(xi, k // 2 + 3)

            def turn_tok(s, turn, source_free, source_turns, n_tiles=4):
                pe.wait_ge(acc_free[source_free], source_turns)
                pe.wait_ge(acc_free[s], 2 * turn)
                for j in range(4):
                    for m in range(MT):
                        last = pe.transpose(ps[:, 2 * s + j // 2, (j % 2) * SEQ + m * P:(j % 2) * SEQ + (m + 1) * P],
                                            tok[:, m, j * P:(j + 1) * P], ident[:, :])
                last.then_inc(tok_turned, 1)

            def attend(s, hc, quads, shared, first_waits, value_waits):
                if s < HG:
                    if s == 0:
                        first_waits()
                    if s >= 2:
                        pe.wait_ge(scores_used, hc + (s - 1))
                    if s == 0:
                        pe.wait_ge(oT_low, quads)
                    rows = slice(HD * (s % 2), HD * (s % 2) + HD)
                    kt = 0 if shared else s // 2
                    o = ps[:, S_BANK + s % 2, :]
                    pe.matmul(o[:, 0:P], qT[rows, s // 2, 0:P], kT[rows, kt, 0:P], start=True, stop=True)
                    pe.matmul(o[:, P:SPAN], qT[rows, s // 2, P:SEQ], kT[rows, kt, :], start=True, stop=True).then_inc(scores_ready, 1)
                j = s - 2
                if 0 <= j < HG:
                    pe.wait_ge(probs_ready, hc + (j + 1))
                    if j >= 1:
                        pe.wait_ge(probsT_ready, hc + j)
                    for b in range(3):
                        last = pe.transpose(ps[:, PT_BANK, b * P:(b + 1) * P], prob[:, j % 4, b * P:(b + 1) * P], ident[:, :])
                    last.then_inc(probsT_turned, 1)
                j = s - 3
                if 0 <= j < HG:
                    if j == 0:
                        value_waits()
                    if j % 4 == 0:
                        pe.wait_ge(o_ready, quads + j // 4)
                    pe.wait_ge(probsT_ready, hc + (j + 1))
                    cols = slice(0, HD) if shared else slice(j * HD, (j + 1) * HD)
                    o = [ps[:, O_BANK, m * 4 * HD + (j % 4) * HD:m * 4 * HD + (j % 4 + 1) * HD] for m in range(MT)]
                    pt = probT[:, j % 2, :]
                    pe.matmul(o[0], pt[:, 0:P], vv[:, 0, cols], start=True, stop=True)
                    pe.matmul(o[1], pt[:, P:2 * P], vv[:, 0, cols], start=True, stop=False)
                    pe.matmul(o[1], pt[:, 2 * P:SPAN], vv[:, 1, cols], start=False, stop=True).then_inc(pv_done, 1)

            def turn_out(q, quads):
                pe.wait_ge(o_ready, quads + (q + 1))
                for a in range(2):
                    for m in range(MT):
                        last = pe.transpose(ps[:, S_BANK + q, a * SEQ + m * P:a * SEQ + (m + 1) * P],
                                            onorm[:, m, a * P:(a + 1) * P], ident[:, :])
                last.then_inc(oT_turned, 1)

            def attention_slot(k, hc, quads, shared, first_waits, value_waits):
                if FIRST_STEP <= k < FIRST_STEP + STEPS:
                    attend(k - FIRST_STEP, hc, quads, shared, first_waits, value_waits)
                if k == 11:
                    pe.wait_ge(scores_used, hc + HG)
                    turn_out(0, quads)
                if k == 14:
                    turn_out(1, quads)

            def out_pair(l):
                for slot, (i, k) in enumerate(WOVEN_OUT):
                    s = (i + 1) % 2
                    if k == 0:
                        pe.wait_ge(acc_free[s], 2 * TURN_O[l][s])
                    if slot == 0:
                        pe.wait_ge(oT_low, 2 * GROUPS * l + 2 * (GROUPS - 1))
                    if i == 0 and k in (LATE, LATE + 2):
                        pe.wait_ge(oT_low, 2 * GROUPS * l + 2 * (GROUPS - 1) + (k - LATE) // 2 + 1)
                    if slot % 2 == 0:
                        pe.wait_ge(low_ready, CH_O[l] + slot // 2 + 1)
                    last = product(s, k, KT, oh, ol, (slot // 2) % RING)
                    if slot % 2 == 1:
                        last.then_inc(chunks_used, 1)
                    yield slot

            def mixer_a():
                for k in group(0, TURN_A_KV, CH_A_KV // 4, 0, before=x_ready(0)):
                    x_next(0, k)
                    if k == 7:
                        pe.wait_ge(par_in, 96)
                        rows = tok[:, :, :].rearrange("p m (a b) -> p (m a) b", b=P)
                        pe.transpose(ps[:, 2, 0:P], cu[:, 0, 0:P], ident[:, :]).then_inc(par_turned, 1)
                        for l in range(DEPTH):
                            if l == 1:
                                pe.wait_ge(par_ready, 1)
                            for w in range(4):
                                last = pe.transpose(ps[:, 2 + (1 + l) % 2, w * 2 * FT:(w + 1) * 2 * FT],
                                                    rows[0:2 * FT, 4 * l + w, :], ident[0:2 * FT, 0:2 * FT])
                            last.then_inc(par_turned, 1)
                pe.wait_ge(par_ready, 5)
                for k in group(1, TURN_A_Q, CH_A_Q // 4, 0):
                    if k == 1:
                        turn_tok(0, TURN_A_KV + 1, 0, 2 * (TURN_A_KV + 1))

                def woven(k, n):
                    if k == 1:
                        turn_tok(0, n - 1 + TURN_A_QT, 1, 2 * (n + TURN_A_Q))

                    def first_waits():
                        pe.wait_ge(acc_free[0], 2 * (n + TURN_A_QT))
                        pe.wait_ge(kv_ready, 2 * n - 1)
                    attention_slot(k, (n - 1) * HG, (n - 1) * 2, True, first_waits, lambda: pe.wait_ge(kv_ready, 2 * n))

                with pe.Fori(0, GROUPS - 1) as i:
                    for k in group(1, i + (TURN_A_Q + 1), i * (KC // 4) + (CH_A_Q + KC) // 4, 0):
                        woven(k, i + 1)
                for k in out_pair(0):
                    woven(k, GROUPS)

            def mixer_b():
                t0, t1 = TURN_B

                def woven(k, n):
                    def first_waits():
                        pe.wait_ge(acc_free[1], 2 * (n * 2 + t1))
                        pe.wait_ge(acc_free[0], 2 * (n * 3 - 1 + t0))
                    attention_slot(k, (n + (GROUPS - 1)) * HG, (n + (GROUPS - 1)) * 2, False, first_waits,
                                   lambda: pe.wait_ge(acc_free[0], 2 * (n * 3 + t0)))

                def turn(n, b4, first=False):
                    for k in group(0, n * 3 + t0, b4, 0, before=x_ready(2) if first else None):
                        if first:
                            x_next(2, k)
                        else:
                            woven(k, n)
                    if first:
                        pe.wait_ge(wf_low, 1)
                        o = ps[0:HEADS, 6, 0:SEQ]
                        for k in range(KT):
                            pe.matmul(o, wf_lo[:, k, :], xh[:, k, :], start=(k == 0), stop=False)
                            pe.matmul(o, wf_hi[:, k, :], xl[:, k, :], start=False, stop=False)
                            last = pe.matmul(o, wf_hi[:, k, :], xh[:, k, :], start=False, stop=(k == KT - 1))
                        last.then_inc(fz_done, 1)
                    for k in group(1, n * 2 + t1, b4, KC):
                        if k == 1:
                            turn_tok(0, n * 3 + (t0 + 1), 0, 2 * (n * 3 + (t0 + 1)))
                        if first and k == 12:
                            pe.wait_ge(cum_ready, 1)
                            for m in range(MT):
                                last = pe.transpose(ps[:, 7, m * HEADS:(m + 1) * HEADS], fs[7][:, m * P:(m + 1) * P],
                                                    ident[0:HEADS, 0:HEADS])
                            last.then_inc(cum_turned, 1)
                    for k in group(0, n * 3 + (t0 + 2), b4, 2 * KC):
                        if k == 1:
                            turn_tok(1, n * 2 + (t1 + 1), 1, 2 * (n * 2 + (t1 + 1)))

                turn(0, CH_B // 4, first=True)
                with pe.Fori(0, GROUPS - 1) as i:
                    turn(i + 1, i * (3 * KC // 4) + (CH_B + 3 * KC) // 4)
                for k in out_pair(1):
                    woven(k, GROUPS)

            def out_projection(l):
                for i in range(2, OUT_GROUPS):
                    for k in group((i + 1) % 2, TURN_O[l][(i + 1) % 2] + 1, CH_O[l] // 4, i * KC, oh, ol):
                        pass

            def mlp(l):
                t0, t1 = TURN_UP[l]

                def turn(n, b4, first=False):
                    for k in group(0, n * 2 + t0, b4, 0, before=x_ready(1 + 2 * l) if first else None):
                        if first:
                            x_next(1 + 2 * l, k)
                        elif k == 2:
                            turn_tok(1, n * 2 + (t1 - 1), 1, 2 * (n * 2 + (t1 - 1)))
                    for k in group(1, n * 2 + t1, b4, KC):
                        if k == 2:
                            turn_tok(0, n * 2 + (t0 + 1), 0, 2 * (n * 2 + (t0 + 1)))

                turn(0, CH_UP[l] // 4, first=True)
                with pe.Fori(0, UP_PAIRS - 1) as i:
                    turn(i + 1, i * (2 * KC // 4) + (CH_UP[l] + 2 * KC) // 4)
                last_turn = t1 + 2 * UP_PAIRS - 1
                turn_tok(1, last_turn, 1, 2 * last_turn)
                with pe.Fori(0, OUT_GROUPS // 2) as n:
                    for i in range(2):
                        for k in group(i, n + TURN_DOWN[l][i], n * (2 * FC // 4) + CH_DOWN[l] // 4, i * FC, hid_h, hid_l, FT,
                                       before=lambda c: pe.wait_ge(hid_low, UP_PAIRS * (l + 1) - (1 if c < FC - 2 else 0))
                                       if c in (0, FC - 2) else None):
                            pass

            pe.wait_ge(ident_ready, 1)
            mixer_a()
            for l in range(DEPTH):
                if l == 1:
                    mixer_b()
                out_projection(l)
                mlp(l)


_INS = ['x', 'a_w_qkv', 'a_w_o', 'a_sinks', 'rel_bias', 'b_w_qkvf', 'b_f_bias', 'b_w_o',
        'ffn_w_up', 'ffn_conv_w', 'ffn_conv_b', 'ffn_w_down', 'ln_g', 'ln_b']
_OUTS = [((1, 256, 2048), 'float32')]


def kernel(**inputs):
    import numpy as _np
    import concourse.bacc as _bacc
    from concourse import mybir as _mybir
    from concourse.bass_utils import run_bass_kernel_spmd as _run

    nc = _bacc.Bacc("TRN2", target_bir_lowering=False, num_devices=1)
    arrays, args = {}, []
    for name in _INS:
        a = _np.ascontiguousarray(inputs[name])
        arrays[f"in_{name}_dram"] = a
        args.append(nc.dram_tensor(f"in_{name}_dram", a.shape, _mybir.dt.from_np(a.dtype), kind="ExternalInput").ap())
    for i, (shape, dtype) in enumerate(_OUTS):
        dt = _mybir.dt.from_np(_np.dtype(dtype))
        args.append(nc.dram_tensor(f"out_{i}_dram", shape, dt, kind="ExternalOutput").ap())
    trunk(nc, *args)
    r = _run(nc, [arrays], core_ids=[0])
    got = tuple(r.results[0][f"out_{i}_dram"] for i in range(len(_OUTS)))
    return got[0]
```

```python
import math
from contextlib import ExitStack

import concourse.bass as bass
from concourse import mybir

FP32 = mybir.dt.float32
F32R = mybir.dt.float32r
ALU = mybir.AluOpType
ACT = mybir.ActivationFunctionType

P = 128
D = 2048
SEQ = 256
MT = SEQ // P
DEPTH = 2
HD = 64
HEADS = D // HD
KV_HEADS = 4
BUCKETS = 32
MAX_DIST = 128
D_FF = 5632
COLS = 512
KT = D // P
FT = D_FF // P
HG = 8
GROUPS = HEADS // HG
UP_PAIRS = D_FF // COLS
OUT_GROUPS = D // COLS
RING = 4
AHEAD = 3
LOW_AHEAD = 2
ALPHA = (2 * DEPTH) ** 0.25
SCALE = HD ** -0.5
LN_EPS = 1e-5
GP_COLS = slice(D - 5 * P, D)
DVE_FULL = (0, 1, 2, 4, 6)
FULLS = len(DVE_FULL)
MASKED = -3.0e38
SPAN = 3 * P
FIRST_STEP = 3
STEPS = HG + 3

KC = KT // 2
FC = FT // 2
CH_A_KV = 0
CH_A_Q = CH_A_KV + KC
CH_O = [CH_A_Q + GROUPS * KC]
CH_UP = [CH_O[0] + OUT_GROUPS * KC]
CH_DOWN = [CH_UP[0] + 2 * UP_PAIRS * KC]
CH_B = CH_DOWN[0] + OUT_GROUPS * FC
CH_O.append(CH_B + 3 * GROUPS * KC)
CH_UP.append(CH_O[1] + OUT_GROUPS * KC)
CH_DOWN.append(CH_UP[1] + 2 * UP_PAIRS * KC)
CH_END = CH_DOWN[1] + OUT_GROUPS * FC

TURN_A_KV = 0
TURN_A_QT = 2
TURN_A_Q = 0
TURN_O = [(TURN_A_QT + GROUPS, TURN_A_Q + GROUPS)]
TURN_UP = [tuple(t + 2 for t in TURN_O[0])]
TURN_DOWN = [tuple(t + 2 * UP_PAIRS for t in TURN_UP[0])]
TURN_B = tuple(t + 2 for t in TURN_DOWN[0])
TURN_O.append((TURN_B[0] + 3 * GROUPS, TURN_B[1] + 2 * GROUPS))
TURN_UP.append(tuple(t + 2 for t in TURN_O[1]))
TURN_DOWN.append(tuple(t + 2 * UP_PAIRS for t in TURN_UP[1]))

TT_A = 0
TT_UP = [TT_A + 1 + GROUPS]
TT_B = TT_UP[0] + 2 * UP_PAIRS
TT_UP.append(TT_B + 2 * GROUPS)

LATE = KT - KT // GROUPS
OUT_DONE = 2 * KT - KT // GROUPS
WOVEN_OUT = [(i, k) for ks in (range(LATE), range(LATE, KT)) for i in range(2) for k in ks]


def bucket(dist):
    exact = BUCKETS // 2
    if dist < exact:
        return dist
    return min(BUCKETS - 1, exact + int(math.log(dist / exact) / math.log(MAX_DIST / exact) * (BUCKETS - exact)))


BIAS_AFTER = [(0, KC - 1), (1, KC // 2 - 1), (1, KC - 1)]


class Links:

    def __init__(self, eng, sem):
        self.eng, self.sem, self.base, self.n = eng, sem, 0, 0

    def link(self, ins):
        ins.then_inc(self.sem, 1)
        self.n += 1
        self.eng.wait_ge(self.sem, self.base + self.n)

    def enter(self, i, per):
        self.start, self.per = self.n + (self.base if isinstance(self.base, int) else 0), per
        self.base, self.n = i * per + self.start, 0

    def leave(self, turns):
        assert self.n == self.per, (self.n, self.per)
        self.base, self.n = self.start + turns * self.per, 0


def trunk(nc, x, a_w_qkv, a_w_o, a_sinks, rel_bias, b_w_qkvf, b_f_bias, b_w_o,
          ffn_w_up, ffn_conv_w, ffn_conv_b, ffn_w_down, ln_g, ln_b, out):
    ctx = ExitStack()
    with ctx:
        def sb(name, shape, dt=FP32, where=ctx):
            return where.enter_context(nc.sbuf_tensor(name, shape, dt))

        def sem(name):
            return ctx.enter_context(nc.semaphore(name))

        res = sb("res", [P, MT, D])
        raw = sb("raw", [P, RING, 2, COLS])
        w_hi = sb("w_hi", [P, RING, 2, COLS], F32R)
        w_lo = sb("w_lo", [P, RING, 2, COLS], F32R)
        tok = sb("tok", [P, MT, COLS])
        cg = sb("cg", [P, 4, SEQ])
        cu = sb("cu", [P, 4, SEQ])
        lnp = sb("lnp", [P, 2, COLS])
        ident = sb("ident", [P, P])
        lncol = sb("lncol", [P, 2, DEPTH, 2, KT])
        convcol = sb("convcol", [P, DEPTH, 4, 2 * FT])
        cw = sb("cw", [P, 2, 4, 4])
        stats = sb("stats", [P, MT, OUT_GROUPS, 6])
        mv = sb("mv", [P, MT, 2])
        var = sb("var", [P, MT])
        sd = sb("sd", [P, MT])
        rstd = sb("rstd", [P, 3, MT])
        mark = sb("mark", [P, HG])
        nmr = sb("nmr", [P, MT])
        warm = sb("warm", [P, 1])
        with ExitStack() as first:
            xh = sb("xh", [P, KT, SEQ], F32R, first)
        with ExitStack() as later:
            lnfull = sb("lnfull", [P, 2, D], FP32, later)
        xh_hold = sb("xh_hold", [P, KT * SEQ])
        xl = sb("xl", [P, KT, SEQ], F32R)
        with ExitStack() as mix:
            oh = sb("oh", [P, KT, SEQ], F32R, mix)
            ol = sb("ol", [P, KT, SEQ], F32R, mix)
            bias = sb("bias", [P, HG, SPAN], FP32, mix)
            qT = sb("qT", [P, 4, SEQ], FP32, mix)
            kT = sb("kT", [P, 4, SEQ], FP32, mix)
            vv = sb("vv", [P, MT, COLS], FP32, mix)
            kTall = sb("kTall", [P, KV_HEADS, SEQ], FP32, mix)
            vall = sb("vall", [P, MT, KV_HEADS * HD], FP32, mix)
            prob = sb("prob", [P, 4, SPAN], FP32, mix)
            probT = sb("probT", [P, 2, SPAN], FP32, mix)
            onorm = sb("onorm", [P, MT, 4 * HD], FP32, mix)
            nmax = sb("nmax", [P, MT, HG], FP32, mix)
            rsum = sb("rsum", [P, 2, MT, 4], FP32, mix)
            esink = sb("esink", [P, 2, MT, 4], FP32, mix)
            den = sb("den", [P, 2, MT * 4], FP32, mix)
            rden = sb("rden", [P, 2, MT * 4], FP32, mix)
            sinks = sb("sinks", [P, 2, HEADS], FP32, mix)
            sinkc = sb("sinkc", [P, 2, HG], FP32, mix)
            relT = sb("relT", [BUCKETS, HEADS], FP32, mix)
            reld = sb("reld", [HEADS, SPAN], FP32, mix)
            wf = sb("wf", [P, KT, HEADS], FP32, mix)
            wf_hi = sb("wf_hi", [P, KT, HEADS], F32R, mix)
            wf_lo = sb("wf_lo", [P, KT, HEADS], F32R, mix)
            fbc = sb("fbc", [HEADS, 1], FP32, mix)
            fs = [sb(f"fs{i}", [HEADS, SEQ], FP32, mix) for i in range(9)]
            cumq = sb("cumq", [P, MT, HEADS], FP32, mix)
        hid_h = sb("hid_h", [P, FT, SEQ], F32R)
        hid_l = sb("hid_l", [P, FT, SEQ], F32R)
        ps = ctx.enter_context(nc.psum_tensor("ps", [P, 8, COLS], FP32))
        S_BANK, O_BANK, PT_BANK, X_BANK = 4, 6, 7, 4
        FIRST_BANK = X_BANK + 3

        rel_dram = nc.dram_tensor("rel_by_distance", (HEADS, P, SPAN), FP32).ap()
        cum_dram = nc.dram_tensor("minus_cumulated_decay", (HEADS, SEQ), FP32).ap()

        raw_in = [sem(f"raw_in{i}") for i in range(RING)]
        res_in = [sem(f"res_in{i}") for i in range(4)]
        par_in = sem("par_in")
        high_ready = sem("high_ready")
        low_ready = sem("low_ready")
        chunks_used = sem("chunks_used")
        acc_free = [[sem(f"acc_free{s}{m}") for m in range(MT)] for s in range(2)]
        tok_tile0 = sem("tok_tile0")
        v_tile0 = sem("v_tile0")
        last_tile0 = sem("last_tile0")
        tok_turned = sem("tok_turned")
        ident_ready = sem("ident_ready")
        par_turned = sem("par_turned")
        par_ready = sem("par_ready")
        xt_turned = sem("xt_turned")
        xt_full = sem("xt_full")
        first_turned = sem("first_turned")
        first_full = sem("first_full")
        first_high = sem("first_high")
        first_low = sem("first_low")
        xt_high = sem("xt_high")
        xt_low = sem("xt_low")
        scores_ready = sem("scores_ready")
        scores_used = sem("scores_used")
        probs_ready = sem("probs_ready")
        probsT_turned = sem("probsT_turned")
        probsT_ready = sem("probsT_ready")
        pv_done = sem("pv_done")
        o_ready = sem("o_ready")
        oT_turned = sem("oT_turned")
        oT_high = sem("oT_high")
        oT_low = sem("oT_low")
        rel_built = sem("rel_built")
        rel_out = sem("rel_out")
        bias_ready = sem("bias_ready")
        kv_ready = sem("kv_ready")
        conv_started = sem("conv_started")
        silu_done = sem("silu_done")
        prod_ready = sem("prod_ready")
        hid_high = sem("hid_high")
        hid_low = sem("hid_low")
        cw_ready = sem("cw_ready")
        var_ready = sem("var_ready")
        sd_ready = sem("sd_ready")
        norm_ready = sem("norm_ready")
        z0_ready = sem("z0_ready")
        z1_ready = sem("z1_ready")
        res_ready = sem("res_ready")
        wf_in = sem("wf_in")
        wf_high = sem("wf_high")
        wf_low = sem("wf_low")
        fz_done = sem("fz_done")
        decay_abs = sem("decay_abs")
        decay_exp = sem("decay_exp")
        decay_u = sem("decay_u")
        decay_ln = sem("decay_ln")
        cum_ready = sem("cum_ready")
        cum_turned = sem("cum_turned")
        cumq_ready = sem("cumq_ready")
        fin_ready = sem("fin_ready")
        fin_gp = sem("fin_gp")
        full_in = sem("full_in")
        out_done = sem("out_done")
        gp_in = sem("gp_in")
        dve_own = sem("dve_own")
        act_own = sem("act_own")
        gp_own = sem("gp_own")

        block = ctx.enter_context(nc.Block())

        def k_tiles(w):
            return w.rearrange("(k p) n -> p k n", p=P)

        def bank(s, m):
            return ps[:, 2 * s + m, :]

        def wait_free(eng, s, turns):
            for m in range(MT):
                eng.wait_ge(acc_free[s][m], turns)

        @block.sync
        def _(sp):
            def load_input(i):
                sp.dma_start(res[:, :, i * COLS:(i + 1) * COLS],
                             x[0].rearrange("(m p) d -> p m d", p=P)[:, :, i * COLS:(i + 1) * COLS]).then_inc(res_in[i], 16)

            def repeat_bias(n):
                if n == 0:
                    sp.wait_ge(rel_built, 1)
                else:
                    sp.wait_ge(rel_out, 16 * n)
                heads = slice(n * HG, (n + 1) * HG)
                sp.dma_start(rel_dram[heads], reld[heads, :].unsqueeze(1).to_broadcast([HG, P, SPAN])).then_inc(rel_out, 16)

            def load_chunk(w, col, b4, loc, c):
                if not (isinstance(b4, int) and 4 * b4 + loc < RING):
                    sp.wait_ge(low_ready, b4 * 4 + (loc - RING + 1))
                sp.dma_start(raw[:, loc % RING], w[:, 2 * c:2 * c + 2, bass.ds(col, COLS)]).then_inc(raw_in[loc % RING], 16)

            def load_group(w, col, b4, loc0, chunks):
                for c in range(chunks):
                    load_chunk(w, col, b4, loc0 + c, c)

            wa = k_tiles(a_w_qkv[0])
            wb = k_tiles(b_w_qkvf[0])
            for c in range(KC):
                if c < 4:
                    load_input(c)
                load_chunk(wa, D, CH_A_KV // 4, c, c)
            repeat_bias(0)
            for n in range(2):
                for c in range(KC):
                    load_chunk(wa, n * COLS, n * (KC // 4) + CH_A_Q // 4, c, c)
                    if (n, c) in BIAS_AFTER:
                        repeat_bias(BIAS_AFTER.index((n, c)) + 1)
            with sp.Fori(2, GROUPS) as n:
                load_group(wa, n * COLS, n * (KC // 4) + CH_A_Q // 4, 0, KC)
            for l in range(DEPTH):
                if l == 1:
                    with sp.Fori(0, GROUPS) as n:
                        for part in range(3):
                            load_group(wb, n * COLS + part * D, n * (3 * KC // 4) + CH_B // 4, part * KC, KC)
                wo = k_tiles((a_w_o if l == 0 else b_w_o)[0])
                for loc, (i, k) in enumerate(WOVEN_OUT[::2]):
                    load_chunk(wo, i * COLS, CH_O[l] // 4, loc, k // 2)
                for i in range(2, OUT_GROUPS):
                    load_group(wo, i * COLS, CH_O[l] // 4, i * KC, KC)
                wu = k_tiles(ffn_w_up[l])
                with sp.Fori(0, UP_PAIRS) as n:
                    for i in range(2):
                        load_group(wu, n * COLS + i * D_FF, n * (2 * KC // 4) + CH_UP[l] // 4, i * KC, KC)
                wd = k_tiles(ffn_w_down[l])
                with sp.Fori(0, OUT_GROUPS // 2) as n:
                    for i in range(2):
                        load_group(wd, n * (2 * COLS) + i * COLS, n * (2 * FC // 4) + CH_DOWN[l] // 4, i * FC, FC)
            ov = out[0].rearrange("(m p) d -> p m d", p=P)
            for i in (0, 1, 3, 2):
                if i < 3:
                    cols = slice(i * COLS, min((i + 1) * COLS, GP_COLS.start))
                    sp.wait_ge(fin_ready, 2 * i + 2)
                else:
                    cols = GP_COLS
                    sp.wait_ge(fin_gp, 2)
                sp.dma_start(ov[:, :, cols], res[:, :, cols]).then_inc(out_done, 16)
            sp.wait_ge(out_done, 64)

        @block.gpsimd
        def _(gp):
            own = Links(gp, gp_own)
            own.link(gp.memset(ident[:, :], 0.0))
            gp.affine_select(out=ident[:, :], in_=ident[:, :], compare_op=ALU.not_equal, fill=1.0, base=0,
                             pattern=[[-1, P]], channel_multiplier=1).then_inc(ident_ready, 1)
            gp.dma_start(sinks[:, 0, :], a_sinks[0:1, :].to_broadcast([P, HEADS])).then_inc(gp_in, 16)
            gp.dma_start(relT[:, :], rel_bias.rearrange("b h -> h b"), allow_slow_non_contiguous=True).then_inc(gp_in, 16)
            own.link(gp.memset(reld[:, :], MASKED))
            gp.wait_ge(gp_in, 32)
            own.link(gp.tensor_scalar(sinks[:, 1, :], sinks[:, 0, :], -1.0, None, ALU.mult))
            for b in range(BUCKETS):
                ds_ = [d for d in range(P) if bucket(d) == b]
                lo, n = 2 * P - 1 - ds_[-1], len(ds_)
                last = gp.tensor_copy(reld[:, lo:lo + n], relT[:, b:b + 1].to_broadcast([HEADS, n]))
            own.link(last)
            gp.sem_inc(rel_built, 1)

            with gp.Fori(0, GROUPS) as n:
                own.enter(n, 0)
                gp.wait_ge(rel_out, n * 16 + 16)
                gp.wait_ge(scores_used, n * HG)
                off = n * (HG * P * SPAN)
                for lo, hi, at in ((P, SPAN, P - 1), (0, P, 2 * P - 1)):
                    gp.dma_start(bias[:, :, lo:hi], bass.AP(rel_dram.tensor, off + at, [[SPAN - 1, P], [P * SPAN, HG], [1, hi - lo]])).then_inc(gp_in, 16)
                gp.wait_ge(probs_ready, n * HG)
                gp.tensor_copy(sinkc[:, :, :], sinks[:, :, bass.ds(n * HG, HG)])
                wait_free(gp, 0, TURN_A_KV + 2)
                gp.wait_ge(scores_ready, n * HG)
                gp.tensor_copy(kT[:, 0:1, :], kTall[:, bass.ds(n, 1), :]).then_inc(kv_ready, 1)
                gp.wait_ge(pv_done, n * HG)
                gp.tensor_copy(vv[:, :, 0:HD], vall[:, :, bass.ds(n * HD, HD)]).then_inc(kv_ready, 1)
                gp.wait_ge(gp_in, n * 32 + 64)
                gp.wait_ge(kv_ready, n * 2 + 2)
                gp.sem_inc(bias_ready, 1)
                own.leave(GROUPS)
            gp_loads = 32 + 32 * GROUPS

            def scale_residual(l, s, count, loads):
                row_g, row_b = ln_g[l, s:s + 1, :], ln_b[l, s:s + 1, :]
                for i in range(4):
                    cols = slice(i * COLS, (i + 1) * COLS)
                    gp.dma_start(lnp[:, 0, :], row_g[:, cols].to_broadcast([P, COLS])).then_inc(gp_in, 16)
                    gp.dma_start(lnp[:, 1, :], row_b[:, cols].to_broadcast([P, COLS])).then_inc(gp_in, 16)
                    loads += 32
                    gp.wait_ge(gp_in, loads)
                    gp.wait_ge(xt_turned, KC * (count + 1) + 2 * (i + 1))
                    for m in range(MT):
                        last = gp.tensor_tensor(res[:, m, cols], res[:, m, cols], lnp[:, 0, :], ALU.mult)
                    own.link(last)
                    for m in range(MT):
                        last = gp.tensor_tensor(res[:, m, cols], res[:, m, cols], lnp[:, 1, :], ALU.add)
                    last.then_inc(res_ready, 1)
                    gp.wait_ge(res_ready, 4 * count + i + 1)
                return loads

            def conv_weights(l):
                with gp.Fori(0, UP_PAIRS) as n:
                    for h in range(2):
                        wait_free(gp, h, n * 2 + TURN_UP[l][h])
                        gp.tensor_copy(cw[:, h], convcol[:, l, :, bass.ds(n * 4 + h * FT, 4)]).then_inc(cw_ready, 1)

            gp_loads = scale_residual(0, 0, 0, gp_loads)
            gp.wait_ge(par_ready, 5)
            conv_weights(0)
            gp.wait_ge(chunks_used, CH_B)
            gp.dma_start(wf[:, :, :], k_tiles(b_w_qkvf[0])[:, :, 3 * D:3 * D + HEADS]).then_inc(wf_in, 16)
            gp.dma_start(fbc[:, :], b_f_bias.rearrange("a h -> h a"), allow_slow_non_contiguous=True).then_inc(wf_in, 16)
            gp_loads = scale_residual(0, 1, 1, gp_loads)

            gp.wait_ge(cum_ready, 1)
            gp.dma_start(cum_dram, fs[8][:, :]).then_inc(gp_in, 16)
            gp_loads += 16
            gp.wait_ge(gp_in, gp_loads)
            gp.wait_ge(cumq_ready, 1)
            with gp.Fori(0, GROUPS) as n:
                own.enter(n, 2)
                gp.wait_ge(scores_used, n * HG + GROUPS * HG)
                off = n * (HG * SEQ)
                gp.dma_start(bias[:, :, P:SPAN], bass.AP(cum_dram.tensor, off, [[0, P], [SEQ, HG], [1, 2 * P]])).then_inc(gp_in, 16)
                gp.dma_start(bias[:, :, 0:P], bass.AP(cum_dram.tensor, off, [[0, P], [SEQ, HG], [1, P]])).then_inc(gp_in, 16)
                gp.wait_ge(gp_in, n * 32 + (gp_loads + 32))

                def add_query(a, m):
                    return gp.tensor_tensor(bias[:, :, a:a + P], bias[:, :, a:a + P],
                                            cumq[:, m, bass.ds(n * HG, HG)].unsqueeze(2).to_broadcast([P, HG, P]), ALU.add)
                add_query(P, 1)
                for a in (0, 2 * P):
                    last = gp.affine_select(out=bias[:, :, a:a + P], in_=bias[:, :, a:a + P], compare_op=ALU.is_ge,
                                            fill=MASKED, base=0, pattern=[[0, HG], [-1, P]], channel_multiplier=1)
                own.link(last)
                add_query(0, 0)
                own.link(add_query(2 * P, 1))
                gp.sem_inc(bias_ready, 1)
                own.leave(GROUPS)
            gp_loads += 32 * GROUPS
            gp_loads = scale_residual(1, 0, 2, gp_loads)
            conv_weights(1)
            gp.wait_ge(chunks_used, CH_DOWN[1])
            for i, src in enumerate((ln_g, ln_b)):
                gp.dma_start(lnfull[:, i, :], src[1, 1:2, :].to_broadcast([P, D])).then_inc(full_in, 16)
            gp.wait_ge(full_in, 32)
            for m in range(MT):
                gp.wait_ge(z0_ready, 3 * KC + m + 1)
                own.link(gp.tensor_tensor(res[:, m, GP_COLS], res[:, m, GP_COLS], lnfull[:, 0, GP_COLS], ALU.mult))
                gp.tensor_tensor(res[:, m, GP_COLS], res[:, m, GP_COLS], lnfull[:, 1, GP_COLS], ALU.add).then_inc(fin_gp, 1)

        @block.scalar
        def _(act):
            own = Links(act, act_own)

            def load_table(func):
                own.link(act.activation(warm[:, :], ident[:, 0:1], func))

            act.wait_ge(ident_ready, 1)
            load_table(ACT.Copy)

            def split(b4, loc):
                if isinstance(b4, int) and 4 * b4 + loc >= CH_END:
                    return
                act.wait_ge(raw_in[loc % RING], b4 * 16 + 16 * (loc // RING + 1))
                if not (isinstance(b4, int) and 4 * b4 + loc < RING):
                    act.wait_ge(chunks_used, b4 * 4 + (loc - RING + 1))
                act.activation(w_hi[:, loc % RING], raw[:, loc % RING], ACT.Copy).then_inc(high_ready, 1)

            def slots(b4, loc0, nk=KT):
                for k in range(nk):
                    if k == nk - 2:
                        split(b4, loc0 + k // 2 + AHEAD)
                    yield k
                    if k % 2 == 0 and k != nk - 2:
                        split(b4, loc0 + k // 2 + AHEAD)

            def split_run(b4, loc0, count):
                while loc0 % 4 and count:
                    split(b4, loc0)
                    loc0, count = loc0 + 1, count - 1
                if count >= 8:
                    with act.Fori(0, count // 4) as i:
                        for c in range(4):
                            split(i + (b4 + loc0 // 4), c)
                    loc0, count = loc0 + count // 4 * 4, count % 4
                for c in range(count):
                    split(b4, loc0 + c)

            def xt_evacuate(xi, l, s, g):
                if xi == 0:
                    act.wait_ge(xt_turned, g + 1)
                    src = ps[:, X_BANK + g % 4, :].rearrange("p (a t) -> p a t", a=2)
                else:
                    if g == 0:
                        act.wait_ge(first_full, xi)
                        act.activation(xh[:, 0, :], cg[:, 0, :], ACT.Copy).then_inc(first_high, 1)
                        act.wait_ge(xt_full, FULLS * (xi - 1) + 1)
                        act.activation(xh[:, 1, :], cg[:, 1, :], ACT.Copy).then_inc(xt_high, 1)
                        return
                    src = cg[:, 2 * (g % 2):2 * (g % 2) + 2, :]
                    if g in DVE_FULL:
                        act.wait_ge(xt_full, FULLS * (xi - 1) + DVE_FULL.index(g) + 1)
                    else:
                        act.wait_ge(xt_low, KC * xi + g - 1)
                        act.wait_ge(xt_turned, KC * xi + g + 1)
                        for a in range(2):
                            k = 2 * g + a
                            last = act.activation(cg[:, 2 * (g % 2) + a, :], ps[:, X_BANK + g % 4, a * SEQ:(a + 1) * SEQ],
                                                  ACT.Identity, scale=lncol[:, 0, l, s, k:k + 1], bias=lncol[:, 1, l, s, k:k + 1])
                        own.link(last)
                act.activation(xh[:, 2 * g:2 * g + 2, :], src, ACT.Copy).then_inc(xt_high, 1)

            def tok_copy(s, batch, scale=1.0):
                act.wait_ge(tok_turned, batch)
                act.wait_ge(tok_tile0, batch + 1)
                act.activation(tok[:, 0, :], bank(s, 0), ACT.Copy, scale=scale).then_inc(acc_free[s][0], 1)

            def turned_copy(dst, s, batch):
                act.wait_ge(tok_turned, batch + 1)
                act.activation(dst[:, 0:2, :], bank(s, 0).rearrange("p (a t) -> p a t", a=2), ACT.Copy).then_inc(acc_free[s][0], 1)

            def attend(s, hc, sink):
                if s < HG:
                    act.wait_ge(scores_used, hc + s + 1)
                    q, j = s // 4, s % 4
                    if sink:
                        act.activation(esink[:, q, :, j], nmax[:, :, s], ACT.Exp, bias=sinkc[:, 0, s:s + 1])
                    b = s % 4
                    act.activation(prob[:, b, 0:P], prob[:, b, 0:P], ACT.Exp, scale=-1.0, bias=nmax[:, 0, s:s + 1],
                                   accum_out=rsum[:, q, 0, j:j + 1])
                    act.activation(prob[:, b, P:SPAN], prob[:, b, P:SPAN], ACT.Exp, scale=-1.0, bias=nmax[:, 1, s:s + 1],
                                   accum_out=rsum[:, q, 1, j:j + 1]).then_inc(probs_ready, 1)

            def out_high(q, quads, kt):
                act.wait_ge(oT_turned, quads + (q + 1))
                act.activation(oh[:, bass.ds(kt + 2 * q, 2), :], ps[:, S_BANK + q, :].rearrange("p (a t) -> p a t", a=2),
                               ACT.Copy).then_inc(oT_high, 1)

            def attention_slot(k, hc, quads, kt, sink):
                if FIRST_STEP <= k < FIRST_STEP + STEPS:
                    attend(k - FIRST_STEP, hc, sink)
                if k == 12:
                    out_high(0, quads, kt)
                if k == 14:
                    out_high(1, quads, kt)

            def layer_norm(xi):
                act.wait_ge(var_ready, xi)
                act.activation(sd[:, :], var[:, :], ACT.Sqrt).then_inc(sd_ready, 1)

            def normalise(i):
                cols = slice(i * 2 * P, (i + 1) * 2 * P)
                act.activation(res[:, 0, cols], res[:, 0, cols], ACT.Identity, scale=rstd[:, 2, 0:1],
                               bias=nmr[:, 0:1]).then_inc(z0_ready, 1)

            def norm_and_first(xi, l, s):
                layer_norm(xi)
                act.wait_ge(norm_ready, xi)
                for i in range(2):
                    normalise(i)
                xt_evacuate(xi, l, s, 0)
                for i in range(2, 6):
                    normalise(i)
                xt_evacuate(xi, l, s, 1)
                for i in range(6, KC):
                    normalise(i)

            def mixer_a():
                for k in slots(CH_A_KV // 4, 0):
                    if k % 2 == 0 and k // 2 + 2 < KC:
                        xt_evacuate(0, 0, 0, k // 2 + 2)
                for k in slots(CH_A_Q // 4, 0):
                    if k == 0:
                        act.wait_ge(chunks_used, CH_A_Q)
                        act.activation(vall[:, 0, :], bank(0, 0)[:, KV_HEADS * HD:], ACT.Copy)
                        both = tok[:, 0, :].rearrange("p (h c d) -> p h c d", c=2, d=HD)
                        for c in range(2):
                            last = act.activation(both[:, :, c, :], bank(0, 0)[:, 0:KV_HEADS * HD].rearrange("p (h d) -> p h d", d=HD), ACT.Copy)
                        last.then_inc(acc_free[0][0], 1)
                    if k == 2:
                        turned_copy(kTall, 0, TT_A)

                def turn(n, b4, nk=KT):
                    tok_copy(1, n + TT_A, SCALE)
                    for k in slots(b4, 0, nk):
                        if k == 2:
                            turned_copy(qT, 0, n + TT_A)
                        attention_slot(k, (n - 1) * HG, (n - 1) * 2, (n - 1) * 4, True)

                with act.Fori(0, GROUPS - 1) as i:
                    turn(i + 1, i * (KC // 4) + (CH_A_Q + KC) // 4)
                turn(GROUPS, CH_O[0] // 4, 2 * KT)

            def mixer_b():
                def turn(n, b4, first=False, nk=KT):
                    if not first:
                        load_table(ACT.Exp)
                        act.wait_ge(pv_done, n * HG + (GROUPS - 1) * HG)
                        act.wait_ge(chunks_used, n * (3 * KC) + CH_B)
                        act.activation(vv[:, 1, :], bank(0, 1), ACT.Copy).then_inc(acc_free[0][1], 1)
                    for k in slots(b4, 0, nk):
                        if first:
                            if k % 2 == 0 and k // 2 + 2 < KC:
                                xt_evacuate(2, 0, 1, k // 2 + 2)
                            if k == 13:
                                act.wait_ge(wf_in, 32)
                                act.activation(wf_hi[:, :, :], wf[:, :, :], ACT.Copy).then_inc(wf_high, 1)
                            continue
                        attention_slot(k, (n + (GROUPS - 1)) * HG, (n + (GROUPS - 1)) * 2, (n - 1) * 4, False)
                    if nk > KT:
                        return
                    tok_copy(0, n * 2 + TT_B, SCALE)
                    for k in slots(b4, KC):
                        if k == 2:
                            turned_copy(qT, 0, n * 2 + TT_B)
                        if first and k == 7:
                            act.wait_ge(decay_abs, 1)
                            act.activation(fs[2][:, :], fs[1][:, :], ACT.Exp).then_inc(decay_exp, 1)
                        if first and k == 9:
                            act.wait_ge(decay_u, 1)
                            act.activation(fs[4][:, :], fs[3][:, :], ACT.Ln).then_inc(decay_ln, 1)
                    tok_copy(1, n * 2 + (TT_B + 1))
                    for k in slots(b4, 2 * KC):
                        if k == 2:
                            turned_copy(kT, 1, n * 2 + (TT_B + 1))

                turn(0, CH_B // 4, first=True)
                with act.Fori(0, GROUPS - 1) as i:
                    own.enter(i, 1)
                    turn(i + 1, i * (3 * KC // 4) + (CH_B + 3 * KC) // 4)
                    own.leave(GROUPS - 1)
                turn(GROUPS, CH_O[1] // 4, nk=2 * KT)

            def conv(dst, h, l, n, j0, wait_sem, wait_val):
                if j0 == 0:
                    act.wait_ge(tok_turned, n * 2 + (TT_UP[l] + h + 1))
                    act.wait_ge(cw_ready, n * 2 + (l * 2 * UP_PAIRS + h + 1))
                    act.wait_ge(wait_sem, wait_val)
                for j in (j0, j0 + 1):
                    act.activation(dst[:, j, :], ps[:, 2 * h + j // 2, (j % 2) * SEQ:(j % 2 + 1) * SEQ], ACT.Identity,
                                   scale=cw[:, h, 2, j:j + 1], bias=cw[:, h, 3, j:j + 1]).then_inc(conv_started, 1)

            def up_copy(l, n):
                tok_copy(1, n * 2 + (TT_UP[l] + 1))

            def up_finish(k, l, n):
                if k in (3, 5):
                    conv(cu, 1, l, n, k - 3, hid_low, n + l * UP_PAIRS)
                if k == 11:
                    act.wait_ge(prod_ready, n + (l * UP_PAIRS + 1))
                    act.activation(hid_h[:, bass.ds(n * 4, 4), :], cu[:, :, :], ACT.Copy).then_inc(hid_high, 1)

            def mlp(l):
                def turn(n, b4, first=False):
                    if not first:
                        up_copy(l, n - 1)
                    for k in slots(b4, 0):
                        if first:
                            if k % 2 == 0 and k // 2 + 2 < KC:
                                xt_evacuate(1 + 2 * l, l, 0, k // 2 + 2)
                        else:
                            up_finish(k, l, n - 1)
                    tok_copy(0, n * 2 + TT_UP[l])
                    for k in slots(b4, KC):
                        if k in (3, 5):
                            conv(cg, 0, l, n, k - 3, prod_ready, n + l * UP_PAIRS)
                        if k == 9:
                            wait_free(act, 0, n * 2 + (TURN_UP[l][0] + 2))
                            act.activation(cg[:, :, :], cg[:, :, :], ACT.Silu).then_inc(silu_done, 1)

                turn(0, CH_UP[l] // 4, first=True)
                with act.Fori(0, UP_PAIRS - 1) as i:
                    turn(i + 1, i * (2 * KC // 4) + (CH_UP[l] + 2 * KC) // 4)
                b4 = CH_DOWN[l] // 4
                up_copy(l, UP_PAIRS - 1)
                for k in slots(b4, 0, KT):
                    up_finish(k, l, UP_PAIRS - 1)
                split_run(b4, KC + AHEAD, OUT_GROUPS * FC - KC - (AHEAD if l == DEPTH - 1 else 0))

            xt_evacuate(0, 0, 0, 0)
            split(0, 0)
            xt_evacuate(0, 0, 0, 1)
            for c in range(1, AHEAD):
                split(0, c)
            act.dma_start(cg[0:2 * FT, :, :].rearrange("p m (a b) -> p (m a) b", b=P)[:, 0:3, :],
                          ffn_conv_w[0].rearrange("w (t p) -> t w p", p=P)).then_inc(par_in, 16)
            act.dma_start(cg[0:2 * FT, :, :].rearrange("p m (a b) -> p (m a) b", b=P)[:, 4:7, :],
                          ffn_conv_w[1].rearrange("w (t p) -> t w p", p=P)).then_inc(par_in, 16)
            for l in range(DEPTH):
                act.dma_start(cg[0:2 * FT, :, :].rearrange("p m (a b) -> p (m a) b", b=P)[:, 4 * l + 3, :],
                              ffn_conv_b[l].rearrange("(t p) -> t p", p=P)).then_inc(par_in, 16)
            for i, src in enumerate((ln_g, ln_b)):
                act.dma_start(cu[64 * i:64 * i + 64, 0, 0:P], src.rearrange("l s (k p) -> (l s k) p", p=P)).then_inc(par_in, 16)
            mixer_a()
            for l in range(DEPTH):
                if l == 1:
                    mixer_b()
                split_run(CH_O[l] // 4, 2 * KC + AHEAD, (OUT_GROUPS - 2) * KC)
                norm_and_first(1 + 2 * l, l, 0)
                mlp(l)
                if l == 0:
                    norm_and_first(2, 0, 1)
            layer_norm(4)
            act.wait_ge(norm_ready, 4)
            for m in range(MT):
                act.activation(res[:, m, GP_COLS], res[:, m, GP_COLS], ACT.Identity, scale=rstd[:, 2, m:m + 1],
                               bias=nmr[:, m:m + 1]).then_inc(z0_ready, 1)

        @block.vector
        def _(dve):
            own = Links(dve, dve_own)

            def split(b4, loc):
                if isinstance(b4, int) and 4 * b4 + loc >= CH_END:
                    return
                dve.wait_ge(high_ready, b4 * 4 + (loc + 1))
                if not (isinstance(b4, int) and 4 * b4 + loc < RING):
                    dve.wait_ge(chunks_used, b4 * 4 + (loc - RING + 1))
                s = loc % RING
                dve.tensor_tensor(w_lo[:, s], raw[:, s], w_hi[:, s].bitcast(FP32), ALU.subtract).then_inc(low_ready, 1)

            def slots(b4, loc0, nk=KT, after_norm=False):
                for k in range(nk):
                    if k == nk - 2 and not after_norm:
                        split(b4, loc0 + k // 2 + LOW_AHEAD)
                    yield k
                    if k % 2 == 0 and k != nk - 2:
                        split(b4, loc0 + k // 2 + LOW_AHEAD + (1 if after_norm else 0))


            def split_run(b4, loc0, count):
                while loc0 % 4 and count:
                    split(b4, loc0)
                    loc0, count = loc0 + 1, count - 1
                if count >= 8:
                    with dve.Fori(0, count // 4) as i:
                        for c in range(4):
                            split(i + (b4 + loc0 // 4), c)
                    loc0, count = loc0 + count // 4 * 4, count % 4
                for c in range(count):
                    split(b4, loc0 + c)

            def xt_evacuate(xi, l, s, g):
                if xi == 0:
                    src = ps[:, X_BANK + g % 4, :].rearrange("p (a t) -> p a t", a=2)
                elif g == 0:
                    dve.wait_ge(first_high, xi)
                    dve.tensor_tensor(xl[:, 0, :], cg[:, 0, :], xh[:, 0, :].bitcast(FP32), ALU.subtract).then_inc(first_low, 1)
                    dve.wait_ge(xt_high, KC * xi + 1)
                    dve.tensor_tensor(xl[:, 1, :], cg[:, 1, :], xh[:, 1, :].bitcast(FP32), ALU.subtract).then_inc(xt_low, 1)
                    return
                else:
                    src = cg[:, 2 * (g % 2):2 * (g % 2) + 2, :]
                high = xh[:, 2 * g:2 * g + 2, :].bitcast(FP32)
                dve.wait_ge(xt_high, KC * xi + g + 1)
                dve.tensor_tensor(xl[:, 2 * g:2 * g + 2, :], src, high, ALU.subtract).then_inc(xt_low, 1)

            def xt_full_tiles(xi, l, s, g):
                if g >= 2:
                    dve.wait_ge(xt_low, KC * xi + g - 1)
                for a in range(2):
                    k = 2 * g + a
                    if k == 0:
                        dve.wait_ge(first_turned, xi)
                    elif k == 1 or a == 0:
                        dve.wait_ge(xt_turned, KC * xi + g + 1)
                    b = FIRST_BANK if k == 0 else X_BANK + g % 4
                    last = dve.tensor_scalar(cg[:, 2 * (g % 2) + a, :], ps[:, b, a * SEQ:(a + 1) * SEQ],
                                             lncol[:, 0, l, s, k:k + 1], lncol[:, 1, l, s, k:k + 1], ALU.mult, ALU.add)
                    if k == 0:
                        last.then_inc(first_full, 1)
                last.then_inc(xt_full, 1)

            def xt_next(xi, l, s, k):
                if k % 2 == 0 and k // 2 + 2 < KC:
                    if k == 0:
                        xt_full_tiles(xi, l, s, 2)
                    xt_evacuate(xi, l, s, k // 2 + 2)
                    if k // 2 + 3 in DVE_FULL:
                        xt_full_tiles(xi, l, s, k // 2 + 3)

            def tok_copy(s, used, batch, scale=None):
                dve.wait_ge(tok_turned, batch)
                dve.wait_ge(chunks_used, used)
                if scale is None:
                    dve.tensor_copy(tok[:, 1, :], bank(s, 1)).then_inc(acc_free[s][1], 1)
                else:
                    dve.tensor_scalar(tok[:, 1, :], bank(s, 1), scale, None, ALU.mult).then_inc(acc_free[s][1], 1)

            def turned_copy(dst, s, batch):
                dve.wait_ge(tok_turned, batch + 1)
                dve.tensor_copy(dst[:, 2:4, :], bank(s, 1).rearrange("p (a t) -> p a t", a=2)).then_inc(acc_free[s][1], 1)

            def attend(s, hc, group, sink):
                if s < HG:
                    if s == 0:
                        dve.wait_ge(bias_ready, group + 1)
                    dve.wait_ge(scores_ready, hc + (s + 1))
                    if s >= 4:
                        dve.wait_ge(probsT_turned, hc + (s - 3))
                    dve.memset(mark[:, s:s + 1], 0.0)
                    b = s % 4
                    src = ps[:, S_BANK + s % 2, :]
                    for m, (lo, hi) in enumerate(((0, P), (P, SPAN))):
                        last = dve.tensor_tensor_reduce(out=prob[:, b, lo:hi], in0=src[:, lo:hi], in1=bias[:, s, lo:hi],
                                                        scale=-1.0, scalar=sinkc[:, 1, s:s + 1] if sink else -MASKED,
                                                        op0=ALU.add, op1=ALU.min, accum_out=nmax[:, m, s:s + 1])
                    last.then_inc(scores_used, 1)
                j = s - 2
                if 0 <= j < HG:
                    dve.wait_ge(probsT_turned, hc + (j + 1))
                    if j >= 2:
                        dve.wait_ge(pv_done, hc + (j - 1))
                    dve.tensor_copy(probT[:, j % 2, :], ps[:, PT_BANK, 0:SPAN]).then_inc(probsT_ready, 1)

            def out_norm(q, hc, quads, sink):
                dve.wait_ge(probs_ready, hc + 4 * (q + 1))
                d = rsum[:, q].rearrange("p m j -> p (m j)")
                if sink:
                    own.link(dve.tensor_tensor(den[:, q, :], d, esink[:, q].rearrange("p m j -> p (m j)"), ALU.add))
                    d = den[:, q, :]
                own.link(dve.reciprocal(rden[:, q, :], d))
                dve.wait_ge(pv_done, hc + 4 * (q + 1))
                dve.wait_ge(oT_turned, quads + q)
                dve.tensor_tensor(onorm[:, :, :].rearrange("p m (j d) -> p (m j) d", d=HD),
                                  ps[:, O_BANK, :].rearrange("p (g d) -> p g d", d=HD),
                                  rden[:, q, :].unsqueeze(2).to_broadcast([P, MT * 4, HD]), ALU.mult).then_inc(o_ready, 1)

            def out_low(q, quads, kt):
                dve.wait_ge(oT_high, quads + (q + 1))
                at = bass.ds(kt + 2 * q, 2)
                dve.tensor_tensor(ol[:, at, :], ps[:, S_BANK + q, :].rearrange("p (a t) -> p a t", a=2),
                                  oh[:, at, :].bitcast(FP32), ALU.subtract).then_inc(oT_low, 1)

            def attention_slot(k, hc, quads, kt, group, sink):
                if k == FIRST_STEP + 7:
                    out_norm(0, hc, quads, sink)
                if FIRST_STEP <= k < FIRST_STEP + STEPS:
                    attend(k - FIRST_STEP, hc, group, sink)
                if k == 12:
                    out_low(0, quads, kt)
                if k == 13:
                    out_norm(1, hc, quads, sink)
                if k == 14:
                    out_low(1, quads, kt)

            def residual(s, turn, used, n, pieces, tile0=0):
                if pieces:
                    dve.wait_ge(res_ready, pieces)
                cols = bass.ds(n * COLS, COLS)
                for m in range(MT):
                    if m == 0 and tile0:
                        dve.wait_ge(last_tile0, tile0)
                    else:
                        dve.wait_ge(chunks_used, used)
                    dve.scalar_tensor_tensor(res[:, m, cols], res[:, m, cols], ALPHA, bank(s, m), ALU.mult, ALU.add)\
                       .then_inc(acc_free[s][m], 1)
                    dve.wait_ge(acc_free[s][m], turn + 1)
                    last = dve.bn_stats(stats[:, m, bass.ds(n, 1), :].rearrange("p a b -> p (a b)"), res[:, m, cols])
                return last

            def out_residual(l, n):
                s = (n + 1) % 2
                used = CH_O[l] + (OUT_DONE // 2 if n == 0 else (n + 1) * KC)
                return residual(s, TURN_O[l][s] + n // 2, used, n, 8 * l, 3 * l + 1 if n == OUT_GROUPS - 1 else 0)

            def out_projection(l):
                for n in range(2, OUT_GROUPS):
                    out_residual(l, n - 1)
                    for k in slots(CH_O[l] // 4, n * KC):
                        pass
                return out_residual(l, OUT_GROUPS - 1)

            def layer_norm(xi, last):
                own.link(last)
                for m in range(MT):
                    last = dve.bn_aggr(mv[:, m, :], stats[:, m, :, :].rearrange("p a b -> p (a b)"))
                own.link(last)
                dve.tensor_scalar(var[:, :], mv[:, :, 1], LN_EPS, None, ALU.add).then_inc(var_ready, 1)
                dve.wait_ge(sd_ready, xi)
                own.link(dve.reciprocal(rstd[:, 0, :], sd[:, :]))
                own.link(dve.scalar_tensor_tensor(rstd[:, 1, :], rstd[:, 0, :], -0.5, rstd[:, 0, :], ALU.mult, ALU.mult))
                own.link(dve.tensor_tensor(rstd[:, 1, :], rstd[:, 1, :], var[:, :], ALU.mult))
                own.link(dve.scalar_tensor_tensor(rstd[:, 2, :], rstd[:, 1, :], 1.5, rstd[:, 0, :], ALU.add, ALU.mult))
                dve.scalar_tensor_tensor(nmr[:, :], mv[:, :, 0], -1.0, rstd[:, 2, :], ALU.mult, ALU.mult).then_inc(norm_ready, 1)
                dve.wait_ge(norm_ready, xi)

            def normalise(i):
                cols = slice(i * 2 * P, (i + 1) * 2 * P)
                dve.tensor_scalar(res[:, 1, cols], res[:, 1, cols], rstd[:, 2, 1:2], nmr[:, 1:2], ALU.mult, ALU.add)\
                   .then_inc(z1_ready, 1)

            def norm_and_first(xi, l, s, last):
                layer_norm(xi, last)
                for i in range(2):
                    normalise(i)
                xt_full_tiles(xi, l, s, 0)
                xt_evacuate(xi, l, s, 0)
                normalise(2)
                normalise(3)
                xt_full_tiles(xi, l, s, 1)
                normalise(4)
                normalise(5)
                xt_evacuate(xi, l, s, 1)
                normalise(6)
                normalise(7)
                split((CH_UP[l] if s == 0 else CH_B) // 4, LOW_AHEAD)

            def mixer_a():
                for k in slots(CH_A_KV // 4, 0):
                    if k % 2 == 0 and k // 2 + 2 < KC:
                        xt_evacuate(0, 0, 0, k // 2 + 2)
                for k in slots(CH_A_Q // 4, 0):
                    if k == 0:
                        dve.wait_ge(chunks_used, CH_A_Q)
                        dve.tensor_copy(vall[:, 1, :], bank(0, 1)[:, KV_HEADS * HD:])
                        both = tok[:, 1, :].rearrange("p (h c d) -> p h c d", c=2, d=HD)
                        for c in range(2):
                            last = dve.tensor_copy(both[:, :, c, :], bank(0, 1)[:, 0:KV_HEADS * HD].rearrange("p (h d) -> p h d", d=HD))
                        last.then_inc(acc_free[0][1], 1)
                    if k == 2:
                        turned_copy(kTall, 0, TT_A)
                    if k == 7:
                        dve.wait_ge(par_turned, 1)
                        dve.tensor_copy(lncol[:, :, :, :, :].rearrange("p a l s k -> p (a l s k)"), ps[:, X_BANK, 0:P]).then_inc(par_ready, 1)
                        for l in range(DEPTH):
                            dve.wait_ge(par_turned, l + 2)
                            dve.tensor_copy(convcol[:, l].rearrange("p w t -> p (w t)"), ps[:, X_BANK + 1 + l, 0:8 * FT]).then_inc(par_ready, 2)

                def turn(n, b4, nk=KT):
                    tok_copy(1, n * KC + CH_A_Q, n + TT_A, SCALE)
                    for k in slots(b4, 0, nk):
                        if k == 2:
                            turned_copy(qT, 0, n + TT_A)
                        attention_slot(k, (n - 1) * HG, (n - 1) * 2, (n - 1) * 4, n - 1, True)
                        if k == OUT_DONE:
                            out_residual(0, 0)

                with dve.Fori(0, GROUPS - 1) as i:
                    own.enter(i, 4)
                    turn(i + 1, i * (KC // 4) + (CH_A_Q + KC) // 4)
                    own.leave(GROUPS - 1)
                turn(GROUPS, CH_O[0] // 4, 2 * KT)

            def decay(k):
                z, nabs, e, u, lnu, d, zero, cum, ncum = fs
                if k == 3:
                    dve.wait_ge(fz_done, 1)
                    dve.wait_ge(wf_in, 32)
                    own.link(dve.tensor_scalar(z[:, :], ps[0:HEADS, 6, 0:SEQ], fbc[:, 0:1], None, ALU.add))
                    dve.scalar_tensor_tensor(nabs[:, :], z[:, :], -1.0, z[:, :], ALU.mult, ALU.min).then_inc(decay_abs, 1)
                if k == 7:
                    dve.wait_ge(decay_exp, 1)
                    dve.tensor_scalar(u[:, :], e[:, :], 1.0, None, ALU.add).then_inc(decay_u, 1)
                    dve.wait_ge(decay_u, 1)
                    own.link(dve.tensor_scalar(d[:, :], u[:, :], -1.0, None, ALU.add))
                    own.link(dve.tensor_scalar(zero[:, :], d[:, :], 0.0, None, ALU.is_equal))
                    own.link(dve.tensor_tensor(d[:, :], d[:, :], zero[:, :], ALU.add))
                    own.link(dve.reciprocal(d[:, :], d[:, :]))
                    own.link(dve.tensor_tensor(d[:, :], d[:, :], e[:, :], ALU.mult))
                if k == 9:
                    dve.wait_ge(decay_ln, 1)
                    own.link(dve.tensor_tensor(lnu[:, :], lnu[:, :], zero[:, :], ALU.add))
                    own.link(dve.tensor_tensor(d[:, :], lnu[:, :], d[:, :], ALU.mult))
                    own.link(dve.scalar_tensor_tensor(z[:, :], z[:, :], 0.0, d[:, :], ALU.min, ALU.subtract))
                    own.link(dve.memset(zero[:, :], 1.0))
                    own.link(dve.tensor_tensor_scan(cum[:, :], zero[:, :], z[:, :], 0.0, ALU.mult, ALU.add))
                    dve.tensor_scalar(ncum[:, :], cum[:, :], -1.0, None, ALU.mult).then_inc(cum_ready, 1)
                if k == 13:
                    dve.wait_ge(cum_turned, 1)
                    dve.tensor_copy(cumq[:, :, :], ps[:, 7, 0:MT * HEADS].rearrange("p (m h) -> p m h", m=MT)).then_inc(cumq_ready, 1)

            def mixer_b():
                def turn(n, b4, first=False, nk=KT):
                    if not first:
                        dve.wait_ge(pv_done, n * HG + (GROUPS - 1) * HG)
                        dve.wait_ge(v_tile0, n)
                        dve.tensor_copy(vv[:, 0, :], bank(0, 0)).then_inc(acc_free[0][0], 1)
                    for k in slots(b4, 0, nk, after_norm=first):
                        if first:
                            xt_next(2, 0, 1, k)
                            if k == 13:
                                dve.wait_ge(wf_high, 1)
                                dve.tensor_tensor(wf_lo[:, :, :], wf[:, :, :], wf_hi[:, :, :].bitcast(FP32), ALU.subtract).then_inc(wf_low, 1)
                            continue
                        attention_slot(k, (n + (GROUPS - 1)) * HG, (n + (GROUPS - 1)) * 2, (n - 1) * 4, n + (GROUPS - 1), False)
                        if k == OUT_DONE:
                            out_residual(1, 0)
                    if nk > KT:
                        return
                    tok_copy(0, n * (3 * KC) + (CH_B + KC), n * 2 + TT_B, SCALE)
                    for k in slots(b4, KC):
                        if k == 2:
                            turned_copy(qT, 0, n * 2 + TT_B)
                        if first:
                            decay(k)
                    tok_copy(1, n * (3 * KC) + (CH_B + 2 * KC), n * 2 + (TT_B + 1))
                    for k in slots(b4, 2 * KC):
                        if k == 2:
                            turned_copy(kT, 1, n * 2 + (TT_B + 1))

                turn(0, CH_B // 4, first=True)
                with dve.Fori(0, GROUPS - 1) as i:
                    own.enter(i, 2)
                    turn(i + 1, i * (3 * KC // 4) + (CH_B + 3 * KC) // 4)
                    own.leave(GROUPS - 1)
                turn(GROUPS, CH_O[1] // 4, nk=2 * KT)

            def conv(dst, h, l, n, j0):
                dve.wait_ge(conv_started, n * 8 + (l * 8 * UP_PAIRS + 4 * h + j0 + 2))
                for tap in (1, 0):
                    for j in (j0, j0 + 1):
                        lag = 2 - tap
                        src = ps[:, 2 * h + j // 2, (j % 2) * SEQ:(j % 2 + 1) * SEQ - lag]
                        last = dve.scalar_tensor_tensor(dst[:, j, lag:SEQ], src, cw[:, h, tap, j:j + 1], dst[:, j, lag:SEQ],
                                                        ALU.mult, ALU.add)
                        if tap == 0 and j0 == 2:
                            last.then_inc(acc_free[h][j - 2], 1)
                    if tap == 1:
                        own.link(last)

            def up_copy(l, n):
                tok_copy(1, n * (2 * KC) + (CH_UP[l] + 2 * KC), n * 2 + (TT_UP[l] + 1))

            def up_finish(k, l, n):
                if k in (5, 7):
                    conv(cu, 1, l, n, k - 5)
                if k == 9:
                    wait_free(dve, 1, n * 2 + (TURN_UP[l][1] + 2))
                    dve.wait_ge(silu_done, n + (l * UP_PAIRS + 1))
                    dve.tensor_tensor(cu[:, :, :], cu[:, :, :], cg[:, :, :], ALU.mult).then_inc(prod_ready, 1)
                if k == 13:
                    dve.wait_ge(hid_high, n + (l * UP_PAIRS + 1))
                    at = bass.ds(n * 4, 4)
                    dve.tensor_tensor(hid_l[:, at, :], cu[:, :, :], hid_h[:, at, :].bitcast(FP32), ALU.subtract).then_inc(hid_low, 1)

            def mlp(l):
                def turn(n, b4, first=False):
                    if not first:
                        up_copy(l, n - 1)
                    for k in slots(b4, 0, after_norm=first):
                        if first:
                            xt_next(1 + 2 * l, l, 0, k)
                        else:
                            up_finish(k, l, n - 1)
                    tok_copy(0, n * (2 * KC) + (CH_UP[l] + KC), n * 2 + TT_UP[l])
                    for k in slots(b4, KC):
                        if k in (5, 7):
                            conv(cg, 0, l, n, k - 5)

                turn(0, CH_UP[l] // 4, first=True)
                with dve.Fori(0, UP_PAIRS - 1) as i:
                    own.enter(i, 4)
                    turn(i + 1, i * (2 * KC // 4) + (CH_UP[l] + 2 * KC) // 4)
                    own.leave(UP_PAIRS - 1)
                b4, (t0, t1) = CH_DOWN[l] // 4, TURN_DOWN[l]
                pieces = 4 if l == 0 else 12
                up_copy(l, UP_PAIRS - 1)
                for k in slots(b4, 0, KT):
                    up_finish(k, l, UP_PAIRS - 1)
                split_run(b4, KC + LOW_AHEAD, FC - KC)
                for n in range(1, OUT_GROUPS):
                    residual((n - 1) % 2, (t0, t1)[(n - 1) % 2] + (n - 1) // 2, CH_DOWN[l] + n * FC, n - 1, pieces)
                    split_run(b4, n * FC + LOW_AHEAD, FC - (LOW_AHEAD if l == DEPTH - 1 and n == OUT_GROUPS - 1 else 0))
                n = OUT_GROUPS
                return residual((n - 1) % 2, (t0, t1)[(n - 1) % 2] + (n - 1) // 2, CH_DOWN[l] + n * FC, n - 1, pieces, 3 * l + 3)

            xt_evacuate(0, 0, 0, 0)
            split(0, 0)
            xt_evacuate(0, 0, 0, 1)
            for c in range(1, LOW_AHEAD):
                split(0, c)
            mixer_a()
            for l in range(DEPTH):
                if l == 1:
                    mixer_b()
                norm_and_first(1 + 2 * l, l, 0, out_projection(l))
                last = mlp(l)
                if l == 0:
                    norm_and_first(2, 0, 1, last)
            layer_norm(4, last)
            dve.wait_ge(full_in, 32)
            for i in range(3):
                cols = slice(i * COLS, min((i + 1) * COLS, GP_COLS.start))
                for m in range(MT):
                    last = dve.scalar_tensor_tensor(res[:, m, cols], res[:, m, cols], mv[:, m, 0:1], lnfull[:, 0, cols],
                                                    ALU.subtract, ALU.mult)
                own.link(last)
                for m in range(MT):
                    dve.scalar_tensor_tensor(res[:, m, cols], res[:, m, cols], rstd[:, 2, m:m + 1], lnfull[:, 1, cols],
                                             ALU.mult, ALU.add).then_inc(fin_ready, 1)

        @block.tensor
        def _(pe):
            def product(s, turn, k, nk, lh, ll, slot, tile0=None, tiles=range(MT)):
                for m in tiles:
                    if k == 0:
                        pe.wait_ge(acc_free[s][m], turn)
                    rows = slice(m * P, (m + 1) * P)
                    o = bank(s, m)
                    pe.matmul(o, lh[:, k, rows], w_lo[:, slot, k % 2, :], start=(k == 0), stop=False)
                    pe.matmul(o, ll[:, k, rows], w_hi[:, slot, k % 2, :], start=False, stop=False)
                    last = pe.matmul(o, lh[:, k, rows], w_hi[:, slot, k % 2, :], start=False, stop=(k == nk - 1))
                    if k == nk - 1 and m == 0 and tile0:
                        last.then_inc(tile0, 1)
                return last

            def group(s, turn, b4, loc0, lh=xh, ll=xl, nk=KT, before=None, tile0=None):
                for k in range(nk):
                    loc = loc0 + k // 2
                    if k % 2 == 0:
                        if before:
                            before(k // 2)
                        pe.wait_ge(low_ready, b4 * 4 + (loc + 1))
                    if tile0 is last_tile0 and k >= nk - 2:
                        if k == nk - 1:
                            for m in range(MT):
                                for kk in (k - 1, k):
                                    last = product(s, turn, kk, nk, lh, ll, loc % RING, tile0, (m,))
                    else:
                        last = product(s, turn, k, nk, lh, ll, loc % RING, tile0)
                    if k % 2 == 1:
                        last.then_inc(chunks_used, 1)
                    yield k

            def keep_clock(us):
                for _ in range(round(us / 0.427)):
                    pe.matmul(ps[:, X_BANK + 3, 0:2 * P], ident[:, :], ident[:, :].unsqueeze(1).to_broadcast([P, 2, P]),
                              start=True, stop=True)

            def xt_turn(xi, g):
                if xi == 0:
                    pe.wait_ge(res_in[g // 2], 16)
                else:
                    pe.wait_ge(z0_ready, KC * (xi - 1) + g + 1)
                    pe.wait_ge(z1_ready, KC * (xi - 1) + g + 1)
                for a in range(2):
                    k = 2 * g + a
                    b = X_BANK + g % 4
                    if xi and k == 0:
                        b = FIRST_BANK
                    for m in range(MT):
                        last = pe.transpose(ps[:, b, a * SEQ + m * P:a * SEQ + (m + 1) * P],
                                            res[:, m, k * P:(k + 1) * P], ident[:, :])
                    if xi and k == 0:
                        last.then_inc(first_turned, 1)
                last.then_inc(xt_turned, 1)

            def x_ready(xi):
                def before(c):
                    if c == 0:
                        keep_clock(1.7 if xi == 0 else 3.4)
                        xt_turn(xi, 0)
                        xt_turn(xi, 1)
                        if xi:
                            pe.wait_ge(first_low, xi)
                            return
                    pe.wait_ge(xt_low, KC * xi + c + 1)
                return before

            def x_next(xi, k):
                if k == 0:
                    if xi:
                        pe.wait_ge(xt_low, KC * xi + 1)
                    xt_turn(xi, 2)
                if k % 2 == 0 and k // 2 + 3 < KC:
                    xt_turn(xi, k // 2 + 3)

            def turn_tok(s, turn, source_free, source_turns):
                wait_free(pe, source_free, source_turns)
                wait_free(pe, s, turn)
                for j in range(4):
                    for m in range(MT):
                        last = pe.transpose(ps[:, 2 * s + j // 2, (j % 2) * SEQ + m * P:(j % 2) * SEQ + (m + 1) * P],
                                            tok[:, m, j * P:(j + 1) * P], ident[:, :])
                last.then_inc(tok_turned, 1)

            def attend(s, hc, quads, shared, first_waits, value_waits):
                if s < HG:
                    if s == 0:
                        first_waits()
                    if s >= 2:
                        pe.wait_ge(scores_used, hc + (s - 1))
                    if s == 0:
                        pe.wait_ge(oT_low, quads)
                    rows = slice(HD * (s % 2), HD * (s % 2) + HD)
                    kt = 0 if shared else s // 2
                    o = ps[:, S_BANK + s % 2, :]
                    pe.matmul(o[:, 0:P], qT[rows, s // 2, 0:P], kT[rows, kt, 0:P], start=True, stop=True)
                    pe.matmul(o[:, P:SPAN], qT[rows, s // 2, P:SEQ], kT[rows, kt, :], start=True, stop=True).then_inc(scores_ready, 1)
                j = s - 2
                if 0 <= j < HG:
                    pe.wait_ge(probs_ready, hc + (j + 1))
                    if j >= 1:
                        pe.wait_ge(probsT_ready, hc + j)
                    for b in range(3):
                        last = pe.transpose(ps[:, PT_BANK, b * P:(b + 1) * P], prob[:, j % 4, b * P:(b + 1) * P], ident[:, :])
                    last.then_inc(probsT_turned, 1)
                j = s - 3
                if 0 <= j < HG:
                    if j == 0:
                        value_waits()
                    if j % 4 == 0:
                        pe.wait_ge(o_ready, quads + j // 4)
                    pe.wait_ge(probsT_ready, hc + (j + 1))
                    cols = slice(0, HD) if shared else slice(j * HD, (j + 1) * HD)
                    o = [ps[:, O_BANK, m * 4 * HD + (j % 4) * HD:m * 4 * HD + (j % 4 + 1) * HD] for m in range(MT)]
                    pt = probT[:, j % 2, :]
                    pe.matmul(o[0], pt[:, 0:P], vv[:, 0, cols], start=True, stop=True)
                    pe.matmul(o[1], pt[:, P:2 * P], vv[:, 0, cols], start=True, stop=False)
                    pe.matmul(o[1], pt[:, 2 * P:SPAN], vv[:, 1, cols], start=False, stop=True).then_inc(pv_done, 1)

            def turn_out(q, quads):
                pe.wait_ge(o_ready, quads + (q + 1))
                for a in range(2):
                    for m in range(MT):
                        last = pe.transpose(ps[:, S_BANK + q, a * SEQ + m * P:a * SEQ + (m + 1) * P],
                                            onorm[:, m, a * P:(a + 1) * P], ident[:, :])
                last.then_inc(oT_turned, 1)

            def attention_slot(k, hc, quads, shared, first_waits, value_waits):
                if FIRST_STEP <= k < FIRST_STEP + STEPS:
                    attend(k - FIRST_STEP, hc, quads, shared, first_waits, value_waits)
                if k == 11:
                    pe.wait_ge(scores_used, hc + HG)
                    turn_out(0, quads)
                if k == 14:
                    turn_out(1, quads)

            def out_pair(l):
                for slot, (i, k) in enumerate(WOVEN_OUT):
                    s = (i + 1) % 2
                    if slot == 0:
                        pe.wait_ge(oT_low, 2 * GROUPS * l + 2 * (GROUPS - 1))
                    if i == 0 and k in (LATE, LATE + 2):
                        pe.wait_ge(oT_low, 2 * GROUPS * l + 2 * (GROUPS - 1) + (k - LATE) // 2 + 1)
                    if slot % 2 == 0:
                        pe.wait_ge(low_ready, CH_O[l] + slot // 2 + 1)
                    last = product(s, TURN_O[l][s], k, KT, oh, ol, (slot // 2) % RING)
                    if slot % 2 == 1:
                        last.then_inc(chunks_used, 1)
                    yield slot

            def mixer_a():
                for k in group(0, TURN_A_KV, CH_A_KV // 4, 0, before=x_ready(0), tile0=tok_tile0):
                    x_next(0, k)
                for k in group(1, TURN_A_Q, CH_A_Q // 4, 0, tile0=tok_tile0):
                    if k == 1:
                        turn_tok(0, TURN_A_KV + 1, 0, TURN_A_KV + 1)
                    if k == 5:
                        pe.wait_ge(par_in, 96)
                        rows = cg[:, :, :].rearrange("p m (a b) -> p (m a) b", b=P)
                        pe.transpose(ps[:, X_BANK, 0:P], cu[:, 0, 0:P], ident[:, :]).then_inc(par_turned, 1)
                        for l in range(DEPTH):
                            for w in range(4):
                                last = pe.transpose(ps[:, X_BANK + 1 + l, w * 2 * FT:(w + 1) * 2 * FT],
                                                    rows[0:2 * FT, 4 * l + w, :], ident[0:2 * FT, 0:2 * FT])
                            last.then_inc(par_turned, 1)
                pe.wait_ge(par_ready, 5)

                def woven(k, n):
                    if k == 1:
                        turn_tok(0, n - 1 + TURN_A_QT, 1, n + TURN_A_Q)

                    def first_waits():
                        wait_free(pe, 0, n + TURN_A_QT)
                        pe.wait_ge(kv_ready, 2 * n - 1)
                    attention_slot(k, (n - 1) * HG, (n - 1) * 2, True, first_waits, lambda: pe.wait_ge(kv_ready, 2 * n))

                with pe.Fori(0, GROUPS - 1) as i:
                    for k in group(1, i + (TURN_A_Q + 1), i * (KC // 4) + (CH_A_Q + KC) // 4, 0, tile0=tok_tile0):
                        woven(k, i + 1)
                for k in out_pair(0):
                    woven(k, GROUPS)

            def mixer_b():
                t0, t1 = TURN_B

                def woven(k, n):
                    def first_waits():
                        wait_free(pe, 1, n * 2 + t1)
                        wait_free(pe, 0, n * 3 - 1 + t0)
                    attention_slot(k, (n + (GROUPS - 1)) * HG, (n + (GROUPS - 1)) * 2, False, first_waits,
                                   lambda: wait_free(pe, 0, n * 3 + t0))

                def turn(n, b4, first=False):
                    for k in group(0, n * 3 + t0, b4, 0, before=x_ready(2) if first else None, tile0=tok_tile0):
                        if first:
                            x_next(2, k)
                        else:
                            woven(k, n)
                    if first:
                        pe.wait_ge(wf_low, 1)
                        o = ps[0:HEADS, 6, 0:SEQ]
                        for k in range(KT):
                            pe.matmul(o, wf_lo[:, k, :], xh[:, k, :], start=(k == 0), stop=False)
                            pe.matmul(o, wf_hi[:, k, :], xl[:, k, :], start=False, stop=False)
                            last = pe.matmul(o, wf_hi[:, k, :], xh[:, k, :], start=False, stop=(k == KT - 1))
                        last.then_inc(fz_done, 1)
                    for k in group(1, n * 2 + t1, b4, KC, tile0=tok_tile0):
                        if k == 1:
                            turn_tok(0, n * 3 + (t0 + 1), 0, n * 3 + (t0 + 1))
                        if first and k == 12:
                            pe.wait_ge(cum_ready, 1)
                            for m in range(MT):
                                last = pe.transpose(ps[:, 7, m * HEADS:(m + 1) * HEADS], fs[7][:, m * P:(m + 1) * P],
                                                    ident[0:HEADS, 0:HEADS])
                            last.then_inc(cum_turned, 1)
                    for k in group(0, n * 3 + (t0 + 2), b4, 2 * KC, tile0=v_tile0):
                        if k == 1:
                            turn_tok(1, n * 2 + (t1 + 1), 1, n * 2 + (t1 + 1))

                turn(0, CH_B // 4, first=True)
                with pe.Fori(0, GROUPS - 1) as i:
                    turn(i + 1, i * (3 * KC // 4) + (CH_B + 3 * KC) // 4)
                for k in out_pair(1):
                    woven(k, GROUPS)

            def out_projection(l):
                for i in range(2, OUT_GROUPS):
                    for k in group((i + 1) % 2, TURN_O[l][(i + 1) % 2] + 1, CH_O[l] // 4, i * KC, oh, ol,
                                   tile0=last_tile0 if i == OUT_GROUPS - 1 else None):
                        pass

            def mlp(l):
                t0, t1 = TURN_UP[l]

                def turn(n, b4, first=False):
                    for k in group(0, n * 2 + t0, b4, 0, before=x_ready(1 + 2 * l) if first else None, tile0=tok_tile0):
                        if first:
                            x_next(1 + 2 * l, k)
                        elif k == 2:
                            turn_tok(1, n * 2 + (t1 - 1), 1, n * 2 + (t1 - 1))
                    for k in group(1, n * 2 + t1, b4, KC, tile0=tok_tile0):
                        if k == 2:
                            turn_tok(0, n * 2 + (t0 + 1), 0, n * 2 + (t0 + 1))

                turn(0, CH_UP[l] // 4, first=True)
                with pe.Fori(0, UP_PAIRS - 1) as i:
                    turn(i + 1, i * (2 * KC // 4) + (CH_UP[l] + 2 * KC) // 4)
                last_turn = t1 + 2 * UP_PAIRS - 1
                turn_tok(1, last_turn, 1, last_turn)
                with pe.Fori(0, OUT_GROUPS // 2) as n:
                    for i in range(2):
                        for k in group(i, n + TURN_DOWN[l][i], n * (2 * FC // 4) + CH_DOWN[l] // 4, i * FC, hid_h, hid_l, FT,
                                       tile0=last_tile0 if i == 1 else None,
                                       before=lambda c: pe.wait_ge(hid_low, UP_PAIRS * (l + 1) - (1 if c < FC - 2 else 0))
                                       if c in (0, FC - 2) else None):
                            pass

            pe.wait_ge(ident_ready, 1)
            mixer_a()
            for l in range(DEPTH):
                if l == 1:
                    mixer_b()
                out_projection(l)
                mlp(l)


_INS = ['x', 'a_w_qkv', 'a_w_o', 'a_sinks', 'rel_bias', 'b_w_qkvf', 'b_f_bias', 'b_w_o',
        'ffn_w_up', 'ffn_conv_w', 'ffn_conv_b', 'ffn_w_down', 'ln_g', 'ln_b']
_OUTS = [((1, 256, 2048), 'float32')]


def kernel(**inputs):
    import numpy as _np
    import concourse.bacc as _bacc
    from concourse import mybir as _mybir
    from concourse.bass_utils import run_bass_kernel_spmd as _run

    nc = _bacc.Bacc("TRN2", target_bir_lowering=False, num_devices=1)
    arrays, args = {}, []
    for name in _INS:
        a = _np.ascontiguousarray(inputs[name])
        arrays[f"in_{name}_dram"] = a
        args.append(nc.dram_tensor(f"in_{name}_dram", a.shape, _mybir.dt.from_np(a.dtype), kind="ExternalInput").ap())
    for i, (shape, dtype) in enumerate(_OUTS):
        dt = _mybir.dt.from_np(_np.dtype(dtype))
        args.append(nc.dram_tensor(f"out_{i}_dram", shape, dt, kind="ExternalOutput").ap())
    trunk(nc, *args)
    r = _run(nc, [arrays], core_ids=[0])
    got = tuple(r.results[0][f"out_{i}_dram"] for i in range(len(_OUTS)))
    return got[0]
```
